# Optimizing a Trainium2 kernel written in Bass

```python
import jax, jax.numpy as jnp
from jax import lax
import numpy as np

D_MODEL = 1024
BATCH = 1
SEQ = 256
DEPTH = 1
DEC_BATCH = 1
DEC_SEQ = 1024
PAST_LEN = 256

GRID_W = 64
NA_HEADS = 8
NA_HEAD_DIM = D_MODEL // 16
NA_WIDTH = NA_HEADS * NA_HEAD_DIM
NA_KH = 8
NA_KW = 16
POOL_WINDOWS = (2, 4, 8, 16)
POOL_GROUPS = 4
POOL_WIDTH = D_MODEL // 4
POOL_GROUP_DIM = POOL_WIDTH // POOL_GROUPS
CONV_WIDTH = D_MODEL // 4
CONV_K = 31
N_BRANCH = 3
N_IN = 3 * NA_WIDTH + POOL_WIDTH + 2 * CONV_WIDTH + N_BRANCH * D_MODEL
FFN_HIDDEN = ((8 * D_MODEL + 3 * 256 - 1) // (3 * 256)) * 256
N_MOD = 6
EPS = 1e-6
NEG_INF = -1e30

kernel_name = "hybrid_na_pool_conv_prefix_dit_step"

def _rmsnorm(x, g):
    xf = x.astype(jnp.float32)
    y = xf * lax.rsqrt(jnp.mean(xf * xf, axis=-1, keepdims=True) + EPS)
    return (y * g.astype(jnp.float32)).astype(x.dtype)

def _layernorm(x, g, b):
    xf = x.astype(jnp.float32)
    mu = jnp.mean(xf, axis=-1, keepdims=True)
    xc = xf - mu
    y = xc * lax.rsqrt(jnp.mean(xc * xc, axis=-1, keepdims=True) + EPS)
    return (y * g.astype(jnp.float32) + b.astype(jnp.float32)).astype(x.dtype)

def _modulation(cond, w_mod, b_mod):
    m = jax.nn.silu(cond) @ w_mod + b_mod
    return jnp.split(m[:, None, :], N_MOD, axis=-1)

def _split_in(u):
    B, L, _ = u.shape
    bounds = np.cumsum([NA_WIDTH, NA_WIDTH, NA_WIDTH, POOL_WIDTH, 2 * CONV_WIDTH]).tolist()
    q, k, v, p_in, c_in, g_in = jnp.split(u, bounds, axis=-1)
    shp = (B, L, NA_HEADS, NA_HEAD_DIM)
    return q.reshape(shp), k.reshape(shp), v.reshape(shp), p_in, c_in, g_in

def _context_attention(q, k, v):
    B, L, H, dh = q.shape
    s = jnp.einsum('bqhd,bkhd->bhqk', q, k).astype(jnp.float32) * (dh ** -0.5)
    p = jax.nn.softmax(s, axis=-1).astype(v.dtype)
    return jnp.einsum('bhqk,bkhd->bqhd', p, v).reshape(B, L, H * dh)

def _neighbourhood_attention(q, k, v, k_ctx, v_ctx, rpb):
    B, L, H, dh = q.shape
    rows = L // GRID_W
    kh = min(NA_KH, rows)
    r = jnp.arange(rows)
    row_start = jnp.clip(r - kh // 2, 0, rows - kh)
    row_idx = row_start[:, None] + jnp.arange(kh)[None, :]
    c = jnp.arange(GRID_W)
    col_start = jnp.clip(c - NA_KW // 2, 0, GRID_W - NA_KW)
    col_in = (c[None, :] >= col_start[:, None]) & (c[None, :] < col_start[:, None] + NA_KW)
    qg = q.reshape(B, rows, GRID_W, H, dh)
    kg = k.reshape(B, rows, GRID_W, H, dh)[:, row_idx]
    vg = v.reshape(B, rows, GRID_W, H, dh)[:, row_idx]
    scale = dh ** -0.5
    s_loc = jnp.einsum('brqhd,brjkhd->bhrqjk', qg, kg).astype(jnp.float32) * scale
    ri = (row_idx - r[:, None]) + NA_KH - 1
    ci = jnp.clip(c[None, :] - c[:, None], -(NA_KW - 1), NA_KW - 1) + NA_KW - 1
    bias = rpb[:, ri[:, None, :, None], ci[None, :, None, :]]
    s_loc = jnp.where(col_in[None, None, None, :, None, :],
                      s_loc + bias[None].astype(jnp.float32), NEG_INF)
    s_ctx = jnp.einsum('brqhd,bchd->bhrqc', qg, k_ctx).astype(jnp.float32) * scale
    n_loc = kh * GRID_W
    s = jnp.concatenate([s_loc.reshape(B, H, rows, GRID_W, n_loc), s_ctx], axis=-1)
    p = jax.nn.softmax(s, axis=-1)
    p_loc = p[..., :n_loc].reshape(B, H, rows, GRID_W, kh, GRID_W).astype(v.dtype)
    p_ctx = p[..., n_loc:].astype(v.dtype)
    o = (jnp.einsum('bhrqjk,brjkhd->brqhd', p_loc, vg)
         + jnp.einsum('bhrqc,bchd->brqhd', p_ctx, v_ctx))
    return o.reshape(B, L, H * dh)

def _pool_mixer(p_in, w_pool, pool_scale):
    B, L, C = p_in.shape
    pf = p_in.astype(jnp.float32)
    cs = jnp.concatenate([jnp.zeros((B, 1, C), jnp.float32), lax.cumsum(pf, axis=1)], axis=1)
    t = jnp.arange(L)
    outs = []
    for g, w in enumerate(POOL_WINDOWS):
        lo = jnp.clip(t - w // 2, 0, L)
        hi = jnp.clip(t - w // 2 + w, 0, L)
        seg = cs[:, :, g * POOL_GROUP_DIM:(g + 1) * POOL_GROUP_DIM]
        cnt = (hi - lo).astype(jnp.float32)[None, :, None]
        outs.append((seg[:, hi] - seg[:, lo]) / cnt)
    pooled = (jnp.concatenate(outs, axis=-1) - pf).astype(p_in.dtype)
    y = jnp.einsum('blgc,gcd->blgd', pooled.reshape(B, L, POOL_GROUPS, POOL_GROUP_DIM), w_pool)
    return y.reshape(B, L, POOL_WIDTH) * pool_scale

def _conv_mixer(c_in, w_dw, b_dw, conv_norm_g, conv_norm_b):
    a, g = jnp.split(c_in, 2, axis=-1)
    h = a * jax.nn.sigmoid(g)
    h = lax.conv_general_dilated(h, w_dw[:, None, :], window_strides=(1,),
                                 padding=[(CONV_K // 2, CONV_K // 2)],
                                 dimension_numbers=('NWC', 'WIO', 'NWC'),
                                 feature_group_count=CONV_WIDTH) + b_dw
    h = _layernorm(h, conv_norm_g, conv_norm_b)
    return jax.nn.silu(h)

def _layer(x, mod, k_ctx, v_ctx, norm1_g, norm2_g, w_in, b_gate, rpb, w_oa, w_pool, pool_scale,
           w_ob, w_dw, b_dw, conv_norm_g, conv_norm_b, w_oc, w_out, w_gu, w_down):
    shift1, scale1, gate1, shift2, scale2, gate2 = mod
    B, L, D = x.shape
    h = _rmsnorm(x, norm1_g) * (1 + scale1) + shift1
    u = h @ w_in
    q, k, v, p_in, c_in, g_in = _split_in(u)
    if k_ctx is None:
        y_a = _context_attention(q, k, v)
        kv_out = (k, v)
    else:
        y_a = _neighbourhood_attention(q, k, v, k_ctx, v_ctx, rpb)
        kv_out = None
    y_a = y_a @ w_oa
    y_b = _pool_mixer(p_in, w_pool, pool_scale) @ w_ob
    y_c = _conv_mixer(c_in, w_dw, b_dw, conv_norm_g, conv_norm_b) @ w_oc
    gates = jax.nn.sigmoid(g_in + b_gate).reshape(B, L, N_BRANCH, D)
    merged = gates[:, :, 0] * y_a + gates[:, :, 1] * y_b + gates[:, :, 2] * y_c
    x = x + gate1 * (merged @ w_out)
    h2 = _rmsnorm(x, norm2_g) * (1 + scale2) + shift2
    a, b = jnp.split(h2 @ w_gu, 2, axis=-1)
    x = x + gate2 * ((jax.nn.silu(a) * b) @ w_down)
    return x, kv_out

def setup_inputs(seed: int = 0) -> dict:
    key = jax.random.key(seed)
    ks = jax.random.split(key, 32)

    def nrm(k, shape, scale):
        return scale * jax.random.normal(k, shape, jnp.float32)

    D = D_MODEL
    kv_shape = (DEC_BATCH, DEPTH, PAST_LEN, NA_HEADS, NA_HEAD_DIM)
    return {
        "x_prompt": nrm(ks[0], (BATCH, SEQ, D), 1.0),
        "x_sample": nrm(ks[1], (DEC_BATCH, DEC_SEQ, D), 1.0),
        "cache_k": nrm(ks[2], kv_shape, 1.0),
        "cache_v": nrm(ks[3], kv_shape, 1.0),
        "c": nrm(ks[4], (DEC_BATCH, D), 1.0),
        "c_ctx": nrm(ks[5], (D,), 1.0),
        "w_mod": nrm(ks[6], (DEPTH, D, N_MOD * D), 0.5 * D ** -0.5),
        "b_mod": nrm(ks[7], (DEPTH, N_MOD * D), 0.02),
        "norm1_g": 1.0 + nrm(ks[8], (DEPTH, D), 0.05),
        "norm2_g": 1.0 + nrm(ks[9], (DEPTH, D), 0.05),
        "w_in": nrm(ks[10], (DEPTH, D, N_IN), D ** -0.5),
        "b_gate": nrm(ks[11], (DEPTH, N_BRANCH * D), 0.02),
        "rpb": nrm(ks[12], (DEPTH, NA_HEADS, 2 * NA_KH - 1, 2 * NA_KW - 1), 0.1),
        "w_oa": nrm(ks[13], (DEPTH, NA_WIDTH, D), NA_WIDTH ** -0.5),
        "w_pool": nrm(ks[14], (DEPTH, POOL_GROUPS, POOL_GROUP_DIM, POOL_GROUP_DIM), POOL_GROUP_DIM ** -0.5),
        "pool_scale": 1.0 + nrm(ks[15], (DEPTH, POOL_WIDTH), 0.05),
        "w_ob": nrm(ks[16], (DEPTH, POOL_WIDTH, D), POOL_WIDTH ** -0.5),
        "w_dw": nrm(ks[17], (DEPTH, CONV_K, CONV_WIDTH), CONV_K ** -0.5),
        "b_dw": nrm(ks[18], (DEPTH, CONV_WIDTH), 0.02),
        "conv_norm_g": 1.0 + nrm(ks[19], (DEPTH, CONV_WIDTH), 0.05),
        "conv_norm_b": nrm(ks[20], (DEPTH, CONV_WIDTH), 0.02),
        "w_oc": nrm(ks[21], (DEPTH, CONV_WIDTH, D), CONV_WIDTH ** -0.5),
        "w_out": nrm(ks[22], (DEPTH, D, D), D ** -0.5),
        "w_gu": nrm(ks[23], (DEPTH, D, 2 * FFN_HIDDEN), D ** -0.5),
        "w_down": nrm(ks[24], (DEPTH, FFN_HIDDEN, D), FFN_HIDDEN ** -0.5),
        "final_g": 1.0 + nrm(ks[25], (D,), 0.05),
    }

def reference(x_prompt, x_sample, cache_k, cache_v, c, c_ctx, w_mod, b_mod, norm1_g, norm2_g,
              w_in, b_gate, rpb, w_oa, w_pool, pool_scale, w_ob, w_dw, b_dw, conv_norm_g,
              conv_norm_b, w_oc, w_out, w_gu, w_down, final_g):
    xp = x_prompt
    xs = x_sample
    ks_out, vs_out = [], []
    for l in range(DEPTH):
        prm = dict(norm1_g=norm1_g[l], norm2_g=norm2_g[l], w_in=w_in[l], b_gate=b_gate[l],
                   rpb=rpb[l], w_oa=w_oa[l], w_pool=w_pool[l], pool_scale=pool_scale[l],
                   w_ob=w_ob[l], w_dw=w_dw[l], b_dw=b_dw[l], conv_norm_g=conv_norm_g[l],
                   conv_norm_b=conv_norm_b[l], w_oc=w_oc[l], w_out=w_out[l], w_gu=w_gu[l],
                   w_down=w_down[l])
        mod_ctx = _modulation(c_ctx[None, :], w_mod[l], b_mod[l])
        mod_lat = _modulation(c, w_mod[l], b_mod[l])
        xp, kv = _layer(xp, mod_ctx, None, None, **prm)
        xs, _ = _layer(xs, mod_lat, cache_k[:, l], cache_v[:, l], **prm)
        ks_out.append(kv[0])
        vs_out.append(kv[1])
    y_prompt = _rmsnorm(xp, final_g)
    y_sample = _rmsnorm(xs, final_g)
    new_k = jnp.stack(ks_out, axis=1)
    new_v = jnp.stack(vs_out, axis=1)
    return (y_prompt, y_sample, new_k, new_v)


_drawn_inputs = setup_inputs


def setup_inputs(seed=0):
    import zlib

    import numpy as np

    out = dict(_drawn_inputs(seed))
    spreads = {}
    factors = {'cache_k': 6.071,
     'cache_v': 5.044,
     'norm2_g': 3.706,
     'b_gate': 8.0,
     'rpb': 64.0,
     'pool_scale': 7.856,
     'b_dw': 8.0,
     'conv_norm_g': 8.0,
     'conv_norm_b': 33.991}
    for name, (base, spread) in spreads.items():
        noise = np.random.default_rng([zlib.crc32(name.encode()), seed]).standard_normal(out[name].shape)
        drawn = base * np.exp(spread * noise) if base else spread * noise
        out[name] = __import__('jax').numpy.asarray(drawn.astype(out[name].dtype))
    for name, factor in factors.items():
        out[name] = (out[name] * factor).astype(out[name].dtype)
    return out
```

```python
from contextlib import ExitStack

import numpy as np
import concourse.bass as bass
from concourse import mybir

F32 = mybir.dt.float32
FR = mybir.dt.float32r
ACT = mybir.ActivationFunctionType
ALU = mybir.AluOpType
AX = mybir.AxisListType.X

P = 128
D = 1024
KD = D // P
LAT, CTX, PAST = 1024, 256, 256
T = LAT + CTX
NT = T // P
CHUNKS = ((0, 448), (448, 896), (896, 1280))
C2 = LAT - CHUNKS[2][0]
HEADS, DH = 8, 64
NAW = HEADS * DH
KH, KW, GW = 8, 16, 64
ROWS = LAT // GW
PW = CW = D // 4
CONV_K = 31
HALF = CONV_K // 2
HID = 2816
BLOCKS = HID // (2 * P)
EPS = 1e-6
NEG = -1e30
N_IN = 3 * NAW + PW + 2 * CW + 3 * D
P_COL, A_COL, G_COL, GATE_COL = 3 * NAW, 3 * NAW + PW, 3 * NAW + PW + CW, 3 * NAW + PW + 2 * CW
OFF = {}
_at = 0
for _name, _n in (("c", 2 * KD), ("b_mod", 6 * KD), ("norm1_g", KD), ("norm2_g", KD), ("final_g", KD),
                  ("b_gate", 3 * KD), ("pool_scale", 2), ("b_dw", 2), ("cn_g", 2), ("cn_b", 2),
                  ("w_dw", 2 * CONV_K)):
    OFF[_name] = _at
    _at += _n
NCOLS = _at
CB = HALF + LAT + HALF + CTX + HALF
CV = LAT + HALF + CTX
CCTX = LAT + HALF
PB = 8 + LAT + 16 + CTX + 8
PCTX = 8 + LAT + 16
SLOTS = 14
WIN = 10


class Ctx:
    pass


def chunk_views(ps, sbuf_row):
    n = CHUNKS[0][1]
    return ((ps[:, 0:2, 0:n], sbuf_row[:, 0:2 * n].rearrange("p (c n) -> p c n", c=2)),
            (ps[:, 2, 0:T - 2 * n], sbuf_row[:, 2 * n:T]))


def gemm(nc, ps, wh, wl, ah, al, ktiles, first=True, last=True):
    for n, (w0, k) in enumerate(ktiles):
        for part, (w, a) in enumerate(((wh, ah), (wh, al), (wl, ah))):
            for c, (c0, c1) in enumerate(CHUNKS):
                mm = nc.tensor.matmul(ps[:, c, 0:c1 - c0], w[:, w0:w0 + P], a[:, k, c0:c1],
                                      start=(first and n == 0 and part == 0),
                                      stop=(last and n == len(ktiles) - 1 and part == 2))
    return mm


def phase_input(g):
    nc = g.nc
    with ExitStack() as ctx:
        sb = lambda name, shape, dt=F32: ctx.enter_context(nc.sbuf_tensor(name, shape, dt))
        sem = lambda name: ctx.enter_context(nc.semaphore(name))
        XT = sb("XT0", [P, KD, T])
        x_rows = sb("x_rows", [P, NT, D])
        w_mod_sb = sb("w_mod_sb", [P, 2, KD * 2 * P])
        square = sb("square0", [P, 2, 512])
        sumsq = sb("sumsq0", [P, T])
        rstd = sb("rstd0", [P, T])
        normed = sb("normed0", [P, 2, T])
        cs = sb("silu_c", [P, 2 * KD])
        const_in, x_in0, x_in1, x_in2 = sem("const_in"), sem("x_in0"), sem("x_in1"), sem("x_in2")
        x_in = (x_in0, x_in1, x_in2)
        w_in = (sem("wmod_in0"), sem("wmod_in1"))
        w_used, mod_done, mod_ready = sem("wmod_used"), sem("mod_done"), sem("mod_ready")
        ones_ready, silu_ready, turned, xt_ready = sem("ones_ready"), sem("silu_ready"), sem("turned"), sem("xt_ready")
        sq_ready, sq_added, stat_done, root_ready = sem("sq_ready"), sem("sq_added"), sem("stat_done"), sem("root_ready")
        rstd_ready, scaled, t_ready, ah_ready, al_ready = (sem("rstd_ready"), sem("scaled"), sem("t_ready"),
                                                           sem("ah_ready"), sem("al_ready"))
        acc_zero, mod_step, spilled = sem("acc_zero"), sem("mod_step"), sem("spilled")
        groups = [(0, 4), (4, 8), (8, 10)]
        banks = [g.ps[:, n // 3, n % 3, :] for n in range(6)]
        modp = g.aux[:, 0, 0:2 * 6 * KD]
        NG = 6 * D // (2 * P)
        with nc.Block() as block:

            @block.sync
            def _(sp):
                sp.dma_start(g.cols[:, :], g.d["cols"]).then_inc(const_in, 16)
                sp.dma_start(g.ident[:, :], g.d["ident"]).then_inc(const_in, 16)
                for n, (a, b) in enumerate(groups[:2]):
                    sp.dma_start(x_rows[:, a:b, :], g.d["x_sample"][a * P:b * P, :].rearrange("(t p) n -> p t n", p=P)).then_inc(x_in[n], 16)
                sp.dma_start(x_rows[:, 8:10, :], g.d["x_prompt"].rearrange("(t p) n -> p t n", p=P)).then_inc(x_in[2], 16)
                wv = g.d["w_mod"].rearrange("(k p) n -> p k n", p=P)

                def load(i, b, col):
                    sp.dma_start(w_mod_sb[:, b, :].rearrange("p (k n) -> p k n", k=KD), wv[:, :, bass.ds(col, 2 * P)]).then_inc(w_in[b], 16)

                load(0, 0, 0)
                load(0, 1, 2 * P)
                with sp.Fori(1, NG // 2) as i:
                    for b in range(2):
                        sp.wait_ge(w_used, i * 2 + (b - 1))
                        load(i, b, i * (4 * P) + b * 2 * P)
                sp.wait_ge(xt_ready, 24)
                sp.dma_start(g.d["xT"].rearrange("k p t -> p k t"), XT[:, :, :]).then_inc(spilled, 16)
                sp.wait_ge(spilled, 16)

            @block.tensor
            def _(pe):
                pe.wait_ge(const_in, 32)
                for n in range(24):
                    gi, f = n // KD, n % KD
                    a, b = groups[gi]
                    if f == 0:
                        pe.wait_ge(x_in[gi], 16)
                    if n >= 6:
                        pe.wait_ge(xt_ready, n - 5)
                    for t in range(a, b):
                        mm = nc.tensor.transpose(banks[n % 6][:, (t - a) * P:(t - a + 1) * P],
                                                 x_rows[:, t, f * P:(f + 1) * P], g.ident[:, :])
                    mm.then_inc(turned, 1)
                pe.wait_ge(silu_ready, 1)
                with pe.Fori(0, NG // 2) as i:
                    for b in range(2):
                        pe.wait_ge(w_in[b], i * 16 + 16)
                        for m in range(2):
                            for k in range(KD):
                                mm = nc.tensor.matmul(modp[:, bass.ds(i * 8 + (b * 4 + m * 2), 2)],
                                                      w_mod_sb[:, b, k * 2 * P + m * P:k * 2 * P + (m + 1) * P],
                                                      cs[:, 2 * k:2 * k + 2], start=(k == 0), stop=(k == KD - 1))
                        mm.then_inc(w_used, 1)
                pe.wait_ge(xt_ready, 24)
                pe.wait_ge(sq_added, 24)
                pe.wait_ge(ones_ready, 1)
                for c, (c0, c1) in enumerate(CHUNKS):
                    mm = nc.tensor.matmul(g.ps[:, 0, c, 0:c1 - c0], g.ones[:, :], sumsq[:, c0:c1], start=True, stop=True)
                mm.then_inc(stat_done, 1)

            @block.scalar
            def _(act):
                act.wait_ge(const_in, 32)
                nc.scalar.activation(cs[:, :], g.cols[:, 0:2 * KD], ACT.Silu).then_inc(silu_ready, 1)
                for n in range(24):
                    gi, f = n // KD, n % KD
                    t0, t1 = groups[gi][0] * P, groups[gi][1] * P
                    act.wait_ge(xt_ready, n + 1)
                    if n >= 2:
                        act.wait_ge(sq_added, n - 1)
                    nc.scalar.activation(square[:, n % 2, 0:t1 - t0], XT[:, f, t0:t1], ACT.Square).then_inc(sq_ready, 1)
                act.wait_ge(stat_done, 1)
                root(g, act, rstd, root_ready)
                copies(g, act, normed, t_ready, ah_ready)

            @block.vector
            def _(dve):
                nc.vector.memset(g.ones[:, :], 1.0)
                nc.vector.memset(g.eps[:, :], EPS).then_inc(ones_ready, 1)
                for n in range(24):
                    gi, f = n // KD, n % KD
                    t0, t1 = groups[gi][0] * P, groups[gi][1] * P
                    dve.wait_ge(turned, n + 1)
                    nc.vector.tensor_copy(XT[:, f, t0:t1], banks[n % 6][:, 0:t1 - t0]).then_inc(xt_ready, 1)
                dve.wait_ge(w_used, NG)
                bm = g.cols[:, OFF["b_mod"]:OFF["b_mod"] + 6 * KD]
                nc.vector.tensor_tensor(g.mod[:, :, :], modp.rearrange("p (m j) -> p m j", j=2),
                                        bm.rearrange("p (m j) -> p m j", j=1).broadcast_to([P, 6 * KD, 2]), ALU.add).then_inc(mod_step, 1)
                dve.wait_ge(mod_step, 1)
                for n, (gain, part) in enumerate((("norm1_g", 1), ("norm2_g", 4))):
                    gv = g.cols[:, OFF[gain]:OFF[gain] + KD].rearrange("p (m j) -> p m j", j=1).broadcast_to([P, KD, 2])
                    nc.vector.scalar_tensor_tensor(g.gain[:, n, :, :], g.mod[:, part * KD:(part + 1) * KD, :], 1.0, gv,
                                                   ALU.add, ALU.mult).then_inc(mod_step, 1)
                dve.wait_ge(mod_step, 3)
                dve.wait_ge(root_ready, 2)
                nc.vector.reciprocal(rstd[:, :], rstd[:, :]).then_inc(rstd_ready, 1)
                dve.wait_ge(rstd_ready, 1)
                scale_shift(g, dve, XT, rstd, normed, 0, 0, scaled, t_ready, al_ready)

            @block.gpsimd
            def _(pool):
                nc.gpsimd.memset(sumsq[:, :], 0.0).then_inc(acc_zero, 1)
                pool.wait_ge(acc_zero, 1)
                for n in range(24):
                    t0, t1 = groups[n // KD][0] * P, groups[n // KD][1] * P
                    pool.wait_ge(sq_ready, n + 1)
                    if n:
                        pool.wait_ge(sq_added, n)
                    nc.gpsimd.tensor_tensor(sumsq[:, t0:t1], sumsq[:, t0:t1], square[:, n % 2, 0:t1 - t0], ALU.add).then_inc(sq_added, 1)
                rests(g, pool, normed, ah_ready, al_ready)


def root(g, act, rstd, root_ready):
    for ps, sb in chunk_views(g.ps[:, 0], rstd):
        g.nc.scalar.activation(sb, ps, ACT.Sqrt, bias=g.eps[:, 0:1], scale=1.0 / D).then_inc(root_ready, 1)


def scale_shift(g, dve, XT, rstd, normed, gain, shift_part, scaled, t_ready, al_ready):
    for f in range(KD):
        if f >= 2:
            dve.wait_ge(al_ready, f - 1)
        nc = g.nc
        nc.vector.tensor_tensor(normed[:, f % 2, :], XT[:, f, :], rstd[:, :], ALU.mult).then_inc(scaled, 1)
        dve.wait_ge(scaled, f + 1)
        for j, (a, b) in enumerate(((0, LAT), (LAT, T))):
            nc.vector.tensor_scalar(normed[:, f % 2, a:b], normed[:, f % 2, a:b], g.gain[:, gain, f, j:j + 1],
                                    g.mod[:, shift_part * KD + f, j:j + 1], ALU.mult, ALU.add).then_inc(t_ready, 1)


def copies(g, act, normed, t_ready, ah_ready):
    for f in range(KD):
        act.wait_ge(t_ready, 2 * (f + 1))
        g.nc.scalar.activation(g.AH[:, f, :], normed[:, f % 2, :], ACT.Copy).then_inc(ah_ready, 1)


def rests(g, pool, normed, ah_ready, al_ready):
    for f in range(KD):
        pool.wait_ge(ah_ready, f + 1)
        g.nc.gpsimd.tensor_tensor(g.AL[:, f, :], normed[:, f % 2, :], g.AH[:, f, :].bitcast(F32), ALU.subtract).then_inc(al_ready, 1)


class Weights:

    def __init__(self, g, ctx, tag):
        nc = g.nc
        self.g = g
        self.raw = ctx.enter_context(nc.sbuf_tensor(f"w_raw{tag}", [P, 2, KD * P], F32))
        self.hi = ctx.enter_context(nc.sbuf_tensor(f"w_hi{tag}", [P, 2, KD * P], FR))
        self.lo = ctx.enter_context(nc.sbuf_tensor(f"w_lo{tag}", [P, 2, KD * P], FR))
        self.raw_in = [ctx.enter_context(nc.semaphore(f"w_raw_in{b}{tag}")) for b in range(2)]
        self.hi_ready = ctx.enter_context(nc.semaphore(f"w_hi_ready{tag}"))
        self.lo_ready = ctx.enter_context(nc.semaphore(f"w_lo_ready{tag}"))
        self.used = ctx.enter_context(nc.semaphore(f"w_used{tag}"))

    def columns(self, slot, width):
        return self.raw[:, slot, :].rearrange("p (k n) -> p k n", n=width)


PIECES = ((0, 0, 448, 0), (1, 0, 448, 448), (2, 0, C2, 896), (2, C2, CTX, LAT))


def padded(tok, lead, ctx_at):
    return lead + tok if tok < LAT else ctx_at


def phase_mixers(g):
    nc = g.nc
    with ExitStack() as ctx:
        sb = lambda name, shape, dt=F32: ctx.enter_context(nc.sbuf_tensor(name, shape, dt))
        sem = lambda name: ctx.enter_context(nc.semaphore(name))
        W = Weights(g, ctx, "m")
        pad = sb("pad", [P, 2, CB])
        summed = sb("summed", [P, 2, CB])
        work = sb("work", [P, 2, CB])
        sig = sb("sig", [P, CB])
        evac = sb("evac", [P, 2, T])
        vt = sb("vt", [P, NT, P])
        kt_ctx = sb("kt_ctx", [P, 2, P])
        cached_k = sb("cached_k", [P, 2, NAW])
        cached_kT = sb("cached_kT", [P, 4, PAST])
        wp = sb("wp", [P, 2, P])
        inv = sb("inv", [P, T])
        free = (sem("set_free0"), sem("set_free1"))
        done = sem("small_products_done")
        ck_in, inv_in, inv_used, zeroed, wp_in = sem("ck_in"), sem("inv_in"), sem("inv_used"), sem("zeroed"), sem("wp_in")
        ck_turned, ck_out = sem("ck_turned"), sem("ck_out")
        pool_step, pooled = sem("pool_step"), sem("pooled")
        sig_ready, glu_ready, conv_step = sem("sig_ready"), sem("glu_ready"), sem("conv_step")
        centred, sq_ready, root_ready, ln_step, silu_ready = sem("centred"), sem("ln_sq"), sem("ln_root"), sem("ln_step"), sem("ln_silu")
        turned, tok_ready = sem("kv_turned"), sem("kv_token_major")
        stored = (sem("evac_stored0"), sem("evac_stored1"))
        tok_stored, ck_stored = sem("tok_stored"), sem("ck_stored")
        wv = g.d["w_in"].rearrange("(k p) n -> p k n", p=P)
        FIRST = [P_COL, P_COL + P, G_COL, A_COL, G_COL + P, A_COL + P]
        U_Q, U_K, U_V, UNITS = 6, 10, 14, 18
        USE_Q, USE_POOL, USE_K, USE_V, USE_LN = 3, 5, 6, 8, 10

        with nc.Block() as block:

            @block.sync
            def _(sp):
                def load(b, col):
                    sp.dma_start(W.columns(b, P), wv[:, :, bass.ds(col, P)]).then_inc(W.raw_in[b], 16)

                def store(b, dst, use):
                    sp.wait_ge(free[b], use)
                    sp.dma_start(dst.rearrange("a p t -> p (a t)"), evac[:, b, :]).then_inc(stored[b], 16)

                def load_inv(t):
                    for half in range(2):
                        sp.dma_start(inv[half * 64:(half + 1) * 64, :],
                                     g.d["inv_count"][2 * t + half:2 * t + half + 1, :].broadcast_to([64, T])).then_inc(inv_in, 16)

                load(0, FIRST[0])
                load(1, FIRST[1])
                sp.dma_start(cached_k[:, :, :], g.d["cache_k"].rearrange("(t p) n -> p t n", p=P)).then_inc(ck_in, 16)
                load_inv(0)
                sp.wait_ge(zeroed, 2)
                for q in range(4):
                    r = 64 * (q % 2)
                    sp.dma_start(wp[r:r + 64, q // 2, r:r + 64], g.d["w_pool"][q, :, :]).then_inc(wp_in, 16)
                for u in range(2, U_Q):
                    sp.wait_ge(W.lo_ready, u - 1)
                    load(u % 2, FIRST[u])
                sp.wait_ge(ck_out, 2)
                sp.dma_start(g.d["kT"][:, :, T:T + PAST].rearrange("a p t -> p a t"), cached_kT[:, :, :]).then_inc(ck_stored, 16)
                sp.wait_ge(inv_used, 2)
                load_inv(1)
                for b in range(2):
                    sp.wait_ge(W.lo_ready, U_Q + b - 1)
                    load(b, b * P)
                with sp.Fori(0, 2) as i:
                    for b in range(2):
                        sp.wait_ge(W.lo_ready, i * 2 + (U_Q + 2 + b - 1))
                        load(b, i * (2 * P) + (2 + b) * P)
                    for b in range(2):
                        store(b, g.d["qT"][bass.ds(i * 2 + b, 1), :, :], i + (USE_Q + 1))
                for b in range(2):
                    store(b, g.d["branch"][4 + b:5 + b, :, :], USE_POOL + 1)
                for i in range(2):
                    for b in range(2):
                        sp.wait_ge(W.lo_ready, i * 2 + (U_K + 2 + b - 1))
                        load(b, i * (2 * P) + (6 + b) * P)
                    for b in range(2):
                        store(b, g.d["kT"][bass.ds(i * 2 + b, 1), :, 0:T], i + (USE_K + 1))
                    for b in range(2):
                        col = i * (2 * P) + b * P
                        sp.wait_ge(tok_ready, i * 2 + (b + 2))
                        sp.dma_start(g.d["new_k"][:, bass.ds(col, P)].rearrange("(t p) n -> p t n", p=P),
                                     kt_ctx[:, :, :]).then_inc(tok_stored, 16)
                for b in range(2):
                    sp.wait_ge(W.lo_ready, UNITS - 2 + b - 1)
                    load(b, (10 + b) * P)
                for i in range(2):
                    for b in range(2):
                        col = bass.ds(i * (2 * P) + b * P, P)
                        sp.wait_ge(tok_ready, i * 6 + (5 + 3 * b + 3))
                        sp.dma_start(g.d["v"][:, col].rearrange("(t p) n -> p t n", p=P), vt[:, :, :]).then_inc(tok_stored, 16)
                        sp.dma_start(g.d["new_v"][:, col].rearrange("(t p) n -> p t n", p=P), vt[:, 8:10, :]).then_inc(tok_stored, 16)
                for b in range(2):
                    sp.wait_ge(silu_ready, 2 * b + 2)
                    sp.dma_start(g.d["branch"][6 + b, :, :], evac[:, b, :]).then_inc(stored[b], 16)
                sp.wait_ge(ck_stored, 16)
                sp.wait_ge(tok_stored, 16 * 12)
                for b in range(2):
                    sp.wait_ge(stored[b], 16 * 6)

            @block.tensor
            def _(pe):
                pe.wait_ge(ck_in, 16)
                for hp in range(4):
                    for t in range(2):
                        mm = nc.tensor.transpose(g.aux[:, hp // 2, (hp % 2) * 256 + t * P:(hp % 2) * 256 + (t + 1) * P],
                                                 cached_k[:, t, hp * P:(hp + 1) * P], g.ident[:, :])
                mm.then_inc(ck_turned, 1)

                def unit(s, w_count, uses):
                    pe.wait_ge(W.lo_ready, w_count)
                    pe.wait_ge(free[s], uses)
                    gemm(nc, g.ps[:, s], W.hi[:, s, :], W.lo[:, s, :], g.AH, g.AL,
                         [(k * P, k) for k in range(KD)]).then_inc(W.used, 1)

                for u in range(U_Q):
                    unit(u % 2, u + 1, u // 2)
                with pe.Fori(0, 2) as i:
                    for s in range(2):
                        unit(s, i * 2 + (U_Q + s + 1), i + USE_Q)
                pe.wait_ge(wp_in, 64)
                pe.wait_ge(pooled, 2)
                for t in range(2):
                    pe.wait_ge(free[t], USE_POOL)
                    for bank, c0, n, tok in PIECES:
                        at = padded(tok, 8, PCTX)
                        mm = nc.tensor.matmul(g.ps[:, t, bank, c0:c0 + n], wp[:, t, :], summed[:, t, at:at + n], start=True, stop=True)
                    mm.then_inc(done, 1)
                pe.wait_ge(ck_out, 2)
                with pe.Fori(0, 2) as i:
                    for s in range(2):
                        unit(s, i * 2 + (U_K + s + 1), i + USE_K)
                    for s in range(2):
                        pe.wait_ge(free[s], i + (USE_K + 1))
                        pe.wait_ge(tok_ready, i * 2 + (s + 1))
                        for t in range(2):
                            mm = nc.tensor.transpose(g.aux[:, 0, t * P:(t + 1) * P], evac[:, s, LAT + t * P:LAT + (t + 1) * P], g.ident[:, :])
                        mm.then_inc(turned, 1)
                with pe.Fori(0, 2) as i:
                    for s in range(2):
                        unit(s, i * 2 + (U_V + s + 1), i + USE_V)
                    for s in range(2):
                        pe.wait_ge(free[s], i + (USE_V + 1))
                        for part, (a, b) in enumerate(V_PARTS):
                            pe.wait_ge(tok_ready, i * 6 + (5 + 3 * s + (1 if part == 2 else 0)))
                            for t in range(a, b):
                                mm = nc.tensor.transpose(g.aux[:, part % 2, (t - a) * P:(t - a + 1) * P], evac[:, s, t * P:(t + 1) * P], g.ident[:, :])
                            mm.then_inc(turned, 1)
                pe.wait_ge(conv_step, 2 * CONV_K)
                pe.wait_ge(free[0], USE_LN)
                for bank, c0, n, tok in PIECES:
                    at = padded(tok, 0, CCTX)
                    for t in range(2):
                        mm = nc.tensor.matmul(g.ps[:, 0, bank, c0:c0 + n], g.ones[:, :], work[:, t, at:at + n], start=(t == 0), stop=(t == 1))
                mm.then_inc(done, 1)
                pe.wait_ge(sq_ready, 2)
                pe.wait_ge(free[1], USE_LN)
                for bank, c0, n, tok in PIECES:
                    at = padded(tok, 0, CCTX)
                    for t in range(2):
                        mm = nc.tensor.matmul(g.ps[:, 1, bank, c0:c0 + n], g.ones[:, :], summed[:, t, at:at + n], start=(t == 0), stop=(t == 1))
                mm.then_inc(done, 1)

            @block.scalar
            def _(act):
                def split(slot, raw_count, used=None):
                    act.wait_ge(W.raw_in[slot], raw_count)
                    if used is not None:
                        act.wait_ge(W.used, used)
                    nc.scalar.activation(W.hi[:, slot, :], W.raw[:, slot, :], ACT.Copy).then_inc(W.hi_ready, 1)

                def copy_out(s, scale=1.0):
                    for n, (ps, out) in enumerate(chunk_views(g.ps[:, s], evac[:, s, :])):
                        last = nc.scalar.activation(out, ps, ACT.Copy, scale=scale)
                    last.then_inc(free[s], 1)

                act.sem_inc(tok_ready, 1)
                split(0, 16)
                split(1, 16)
                act.wait_ge(ck_turned, 1)
                for h in range(2):
                    nc.scalar.activation(cached_kT[:, 2 * h:2 * h + 2, :], g.aux[:, h, :].rearrange("p (a t) -> p a t", a=2), ACT.Copy).then_inc(ck_out, 1)
                act.wait_ge(zeroed, 1)
                for u in range(U_Q):
                    if u in (0, 1):
                        act.wait_ge(W.used, u + 1)
                        for bank, c0, n, tok in PIECES:
                            at = padded(tok, 8, PCTX)
                            last = nc.scalar.activation(pad[:, u, at:at + n], g.ps[:, u, bank, c0:c0 + n], ACT.Copy)
                        last.then_inc(free[u], 1)
                    elif u in (2, 4):
                        act.wait_ge(W.used, u + 1)
                        if u == 4:
                            act.wait_ge(glu_ready, 1)
                        for ps, out in chunk_views(g.ps[:, 0], sig):
                            last = nc.scalar.activation(out, ps, ACT.Sigmoid)
                        last.then_inc(free[0], 1)
                    split(u % 2, 16 * (u // 2 + 2), u + 1)
                for i in range(2):
                    for s in range(2):
                        act.wait_ge(W.used, i * 2 + (U_Q + s + 1))
                        if i:
                            act.wait_ge(stored[s], i * 16)
                        copy_out(s)
                        split(s, i * 16 + 16 * (U_Q // 2 + 2), i * 2 + (U_Q + s + 1))
                for t in range(2):
                    act.wait_ge(done, t + 1)
                    act.wait_ge(stored[t], 32)
                    copy_out(t, g.cols[:, OFF["pool_scale"] + t:OFF["pool_scale"] + t + 1])
                for i in range(2):
                    for s in range(2):
                        act.wait_ge(W.used, i * 2 + (U_K + s + 1))
                        act.wait_ge(stored[s], i * 16 + 48)
                        if i:
                            act.wait_ge(turned, i * 2)
                        copy_out(s)
                        split(s, i * 16 + 16 * (U_K // 2 + 2), i * 2 + (U_K + s + 1))
                    for s in range(2):
                        act.wait_ge(turned, i * 2 + (s + 1))
                        if i or s:
                            act.wait_ge(tok_stored, i * 32 + 16 * s)
                        nc.scalar.activation(kt_ctx[:, :, :], g.aux[:, 0, 0:256].rearrange("p (t n) -> p t n", t=2), ACT.Copy).then_inc(tok_ready, 1)
                for i in range(2):
                    for s in range(2):
                        act.wait_ge(W.used, i * 2 + (U_V + s + 1))
                        act.wait_ge(stored[s], 16 * 5)
                        act.wait_ge(turned, 4 + 6 * i)
                        copy_out(s)
                        if i == 0:
                            split(s, 16 * (U_V // 2 + 2), U_V + s + 1)
                    for s in range(2):
                        for part, (a, b) in enumerate(V_PARTS):
                            act.wait_ge(turned, 4 + 6 * i + 3 * s + part + 1)
                            if part == 0:
                                act.wait_ge(tok_stored, 64 + 64 * i + 32 * s)
                            nc.scalar.activation(vt[:, a:b, :], g.aux[:, part % 2, 0:(b - a) * P].rearrange("p (t n) -> p t n", n=P), ACT.Copy).then_inc(tok_ready, 1)
                act.wait_ge(centred, 6)
                act.wait_ge(done, 2)
                for t in range(2):
                    nc.scalar.activation(summed[:, t, 0:CV], work[:, t, 0:CV], ACT.Square).then_inc(sq_ready, 1)
                act.wait_ge(done, 4)
                for bank, c0, n, tok in PIECES:
                    at = padded(tok, 0, CCTX)
                    nc.scalar.activation(sig[:, at:at + n], g.ps[:, 1, bank, c0:c0 + n], ACT.Sqrt, bias=g.eps[:, 0:1], scale=1.0 / CW).then_inc(root_ready, 1)
                act.wait_ge(turned, 16)
                for t in range(2):
                    act.wait_ge(ln_step, 2 + 2 * (t + 1))
                    for a, b, at in ((0, LAT, 0), (LAT, T, CCTX)):
                        nc.scalar.activation(evac[:, t, a:b], work[:, t, at:at + b - a], ACT.Silu, bias=g.cols[:, OFF["cn_b"] + t:OFF["cn_b"] + t + 1],
                                             scale=g.cols[:, OFF["cn_g"] + t:OFF["cn_g"] + t + 1]).then_inc(silu_ready, 1)

            @block.gpsimd
            def _(pool):
                with pool.Fori(0, UNITS // 2) as i:
                    for b in range(2):
                        pool.wait_ge(W.hi_ready, i * 2 + (b + 1))
                        nc.gpsimd.tensor_tensor(W.lo[:, b, :], W.raw[:, b, :], W.hi[:, b, :].bitcast(F32), ALU.subtract).then_inc(W.lo_ready, 1)

            @block.vector
            def _(dve):
                nc.vector.memset(pad[:, :, :], 0.0).then_inc(zeroed, 1)
                nc.vector.memset(wp[:, :, :], 0.0).then_inc(zeroed, 1)
                for s in range(2):
                    dve.wait_ge(free[s], 1)

                def window_sum(out, a, b):
                    nc.vector.tensor_tensor(out, a, b, ALU.add).then_inc(pool_step, 1)

                window_sum(summed[:, :, 1:PB], pad[:, :, 0:PB - 1], pad[:, :, 1:PB])
                dve.wait_ge(pool_step, 1)
                window_sum(work[:, :, 2:PB - 1], summed[:, :, 1:PB - 2], summed[:, :, 3:PB])
                dve.wait_ge(pool_step, 2)
                window_sum(summed[:, 1, 4:PB - 3], work[:, 1, 2:PB - 5], work[:, 1, 6:PB - 1])
                dve.wait_ge(pool_step, 3)
                window_sum(work[64:P, 1, 8:PB - 7], summed[64:P, 1, 4:PB - 11], summed[64:P, 1, 12:PB - 3])
                dve.wait_ge(pool_step, 4)
                for t in range(2):
                    dve.wait_ge(inv_in, 32 * (t + 1))
                    for src, r in ((summed, 0), (work, 64)):
                        for a, b, at in ((0, LAT, 8), (LAT, T, PCTX)):
                            nc.vector.tensor_tensor(summed[r:r + 64, t, at:at + b - a], src[r:r + 64, t, at:at + b - a], inv[r:r + 64, a:b], ALU.mult).then_inc(inv_used if a == LAT else pool_step, 1)
                    dve.wait_ge(inv_used, 2 * (t + 1))
                    nc.vector.tensor_tensor(summed[:, t, 8:PCTX + CTX], summed[:, t, 8:PCTX + CTX], pad[:, t, 8:PCTX + CTX], ALU.subtract).then_inc(pooled, 1)
                dve.wait_ge(pooled, 2)
                for a in (0, HALF + LAT, CB - HALF):
                    nc.vector.memset(pad[:, :, a:a + HALF], 0.0)
                for t in range(2):
                    dve.wait_ge(W.used, 4 + 2 * t)
                    dve.wait_ge(free[0], t + 2)
                    for bank, c0, n, tok in PIECES:
                        at = padded(tok, HALF, HALF + LAT + HALF)
                        last = nc.vector.tensor_tensor(pad[:, t, at:at + n], g.ps[:, 1, bank, c0:c0 + n], sig[:, tok:tok + n], ALU.mult)
                    last.then_inc(free[1], 1)
                    dve.wait_ge(free[1], t + 2)
                    dve.sem_inc(glu_ready, 1)
                wd, bd = OFF["w_dw"], OFF["b_dw"]
                for t in range(2):
                    nc.vector.tensor_scalar(work[:, t, 0:CV], pad[:, t, 0:CV], g.cols[:, wd + t * CONV_K:wd + t * CONV_K + 1],
                                            g.cols[:, bd + t:bd + t + 1], ALU.mult, ALU.add).then_inc(conv_step, 1)
                with dve.Fori(1, CONV_K) as k:
                    for t in range(2):
                        dve.wait_ge(conv_step, k * 2 + (t - 1))
                        nc.vector.scalar_tensor_tensor(work[:, t, 0:CV], pad[:, t, bass.ds(k, CV)], g.cols[:, bass.ds(k + (wd + t * CONV_K), 1)],
                                                       work[:, t, 0:CV], ALU.mult, ALU.add).then_inc(conv_step, 1)
                dve.wait_ge(done, 3)
                for t in range(2):
                    w = work[:, t, :]
                    for ps, x in ((g.ps[:, 0, 0:2, 0:448], w[:, 0:896].rearrange("p (c n) -> p c n", c=2)),
                                  (g.ps[:, 0, 2, 0:C2], w[:, 896:LAT]), (g.ps[:, 0, 2, C2:C2 + CTX], w[:, CCTX:CCTX + CTX])):
                        nc.vector.scalar_tensor_tensor(x, ps, -1.0 / CW, x, ALU.mult, ALU.add).then_inc(centred, 1)
                dve.wait_ge(root_ready, 4)
                for a, n in ((0, LAT), (CCTX, CTX)):
                    nc.vector.reciprocal(sig[:, a:a + n], sig[:, a:a + n]).then_inc(ln_step, 1)
                dve.wait_ge(ln_step, 2)
                for t in range(2):
                    for a, n in ((0, LAT), (CCTX, CTX)):
                        nc.vector.tensor_tensor(work[:, t, a:a + n], work[:, t, a:a + n], sig[:, a:a + n], ALU.mult).then_inc(ln_step, 1)


V_PARTS = ((0, 4), (4, 8), (8, 10))


QT = NT
LOCAL = WIN * GW
PCOLS = LOCAL + PAST


def tile_plan(n):
    if n >= LAT // P:
        return None
    start = min(max(2 * n - KH // 2, 0), ROWS - KH)
    inner = 0 < 2 * n + 1 - KH // 2 < ROWS - KH
    return start * GW, (LOCAL if inner else KH * GW), start - 2 * n + KH - 2, inner


def blocks(n):
    plan = tile_plan(n)
    if plan is None:
        return [], [(5, 8), (6, 9)]
    v0 = plan[0] // P
    return [(j, v0 + j) for j in range(4)], ([(4, v0 + 4)] if plan[3] else []) + [(5, NT), (6, NT + 1)]


def phase_attention(g):
    nc = g.nc
    with ExitStack() as ctx:
        sb = lambda name, shape, dt=F32: ctx.enter_context(nc.sbuf_tensor(name, shape, dt))
        sem = lambda name: ctx.enter_context(nc.semaphore(name))
        KW_ = T + PAST
        q_src = sb("q_src", [P, T])
        k_src = sb("k_src", [P, KW_])
        v_src = sb("v_src", [P, NT + 2, DH])
        b_src = sb("b_src", [P, SLOTS, GW])
        QS = sb("QS", [P, 2, T], FR)
        KA = sb("KA", [P, 2, KW_], FR)
        KB = sb("KB", [P, 2, KW_], FR)
        VV = sb("VV", [P, 2, NT + 2, 2 * DH], FR)
        bias = sb("bias", [P, 2, SLOTS + WIN, GW])
        col_mask = sb("col_mask", [P, GW])
        prob = sb("prob", [P, 4, PCOLS])
        PT = sb("PT", [P, 2, 7, 2 * P], FR)
        OT = sb("OT", [P, T])
        OLO = sb("OLO", [64, T])
        OUT = sb("OUT", [64, T])
        st = sb("softmax_cols", [P, 4, 6])
        psS = g.ps_all[:, 0:4, :].rearrange("p (s b) n -> p s (b n)", s=2)
        psT = g.ps_all[:, 4:6, :].rearrange("p b n -> p (b n)")
        psV = g.ps_all[:, 6:8, :]
        q_in, k_in, v_in, b_in, mask_in = sem("q_in"), sem("k_in"), sem("v_in"), sem("b_in"), sem("mask_in")
        q_hi, q_lo, k_hi, k_lo, v_hi, v_lo = sem("q_hi"), sem("q_lo"), sem("k_hi"), sem("k_lo"), sem("v_hi"), sem("v_lo")
        table, table_ready = sem("bias_table"), sem("bias_ready")
        scored, max_step, max_ready, exp_ready, sum_step, sum_ready, normal = (
            sem("scored"), sem("max_step"), sem("max_ready"), sem("exp_ready"), sem("sum_step"), sem("sum_ready"), sem("normalised"))
        t_done, p_hi, p_lo = (sem("t_done0"), sem("t_done1")), (sem("p_hi0"), sem("p_hi1")), (sem("p_lo0"), sem("p_lo1"))
        times_v, summed_v, olo_ready, out_ready, out_stored = (sem("times_v"), sem("summed_v"), sem("olo_ready"),
                                                               sem("out_ready"), sem("out_stored"))
        passed = sem("pool_wait_passed")
        NL = LAT // P
        LAST = 2 * QT
        TURN, TIMES = 3, 4

        def tile(i, s):
            return None if isinstance(i, int) and i * LAST + s < 0 else (i, s)

        def b0(gs2, s):
            return gs2 * (2 * NL) + (s // QT) * NL + min(s % QT, NL)

        def wait(eng, semaphore, value):
            if not isinstance(value, int) or value > 0:
                eng.wait_ge(semaphore, value)

        q_rows = g.d["qT"].rearrange("a p t -> (a p) t")
        k_rows = g.d["kT"].rearrange("a p t -> (a p) t")
        out_rows = g.d["branch"].rearrange("a p t -> (a p) t")

        def head_pairs(eng, body):
            body(0, True)
            with eng.Fori(1, HEADS // 2 - 1) as i:
                body(i, True)
            body(HEADS // 2 - 1, False)

        with nc.Block() as block:

            @block.sync
            def _(sp):
                def load(h, i, b):
                    sp.wait_ge(k_lo, h)
                    for half in range(2):
                        sp.dma_start(k_src[half * 64:half * 64 + 64, :], k_rows[bass.ds(i * P + b * 64, 64), :]).then_inc(k_in, 16)
                    sp.wait_ge(q_lo, h)
                    for half in range(2):
                        sp.dma_start(q_src[half * 64:half * 64 + 64, :], q_rows[bass.ds(i * P + b * 64, 64), :]).then_inc(q_in, 16)
                    sp.wait_ge(v_lo, h)
                    sp.dma_start(v_src[:, 0:NT, :], g.d["v"][:, bass.ds(i * P + b * 64, 64)].rearrange("(t p) n -> p t n", p=P)).then_inc(v_in, 16)
                    sp.dma_start(v_src[:, NT:NT + 2, :], g.d["cache_v"][:, bass.ds(i * P + b * 64, 64)].rearrange("(t p) n -> p t n", p=P)).then_inc(v_in, 16)
                    sp.wait_ge(table, h)
                    for half in range(2):
                        sp.dma_start(b_src[half * 64:half * 64 + 64, :, :], rpb_window(g, i, b, 1 - half)).then_inc(b_in, 16)

                sp.dma_start(col_mask[:, :], g.d["col_mask"]).then_inc(mask_in, 16)
                load(0, 0, 0)
                load(1, 0, 1)

                def pair(i, more):
                    for b in range(2):
                        if more:
                            load(i * 2 + (b + 2), i + 1, b)
                        sp.wait_ge(out_ready, i * 2 + (b + 1))
                        sp.dma_start(out_rows[bass.ds(i * P + b * 64, 64), :], OUT[:, :]).then_inc(out_stored, 16)

                for i in range(HEADS // 2):
                    pair(i, i < HEADS // 2 - 1)
                sp.wait_ge(out_stored, 16 * HEADS)

            @block.tensor
            def _(pe):
                def scores(i, s):
                    b, n = s // QT % 2, s % QT
                    if n == 0:
                        pe.wait_ge(q_lo, i * 2 + (b + 1))
                        pe.wait_ge(k_lo, i * 2 + (b + 1))
                    wait(pe, exp_ready, i * LAST + (s - 1))
                    q = QS[:, b, n * P:(n + 1) * P]
                    plan = tile_plan(n)
                    regions = [(LOCAL, LOCAL + PAST, T if plan else LAT)]
                    if plan:
                        regions.insert(0, (0, 512, plan[0]))
                        if plan[3]:
                            regions.insert(1, (512, LOCAL, plan[0] + 512))
                    for c0, c1, k0 in regions:
                        for m, K in enumerate((KA, KB)):
                            mm = nc.tensor.matmul(psS[:, s % 2, c0:c1], q, K[:, b, k0:k0 + c1 - c0], start=(m == 0), stop=(m == 1))
                    mm.then_inc(scored, 1)

                def turn(i, s):
                    n = s % QT
                    pe.wait_ge(normal, i * LAST + (s + 1))
                    for bank, bl in enumerate(blocks(n)):
                        if bl:
                            wait(pe, p_lo[bank], b0(i, s) if bank == 0 else i * LAST + s)
                            for j, _ in bl:
                                mm = nc.tensor.transpose(psT[:, j * P:(j + 1) * P], prob[:, s % 4, j * P:(j + 1) * P], g.ident[:, :])
                            mm.then_inc(t_done[bank], 1)

                def value(i, s):
                    b, n = s // QT % 2, s % QT
                    if n == 0:
                        pe.wait_ge(v_lo, i * 2 + (s // QT + 1))
                    if n < NL:
                        pe.wait_ge(p_lo[0], b0(i, s) + 1)
                    pe.wait_ge(p_lo[1], i * LAST + (s + 1))
                    wait(pe, summed_v, i * LAST + (s - 1))
                    both = sum(blocks(n), [])
                    for m, (j, v) in enumerate(both):
                        mm = nc.tensor.matmul(psV[:, s % 2, 0:2 * P], VV[:, b, v, :], PT[:, s % 2, j, :], start=(m == 0), stop=(m == len(both) - 1))
                    mm.then_inc(times_v, 1)

                def pair(i, more):
                    for s in range(LAST if more else LAST + TIMES):
                        if s < LAST:
                            scores(i, s)
                        if tile(i, s - TURN) and s - TURN < LAST:
                            turn(i, s - TURN)
                        if tile(i, s - TIMES):
                            value(i, s - TIMES)

                head_pairs(pe, pair)

            @block.scalar
            def _(act):
                def prepare(what, h, b):
                    if what == "k":
                        act.wait_ge(k_in, h * 32 + 32)
                        nc.scalar.activation(KA[:, b, :], k_src[:, :], ACT.Copy).then_inc(k_hi, 1)
                    elif what == "q":
                        act.wait_ge(q_in, h * 32 + 32)
                        nc.scalar.activation(QS[:, b, :], q_src[:, :], ACT.Copy, scale=DH ** -0.5).then_inc(q_hi, 1)
                    elif what == "v":
                        act.wait_ge(v_in, h * 32 + 32)
                        nc.scalar.activation(VV[:, b, :, 0:DH], v_src[:, :, :], ACT.Copy).then_inc(v_hi, 1)

                def exponential(i, s):
                    plan = tile_plan(s % QT)
                    act.wait_ge(max_ready, i * LAST + (s + 1))
                    c = st[:, s % 4, :]
                    pr = prob[:, s % 4, :]
                    if plan:
                        nc.scalar.activation(pr[:, 0:plan[1]], pr[:, 0:plan[1]], ACT.Exp, bias=c[:, 2:3], accum_out=c[:, 3:4])
                    nc.scalar.activation(pr[:, LOCAL:PCOLS], psS[:, s % 2, LOCAL:PCOLS], ACT.Exp, bias=c[:, 2:3], accum_out=c[:, 4:5]).then_inc(exp_ready, 1)

                def upper(i, s):
                    n = s % QT
                    wait(act, times_v, i * LAST + (s - 1))
                    for bank, bl in enumerate(blocks(n)):
                        if bl:
                            act.wait_ge(t_done[bank], (b0(i, s) if bank == 0 else i * LAST + s) + 1)
                            j0, j1 = bl[0][0], bl[-1][0] + 1
                            nc.scalar.activation(PT[:, s % 2, j0:j1, 0:P], psT[:, j0 * P:j1 * P].rearrange("p (j n) -> p j n", n=P), ACT.Copy).then_inc(p_hi[bank], 1)

                def pair(i, more):
                    for s in range(LAST if more else LAST + TIMES):
                        if tile(i, s - TURN) and s - TURN < LAST:
                            upper(i, s - TURN)
                        if s < LAST:
                            exponential(i, s)
                        if s in (5, 6, 7):
                            prepare("kqv"[s - 5], i * 2 + 1, 1)
                        if more and s - QT in (5, 6, 7):
                            prepare("kqv"[s - QT - 5], i * 2 + 2, 0)
                        done = tile(i, s - TIMES - QT + 1)
                        if done and (s - TIMES - QT + 1) % QT == 0:
                            h = (s - TIMES - QT + 1) // QT
                            act.wait_ge(summed_v, i * LAST + QT * (h + 1))
                            wait(act, out_ready, i * 2 + h)
                            nc.scalar.activation(OLO[:, :], OT[64:P, :], ACT.Copy).then_inc(olo_ready, 1)

                for w in "kqv":
                    prepare(w, 0, 0)
                head_pairs(act, pair)

            @block.vector
            def _(dve):
                def prepare(what, h, b):
                    if what == "q":
                        dve.wait_ge(q_hi, h + 1)
                        r = 64 if b == 0 else 0
                        nc.vector.scalar_tensor_tensor(QS[r:r + 64, b, :], q_src[r:r + 64, :], DH ** -0.5, QS[r:r + 64, b, :].bitcast(F32),
                                                       ALU.mult, ALU.subtract).then_inc(q_lo, 1)
                    else:
                        dve.wait_ge(b_in, h * 32 + 32)
                        nc.vector.tensor_tensor(bias[:, b, 0:SLOTS, :], b_src[:, :, ::-1],
                                                col_mask[:, :].rearrange("p (a n) -> p a n", a=1).broadcast_to([P, SLOTS, GW]), ALU.add).then_inc(table, 1)
                        nc.vector.memset(bias[0:64, b, SLOTS + KH:SLOTS + WIN, :], NEG)
                        nc.vector.memset(bias[64:P, b, SLOTS:SLOTS + 1, :], NEG)
                        nc.vector.memset(bias[64:P, b, SLOTS + KH + 1:SLOTS + WIN, :], NEG)
                        dve.wait_ge(table, h + 1)
                        nc.vector.tensor_copy(bias[0:64, b, SLOTS:SLOTS + KH, :], bias[0:64, b, KH // 2 - 2:KH // 2 - 2 + KH, :])
                        nc.vector.tensor_copy(bias[64:P, b, SLOTS + 1:SLOTS + KH + 1, :], bias[64:P, b, KH // 2 - 1:KH // 2 - 1 + KH, :]).then_inc(table_ready, 1)

                def maximum(i, s):
                    b, n = s // QT % 2, s % QT
                    plan = tile_plan(n)
                    dve.wait_ge(scored, i * LAST + (s + 1))
                    wait(dve, t_done[1], i * LAST + (s - 3))
                    c = st[:, s % 4, :]
                    if not plan:
                        nc.vector.tensor_reduce(c[:, 2:3], psS[:, s % 2, LOCAL:PCOLS], AX, ALU.max, negate=True).then_inc(max_ready, 1)
                        return
                    if n == 0:
                        dve.wait_ge(table_ready, i * 2 + (b + 1))
                    slot = SLOTS if plan[3] else plan[2]
                    nc.vector.tensor_reduce(c[:, 1:2], psS[:, s % 2, LOCAL:PCOLS], AX, ALU.max).then_inc(max_step, 1)
                    nc.vector.tensor_tensor_reduce(prob[:, s % 4, 0:plan[1]], psS[:, s % 2, 0:plan[1]],
                                                   bias[:, b, slot:slot + plan[1] // GW, :].rearrange("p a n -> p (a n)"),
                                                   1.0, -3.0e38, ALU.add, ALU.max, c[:, 0:1]).then_inc(max_step, 1)
                    dve.wait_ge(max_step, 2 * (b0(i, s) + 1))
                    nc.vector.tensor_scalar(c[:, 2:3], c[:, 0:1], c[:, 1:2], -1.0, ALU.max, ALU.mult).then_inc(max_ready, 1)

                def total(i, s):
                    c = st[:, s % 4, :]
                    dve.wait_ge(exp_ready, i * LAST + (s + 1))
                    if tile_plan(s % QT):
                        nc.vector.tensor_tensor(c[:, 4:5], c[:, 3:4], c[:, 4:5], ALU.add).then_inc(sum_step, 1)
                        dve.wait_ge(sum_step, b0(i, s) + 1)
                    nc.vector.reciprocal(c[:, 5:6], c[:, 4:5]).then_inc(sum_ready, 1)

                def lower(i, s):
                    for bank, bl in enumerate(blocks(s % QT)):
                        if bl:
                            dve.wait_ge(p_hi[bank], (b0(i, s) if bank == 0 else i * LAST + s) + 1)
                            j0, j1 = bl[0][0], bl[-1][0] + 1
                            nc.vector.tensor_tensor(PT[:, s % 2, j0:j1, P:2 * P], psT[:, j0 * P:j1 * P].rearrange("p (j n) -> p j n", n=P),
                                                    PT[:, s % 2, j0:j1, 0:P].bitcast(F32), ALU.subtract).then_inc(p_lo[bank], 1)

                def gather(i, s):
                    n = s % QT
                    dve.wait_ge(times_v, i * LAST + (s + 1))
                    if n == 0:
                        wait(dve, out_ready, i * 2 + s // QT)
                    nc.vector.tensor_reduce(OT[:, n * P:(n + 1) * P], psV[:, s % 2, 0:2 * P].rearrange("p (a q) -> p q a", a=2), AX, ALU.add).then_inc(summed_v, 1)

                def pair(i, more):
                    for s in range(LAST if more else LAST + TIMES):
                        if s < LAST:
                            maximum(i, s)
                        if tile(i, s - 1) and s - 1 < LAST:
                            total(i, s - 1)
                        if tile(i, s - TURN) and s - TURN < LAST:
                            lower(i, s - TURN)
                        if tile(i, s - TIMES):
                            gather(i, s - TIMES)
                        if s in (6, 7):
                            prepare("qb"[s - 6], i * 2 + 1, 1)
                        if more and s - QT in (6, 7):
                            prepare("qb"[s - QT - 6], i * 2 + 2, 0)
                        if tile(i, s - TIMES - QT + 1) and (s - TIMES - QT + 1) % QT == 0:
                            h = (s - TIMES - QT + 1) // QT
                            dve.wait_ge(olo_ready, i * 2 + (h + 1))
                            wait(dve, out_stored, i * 32 + 16 * h)
                            nc.vector.tensor_tensor(OUT[:, :], OT[0:64, :], OLO[:, :], ALU.add).then_inc(out_ready, 1)

                dve.wait_ge(mask_in, 16)
                for w in "qb":
                    prepare(w, 0, 0)
                head_pairs(dve, pair)

            @block.gpsimd
            def _(pool):
                def prepare(what, h, b):
                    if what == "k":
                        pool.wait_ge(k_hi, h + 1)
                        nc.gpsimd.tensor_tensor(KB[:, b, :], k_src[:, :], KA[:, b, :].bitcast(F32), ALU.subtract).then_inc(k_lo, 1)
                    elif what == "v":
                        pool.wait_ge(v_hi, h + 1)
                        nc.gpsimd.tensor_tensor(VV[:, b, :, DH:2 * DH], v_src[:, :, :], VV[:, b, :, 0:DH].bitcast(F32), ALU.subtract).then_inc(v_lo, 1)

                def normalise(i, s):
                    plan = tile_plan(s % QT)
                    pool.wait_ge(sum_ready, i * LAST + (s + 1))
                    pool.sem_inc(passed, 1)
                    c, pr = st[:, s % 4, :], prob[:, s % 4, :]
                    if plan and not plan[3]:
                        nc.gpsimd.tensor_scalar(pr[:, 0:plan[1]], pr[:, 0:plan[1]], c[:, 5:6], 1.0, ALU.mult, ALU.mult)
                    a = 0 if plan and plan[3] else LOCAL
                    nc.gpsimd.tensor_scalar(pr[:, a:PCOLS], pr[:, a:PCOLS], c[:, 5:6], 1.0, ALU.mult, ALU.mult).then_inc(normal, 1)

                def pair(i, more):
                    for s in range(LAST if more else LAST + 1):
                        if tile(i, s - 1):
                            normalise(i, s - 1)
                        if s in (5, 7):
                            prepare("k" if s == 5 else "v", i * 2 + 1, 1)
                        if more and s - QT in (5, 7):
                            prepare("k" if s - QT == 5 else "v", i * 2 + 2, 0)

                for w in "kv":
                    prepare(w, 0, 0)
                head_pairs(pool, pair)


def rpb_window(g, i, b, first):
    rpb = g.d["rpb"]
    rows, width = 2 * KH - 1, 2 * GW - 1
    return bass.AP(tensor=rpb.tensor, offset=rpb.offset + ((2 * i + b) * rows + first) * width,
                   ap=[[1, GW], [width, SLOTS], [1, GW]])


def phase_merge(g):
    nc = g.nc
    with ExitStack() as ctx:
        sb = lambda name, shape, dt=F32: ctx.enter_context(nc.sbuf_tensor(name, shape, dt))
        sem = lambda name: ctx.enter_context(nc.semaphore(name))
        W = Weights(g, ctx, "g")
        BH = sb("BH", [P, KD, T], FR)
        BL = sb("BL", [P, KD, T], FR)
        stage = sb("branch_stage", [P, T])
        gate = sb("gate", [P, T])
        total = sb("total", [P, T])
        part = sb("part", [P, T])
        b_in, b_hi, b_lo = sem("b_in"), sem("b_hi"), sem("b_lo")
        gate_ready, free0, free1 = sem("gate_ready"), sem("merge_free0"), sem("merge_free1")
        part_ready, part_added, stored = sem("part_ready"), sem("part_added"), sem("merged_stored")
        passed = sem("sync_wait_passed")
        wv = g.d["w_in"].rearrange("(k p) n -> p k n", p=P)
        proj = {0: ("w_oa", 4, 0), 1: ("w_ob", 2, 4), 2: ("w_oc", 2, 6)}
        kts = [KD, 4, KD, 2, KD, 2]

        with nc.Block() as block:

            @block.sync
            def _(sp):
                def load(i, j):
                    b = j % 2
                    if b == 0:
                        src = wv[:, :, bass.ds(i * P + (GATE_COL + (j // 2) * D), P)]
                    else:
                        name = proj[j // 2][0]
                        src = g.d[name].rearrange("(k p) n -> p k n", p=P)[:, :, bass.ds(i * P, P)]
                    sp.dma_start(W.raw[:, b, 0:kts[j] * P].rearrange("p (k n) -> p k n", n=P), src).then_inc(W.raw_in[b], 16)

                load(0, 0)
                load(0, 1)
                for k in range(KD):
                    sp.wait_ge(b_lo, k)
                    sp.dma_start(stage[:, :], g.d["branch"][k, :, :]).then_inc(b_in, 16)
                    if k in (3, 7):
                        sp.wait_ge(W.lo_ready, 1 if k == 3 else 2)
                        load(0, 2 if k == 3 else 3)
                for j in (4, 5):
                    sp.wait_ge(W.lo_ready, j - 1)
                    load(0, j)
                with sp.Fori(0, KD - 1) as i:
                    for j in range(6):
                        sp.wait_ge(W.lo_ready, i * 6 + (j + 5))
                        if j % 2:
                            sp.sem_inc(passed, 1)
                        load(i + 1, j)
                    sp.wait_ge(part_added, i * 2 + 2)
                    sp.dma_start(g.d["merged"][bass.ds(i, 1), :, :].rearrange("a p t -> p (a t)"), total[:, :]).then_inc(stored, 16)
                sp.wait_ge(part_added, 2 * KD)
                sp.dma_start(g.d["merged"][KD - 1, :, :], total[:, :]).then_inc(stored, 16)
                sp.wait_ge(stored, 16 * KD)

            @block.tensor
            def _(pe):
                def tile(i, skip):
                    for j in range(6):
                        s = j % 2
                        pe.wait_ge(W.lo_ready, i * 6 + (j + 1))
                        pe.wait_ge((free0, free1)[s], i * 3 + j // 2)
                        if s == 0:
                            ah, al, k0 = g.AH, g.AL, 0
                        else:
                            ah, al, k0 = BH, BL, proj[j // 2][2]
                            if skip:
                                pe.wait_ge(b_lo, k0 + kts[j])
                        gemm(nc, g.ps[:, s], W.hi[:, s, :], W.lo[:, s, :], ah, al,
                             [(k * P, k0 + k) for k in range(kts[j])]).then_inc(W.used, 1)

                tile(0, True)
                with pe.Fori(1, KD) as i:
                    tile(i, False)

            @block.scalar
            def _(act):
                def split(i, j, first=False):
                    b, n = j % 2, kts[j] * P
                    act.wait_ge(W.raw_in[b], i * 48 + 16 * (j // 2 + 1))
                    if not first:
                        act.wait_ge(W.used, i * 6 + (j - 1))
                    nc.scalar.activation(W.hi[:, b, 0:n], W.raw[:, b, 0:n], ACT.Copy).then_inc(W.hi_ready, 1)

                def gate_out(i, j):
                    act.wait_ge(W.used, i * 6 + (j + 1))
                    if not isinstance(i, int) or 3 * i + j:
                        act.wait_ge(free1, i * 3 + j // 2)
                    c = OFF["b_gate"] + (j // 2) * KD
                    for ps, out in chunk_views(g.ps[:, 0], gate):
                        last = nc.scalar.activation(out, ps, ACT.Sigmoid, bias=g.cols[:, bass.ds(i + c, 1)])
                    last.then_inc(free0, 1)

                def tile(i, following):
                    for j in range(6):
                        if j % 2 == 0:
                            gate_out(i, j)
                        if j + 2 < 6:
                            split(i, j + 2)
                        elif following:
                            split(i + 1, j - 4)

                split(0, 0, True)
                split(0, 1, True)
                for k in range(KD):
                    act.wait_ge(b_in, 16 * (k + 1))
                    nc.scalar.activation(BH[:, k, :], stage[:, :], ACT.Copy).then_inc(b_hi, 1)
                tile(0, True)
                with act.Fori(1, KD - 1) as i:
                    tile(i, True)
                tile(KD - 1, False)

            @block.gpsimd
            def _(pool):
                def lower(i, j):
                    b, n = j % 2, kts[j] * P
                    pool.wait_ge(W.hi_ready, i * 6 + (j + 1))
                    nc.gpsimd.tensor_tensor(W.lo[:, b, 0:n], W.raw[:, b, 0:n], W.hi[:, b, 0:n].bitcast(F32), ALU.subtract).then_inc(W.lo_ready, 1)

                lower(0, 0)
                lower(0, 1)
                for k in range(KD):
                    pool.wait_ge(b_hi, k + 1)
                    nc.gpsimd.tensor_tensor(BL[:, k, :], stage[:, :], BH[:, k, :].bitcast(F32), ALU.subtract).then_inc(b_lo, 1)
                for j in range(2, 6):
                    lower(0, j)
                with pool.Fori(1, KD) as i:
                    for j in range(6):
                        lower(i, j)

            @block.vector
            def _(dve):
                def tile(i):
                    for b in range(3):
                        dve.wait_ge(free0, i * 3 + (b + 1))
                        dve.wait_ge(W.used, i * 6 + (2 * b + 2))
                        if b == 0:
                            if not isinstance(i, int):
                                dve.wait_ge(stored, i * 16)
                        elif b == 2:
                            dve.wait_ge(part_added, i * 2 + 1)
                        out = total if b == 0 else part
                        for (ps, o), (_, x) in zip(chunk_views(g.ps[:, 1], out), chunk_views(g.ps[:, 1], gate)):
                            last = nc.vector.tensor_tensor(o, ps, x, ALU.mult)
                        last.then_inc(free1, 1)
                        if b:
                            dve.wait_ge(free1, i * 3 + (b + 1))
                            nc.vector.tensor_tensor(total[:, :], total[:, :], part[:, :], ALU.add).then_inc(part_added, 1)

                tile(0)
                with dve.Fori(1, KD) as i:
                    tile(i)


def residual(g, dve, XT, m, gate_part, s, free):
    nc = g.nc
    ps, x = g.ps[:, s], XT[:, m, :]
    for p, o, j in ((ps[:, 0:2, 0:448], x[..., 0:896].rearrange("p (c n) -> p c n", c=2), 0),
                    (ps[:, 2, 0:C2], x[..., 896:LAT], 0), (ps[:, 2, C2:C2 + CTX], x[..., LAT:T], 1)):
        last = nc.vector.scalar_tensor_tensor(o, p, g.mod[:, gate_part * KD + m, j:j + 1], o, ALU.mult, ALU.add)
    last.then_inc(free, 1)


def phase_output(g):
    nc = g.nc
    with ExitStack() as ctx:
        sb = lambda name, shape, dt=F32: ctx.enter_context(nc.sbuf_tensor(name, shape, dt))
        sem = lambda name: ctx.enter_context(nc.semaphore(name))
        XT = g.XT
        W = Weights(g, ctx, "o")
        stage = sb("merged_stage", [P, 2, T])
        square = sb("square1", [P, 2, T])
        sumsq = sb("sumsq1", [P, T])
        rstd = sb("rstd1", [P, T])
        normed = sb("normed1", [P, 2, T])
        m_in = (sem("merged_in0"), sem("merged_in1"))
        m_hi, m_lo, x_in = sem("m_hi"), sem("m_lo"), sem("x_back")
        free = (sem("out_free0"), sem("out_free1"))
        zero, sq_ready, sq_added, stat_done = sem("out_zero"), sem("out_sq"), sem("out_sq_added"), sem("out_stat")
        root_ready, rstd_ready, scaled, t_ready, ah_ready, al_ready = (
            sem("out_root"), sem("out_rstd"), sem("out_scaled"), sem("out_t"), sem("out_ah"), sem("out_al"))
        wv = g.d["w_out"].rearrange("(k p) n -> p k n", p=P)
        with nc.Block() as block:

            @block.sync
            def _(sp):
                for m in range(2):
                    sp.dma_start(W.columns(m, P), wv[:, :, m * P:(m + 1) * P]).then_inc(W.raw_in[m], 16)
                for k in range(KD):
                    if k >= 2:
                        sp.wait_ge(m_lo, k - 1)
                    sp.dma_start(stage[:, k % 2, :], g.d["merged"][k, :, :]).then_inc(m_in[k % 2], 16)
                sp.dma_start(XT[:, :, :], g.d["xT"].rearrange("k p t -> p k t")).then_inc(x_in, 16)
                with sp.Fori(1, KD // 2) as i:
                    for b in range(2):
                        sp.wait_ge(W.lo_ready, i * 2 + (b - 1))
                        sp.dma_start(W.columns(b, P), wv[:, :, bass.ds(i * (2 * P) + b * P, P)]).then_inc(W.raw_in[b], 16)

            @block.tensor
            def _(pe):
                for m in range(2):
                    pe.wait_ge(W.lo_ready, m + 1)
                for k in range(KD):
                    pe.wait_ge(m_lo, k + 1)
                    for m in range(2):
                        mm = gemm(nc, g.ps[:, m], W.hi[:, m, :], W.lo[:, m, :], g.AH, g.AL, [(k * P, k)], first=k == 0, last=k == KD - 1)
                        if k == KD - 1:
                            mm.then_inc(W.used, 1)
                with pe.Fori(1, KD // 2) as i:
                    for s in range(2):
                        pe.wait_ge(W.lo_ready, i * 2 + (s + 1))
                        pe.wait_ge(free[s], i)
                        gemm(nc, g.ps[:, s], W.hi[:, s, :], W.lo[:, s, :], g.AH, g.AL, [(k * P, k) for k in range(KD)]).then_inc(W.used, 1)
                pe.wait_ge(sq_added, KD)
                pe.wait_ge(free[0], KD // 2)
                for c, (c0, c1) in enumerate(CHUNKS):
                    mm = nc.tensor.matmul(g.ps[:, 0, c, 0:c1 - c0], g.ones[:, :], sumsq[:, c0:c1], start=True, stop=True)
                mm.then_inc(stat_done, 1)

            @block.scalar
            def _(act):
                def split(m):
                    act.wait_ge(W.raw_in[m % 2], 16 * (m // 2 + 1))
                    if m >= 2:
                        act.wait_ge(W.used, m - 1)
                    nc.scalar.activation(W.hi[:, m % 2, :], W.raw[:, m % 2, :], ACT.Copy).then_inc(W.hi_ready, 1)

                split(0)
                split(1)
                for k in range(KD):
                    act.wait_ge(m_in[k % 2], 16 * (k // 2 + 1))
                    nc.scalar.activation(g.AH[:, k, :], stage[:, k % 2, :], ACT.Copy).then_inc(m_hi, 1)
                for m in range(KD):
                    if m + 2 < KD:
                        split(m + 2)
                    act.wait_ge(free[m % 2], m // 2 + 1)
                    if m >= 2:
                        act.wait_ge(sq_added, m - 1)
                    nc.scalar.activation(square[:, m % 2, :], XT[:, m, :], ACT.Square).then_inc(sq_ready, 1)
                act.wait_ge(stat_done, 1)
                root(g, act, rstd, root_ready)
                copies(g, act, normed, t_ready, ah_ready)

            @block.vector
            def _(dve):
                dve.wait_ge(x_in, 16)
                for m in range(KD):
                    dve.wait_ge(W.used, m + 1)
                    residual(g, dve, XT, m, 2, m % 2, free[m % 2])
                dve.wait_ge(root_ready, 2)
                nc.vector.reciprocal(rstd[:, :], rstd[:, :]).then_inc(rstd_ready, 1)
                dve.wait_ge(rstd_ready, 1)
                dve.wait_ge(free[0], KD // 2)
                dve.wait_ge(free[1], KD // 2)
                scale_shift(g, dve, XT, rstd, normed, 1, 3, scaled, t_ready, al_ready)

            @block.gpsimd
            def _(pool):
                nc.gpsimd.memset(sumsq[:, :], 0.0).then_inc(zero, 1)
                for m in range(2):
                    pool.wait_ge(W.hi_ready, m + 1)
                    nc.gpsimd.tensor_tensor(W.lo[:, m, :], W.raw[:, m, :], W.hi[:, m, :].bitcast(F32), ALU.subtract).then_inc(W.lo_ready, 1)
                for k in range(KD):
                    pool.wait_ge(m_hi, k + 1)
                    nc.gpsimd.tensor_tensor(g.AL[:, k, :], stage[:, k % 2, :], g.AH[:, k, :].bitcast(F32), ALU.subtract).then_inc(m_lo, 1)
                pool.wait_ge(zero, 1)
                for m in range(KD):
                    if m + 2 < KD:
                        pool.wait_ge(W.hi_ready, m + 3)
                        b = m % 2
                        nc.gpsimd.tensor_tensor(W.lo[:, b, :], W.raw[:, b, :], W.hi[:, b, :].bitcast(F32), ALU.subtract).then_inc(W.lo_ready, 1)
                    pool.wait_ge(sq_ready, m + 1)
                    if m:
                        pool.wait_ge(sq_added, m)
                    nc.gpsimd.tensor_tensor(sumsq[:, :], sumsq[:, :], square[:, m % 2, :], ALU.add).then_inc(sq_added, 1)
                rests(g, pool, normed, ah_ready, al_ready)


def phase_ffn(g):
    nc = g.nc
    with ExitStack() as ctx:
        sb = lambda name, shape, dt=F32: ctx.enter_context(nc.sbuf_tensor(name, shape, dt))
        sem = lambda name: ctx.enter_context(nc.semaphore(name))
        XT = g.XT
        W = Weights(g, ctx, "f")
        gated = sb("silu_a", [P, T])
        act32 = sb("act32", [P, 2, T])
        actH = sb("actH", [P, 2, T], FR)
        actL = sb("actL", [P, 2, T], FR)
        free = (sem("ffn_free0"), sem("ffn_free1"))
        hid_done, out_done = sem("hidden_done"), sem("down_done")
        a_ready, b_ready, h_hi, h_lo = sem("a_ready"), sem("b_ready"), sem("h_hi"), sem("h_lo")
        gu = g.d["w_gu"].rearrange("(k p) n -> p k n", p=P)
        down = g.d["w_down"].rearrange("(k p) n -> p k n", p=P)
        kinds = ("a0", "b0", "d0", "d1", "a1", "b1")
        with nc.Block() as block:

            def wcount(j, n):
                return j * 6 + (n - 1)

            @block.sync
            def _(sp):
                def load(j, kind):
                    b = int(kind in ("b0", "d1", "b1"))
                    if kind[0] == "d":
                        raw = W.raw[:, b, :].rearrange("p (k n) -> p k n", n=512)
                        src = down[:, bass.ds(j * 2 - 2, 2), b * 512:(b + 1) * 512]
                    else:
                        raw = W.columns(b, P)
                        src = gu[:, :, bass.ds(j * (2 * P) + (int(kind[1]) * P + (HID if kind[0] == "b" else 0)), P)]
                    sp.dma_start(raw, src).then_inc(W.raw_in[b], 16)

                for n, kind in enumerate(("a0", "b0", "a1", "b1")):
                    if n >= 2:
                        sp.wait_ge(W.lo_ready, n - 1)
                    load(0, kind)
                with sp.Fori(1, BLOCKS) as j:
                    for n, kind in enumerate(kinds):
                        sp.wait_ge(W.lo_ready, wcount(j, n) - 2)
                        load(j, kind)
                for b in range(2):
                    sp.wait_ge(W.lo_ready, wcount(BLOCKS, b) - 2)
                    load(BLOCKS, ("d0", "d1")[b])

            @block.tensor
            def _(pe):
                def hidden(s, w, uses):
                    pe.wait_ge(W.lo_ready, w)
                    pe.wait_ge(free[s], uses)
                    gemm(nc, g.ps[:, s], W.hi[:, s, :], W.lo[:, s, :], g.AH, g.AL, [(k * P, k) for k in range(KD)]).then_inc(W.used, 1)

                def output(j, w0, uses):
                    pe.wait_ge(h_lo, j * 2)
                    for m in range(KD):
                        s, ws = m % 2, m // 4
                        if m % 4 == 0:
                            pe.wait_ge(W.lo_ready, w0 + ws + 1)
                        pe.wait_ge(free[s], uses + m // 2)
                        mm = gemm(nc, g.ps[:, s], W.hi[:, ws, :], W.lo[:, ws, :], actH, actL, [(k * 512 + (m % 4) * P, k) for k in range(2)])
                        mm.then_inc(out_done, 1)
                        if m % 4 == 3:
                            pe.wait_ge(out_done, j * KD - KD + (m + 1))
                            pe.sem_inc(W.used, 1)

                for u in range(4):
                    hidden(u % 2, u + 1, u // 2)
                with pe.Fori(1, BLOCKS) as j:
                    for s in range(2):
                        hidden(s, wcount(j, s), j * 6 - 4)
                    output(j, j * 6, j * 6 - 3)
                    for s in range(2):
                        hidden(s, wcount(j, 4 + s), j * 6 + 1)
                output(BLOCKS, wcount(BLOCKS, -1), BLOCKS * 6 - 4)

            @block.scalar
            def _(act):
                def split(b, raw, used=None):
                    act.wait_ge(W.raw_in[b], raw)
                    if used is not None:
                        act.wait_ge(W.used, used)
                    nc.scalar.activation(W.hi[:, b, :], W.raw[:, b, :], ACT.Copy).then_inc(W.hi_ready, 1)

                def silu(w, hid):
                    act.wait_ge(W.used, w)
                    act.wait_ge(b_ready, hid)
                    for ps, out in chunk_views(g.ps[:, 0], gated):
                        last = nc.scalar.activation(out, ps, ACT.Silu)
                    last.then_inc(free[0], 1)

                def upper(t, hid):
                    act.wait_ge(b_ready, hid)
                    nc.scalar.activation(actH[:, t, :], act32[:, t, :], ACT.Copy).then_inc(h_hi, 1)

                split(0, 16)
                split(1, 16)
                for t in range(2):
                    silu(2 * t + 1, t)
                    split(0, 16 * (t + 2), 2 * t + 1)
                    split(1, 16 * (t + 2), 2 * t + 2)
                    upper(t, t + 1)
                with act.Fori(1, BLOCKS) as j:
                    w = j * 6 - 2
                    r = j * 48 - 16
                    silu(w + 1, j * 2)
                    split(0, r + 32, w + 1)
                    split(1, r + 32, w + 2)
                    split(0, r + 48, w + 3)
                    split(1, r + 48, w + 4)
                    act.wait_ge(out_done, j * KD)
                    upper(0, j * 2 + 1)
                    silu(w + 5, j * 2 + 1)
                    split(0, r + 64, w + 5)
                    split(1, r + 64, w + 6)
                    upper(1, j * 2 + 2)

            @block.vector
            def _(dve):
                def product(t, w, uses0, hid):
                    dve.wait_ge(W.used, w)
                    dve.wait_ge(free[0], uses0)
                    dve.wait_ge(h_lo, hid)
                    for (ps, o), (_, x) in zip(chunk_views(g.ps[:, 1], act32[:, t, :]), chunk_views(g.ps[:, 1], gated)):
                        last = nc.vector.tensor_tensor(o, ps, x, ALU.mult)
                    last.then_inc(free[1], 1)
                    dve.wait_ge(free[1], uses0)
                    dve.sem_inc(b_ready, 1)

                def add_output(j):
                    for m in range(KD):
                        dve.wait_ge(out_done, j * KD - KD + (m + 1))
                        residual(g, dve, XT, m, 5, m % 2, free[m % 2])

                for t in range(2):
                    product(t, 2 * t + 2, t + 1, 0)
                with dve.Fori(1, BLOCKS) as j:
                    product(0, j * 6, j * 6 - 3, j * 2 - 1)
                    add_output(j)
                    product(1, j * 6 + 4, j * 6 + 2, j * 2)
                add_output(BLOCKS)

            @block.gpsimd
            def _(pool):
                def lower(b, count):
                    pool.wait_ge(W.hi_ready, count)
                    nc.gpsimd.tensor_tensor(W.lo[:, b, :], W.raw[:, b, :], W.hi[:, b, :].bitcast(F32), ALU.subtract).then_inc(W.lo_ready, 1)

                def rest(t, count):
                    pool.wait_ge(h_hi, count)
                    nc.gpsimd.tensor_tensor(actL[:, t, :], act32[:, t, :], actH[:, t, :].bitcast(F32), ALU.subtract).then_inc(h_lo, 1)

                lower(0, 1)
                lower(1, 2)
                for t in range(2):
                    lower(0, 2 * t + 3)
                    lower(1, 2 * t + 4)
                    rest(t, t + 1)
                with pool.Fori(1, BLOCKS) as j:
                    for n in range(4):
                        lower(n % 2, j * 6 + (n + 1))
                    rest(0, j * 2 + 1)
                    for n in range(2):
                        lower(n % 2, j * 6 + (n + 5))
                    rest(1, j * 2 + 2)


def phase_final(g):
    nc = g.nc
    with ExitStack() as ctx:
        sb = lambda name, shape, dt=F32: ctx.enter_context(nc.sbuf_tensor(name, shape, dt))
        sem = lambda name: ctx.enter_context(nc.semaphore(name))
        XT = g.XT
        square = sb("square2", [P, 2, T])
        sumsq = sb("sumsq2", [P, T])
        rstd = sb("rstd2", [P, T])
        rows = sb("y_rows", [P, 2, D])
        zero, sq_ready, sq_added, stat_done, root_ready = sem("fin_zero"), sem("fin_sq"), sem("fin_sq_added"), sem("fin_stat"), sem("fin_root")
        rstd_ready, y_ready, turned, copied = sem("fin_rstd"), sem("y_ready"), sem("fin_turned"), sem("fin_copied")
        stored = (sem("y_stored0"), sem("y_stored1"))
        with nc.Block() as block:

            @block.sync
            def _(sp):
                for t in range(NT):
                    sp.wait_ge(copied, 2 * t + 2)
                    dst = g.d["y_sample"][t * P:(t + 1) * P, :] if t < LAT // P else g.d["y_prompt"][t * P - LAT:(t + 1) * P - LAT, :]
                    sp.dma_start(dst, rows[:, t % 2, :]).then_inc(stored[t % 2], 16)
                for b in range(2):
                    sp.wait_ge(stored[b], 16 * NT // 2)

            @block.tensor
            def _(pe):
                pe.wait_ge(sq_added, KD)
                for c, (c0, c1) in enumerate(CHUNKS):
                    mm = nc.tensor.matmul(g.ps_all[:, c, 0:c1 - c0], g.ones[:, :], sumsq[:, c0:c1], start=True, stop=True)
                mm.then_inc(stat_done, 1)
                pe.wait_ge(y_ready, KD)
                pe.wait_ge(root_ready, 2)
                for t in range(NT):
                    for h in range(2):
                        n = 2 * t + h
                        if n >= 8:
                            pe.wait_ge(copied, n - 7)
                        for f in range(4):
                            mm = nc.tensor.transpose(g.ps_all[:, n % 8, f * P:(f + 1) * P], XT[:, 4 * h + f, t * P:(t + 1) * P], g.ident[:, :])
                        mm.then_inc(turned, 1)

            @block.scalar
            def _(act):
                for m in range(KD):
                    if m >= 2:
                        act.wait_ge(sq_added, m - 1)
                    nc.scalar.activation(square[:, m % 2, :], XT[:, m, :], ACT.Square).then_inc(sq_ready, 1)
                act.wait_ge(stat_done, 1)
                root(g, act, rstd, root_ready)
                for n in range(2 * NT):
                    t = n // 2
                    act.wait_ge(turned, n + 1)
                    if t >= 2 and n % 2 == 0:
                        act.wait_ge(stored[t % 2], 16 * (t // 2))
                    nc.scalar.activation(rows[:, t % 2, (n % 2) * 512:(n % 2 + 1) * 512], g.ps_all[:, n % 8, :], ACT.Copy).then_inc(copied, 1)

            @block.vector
            def _(dve):
                dve.wait_ge(root_ready, 2)
                nc.vector.reciprocal(rstd[:, :], rstd[:, :]).then_inc(rstd_ready, 1)
                dve.wait_ge(rstd_ready, 1)
                for m in range(KD):
                    c = OFF["final_g"] + m
                    nc.vector.scalar_tensor_tensor(XT[:, m, :], XT[:, m, :], g.cols[:, c:c + 1], rstd[:, :], ALU.mult, ALU.mult).then_inc(y_ready, 1)

            @block.gpsimd
            def _(pool):
                nc.gpsimd.memset(sumsq[:, :], 0.0).then_inc(zero, 1)
                pool.wait_ge(zero, 1)
                for m in range(KD):
                    pool.wait_ge(sq_ready, m + 1)
                    if m:
                        pool.wait_ge(sq_added, m)
                    nc.gpsimd.tensor_tensor(sumsq[:, :], sumsq[:, :], square[:, m % 2, :], ALU.add).then_inc(sq_added, 1)


PHASES = (phase_input, phase_mixers, phase_attention, phase_merge, phase_output, phase_ffn, phase_final)


_OUTS = (("y_prompt", (CTX, D)), ("y_sample", (LAT, D)), ("new_k", (CTX, NAW)), ("new_v", (CTX, NAW)))
_SCRATCH = (("xT", (KD, P, T)), ("qT", (4, P, T)), ("kT", (4, P, T + PAST)), ("v", (T, NAW)),
            ("branch", (KD, P, T)), ("merged", (KD, P, T)))


def build(nc, arrays, phases=9, scratch_kind="Internal"):
    g = Ctx()
    g.nc = nc
    g.d = {n: nc.dram_tensor(n + "_dram", a.shape, F32, kind="ExternalInput").ap() for n, a in arrays.items()}
    for n, shape in _OUTS:
        g.d[n] = nc.dram_tensor(n + "_dram", shape, F32, kind="ExternalOutput").ap()
    for n, shape in _SCRATCH:
        g.d[n] = nc.dram_tensor(n + "_dram", shape, F32, kind=scratch_kind).ap()
    with ExitStack() as ctx:
        sb = lambda name, shape, dt=F32: ctx.enter_context(nc.sbuf_tensor(name, shape, dt))
        g.cols = sb("cols", [P, NCOLS])
        g.mod = sb("mod", [P, 6 * KD, 2])
        g.gain = sb("gain", [P, 2, KD, 2])
        g.ident = sb("ident", [P, P])
        g.ones = sb("ones", [P, P])
        g.eps = sb("eps", [P, 1])
        g.AH = sb("AH", [P, KD, T], FR)
        g.AL = sb("AL", [P, KD, T], FR)
        g.ps_all = ctx.enter_context(nc.psum_tensor("ps_all", [P, 8, 512], F32))
        g.ps = g.ps_all[:, 0:6, :].rearrange("p (s c) n -> p s c n", s=2)
        g.aux = g.ps_all[:, 6:8, :]
        for n, phase in enumerate(PHASES):
            if n < phases:
                if phase is phase_output:
                    g.XT = sb("XT", [P, KD, T])
                phase(g)


def columns(v):
    return np.asarray(v).reshape(-1, P).T


def lay_out(i):
    both = np.stack([columns(i["c"][0]), columns(i["c_ctx"])], axis=2).reshape(P, 2 * KD)
    w_dw = np.asarray(i["w_dw"][0]).T.reshape(2, P, CONV_K).transpose(1, 0, 2).reshape(P, 2 * CONV_K)
    packed = [both] + [columns(v) for v in (i["b_mod"][0], i["norm1_g"][0], i["norm2_g"][0], i["final_g"], i["b_gate"][0],
                                            i["pool_scale"][0], i["b_dw"][0], i["conv_norm_g"][0], i["conv_norm_b"][0])] + [w_dw]
    rpb = np.zeros((HEADS, 2 * KH - 1, 2 * GW - 1), np.float32)
    side = GW - KW
    rpb[:, :, side:side + 2 * KW - 1] = np.asarray(i["rpb"][0])[:, :, ::-1]
    start = np.clip(np.arange(GW) - KW // 2, 0, GW - KW)
    inside = (np.arange(GW)[None] >= start[:, None]) & (np.arange(GW)[None] < start[:, None] + KW)
    inv = []
    for w in (2, 4, 8, 16):
        row = []
        for n in (LAT, CTX):
            t = np.arange(n)
            row.append(1.0 / (np.clip(t - w // 2 + w, 0, n) - np.clip(t - w // 2, 0, n)))
        inv.append(np.concatenate(row))
    a = {
        "cols": np.ascontiguousarray(np.concatenate(packed, axis=1)),
        "ident": np.eye(P, dtype=np.float32),
        "col_mask": np.tile(np.where(inside, 0.0, NEG), (2, 1)).astype(np.float32),
        "inv_count": np.stack(inv).astype(np.float32),
        "rpb": rpb,
        "x_prompt": np.asarray(i["x_prompt"][0]), "x_sample": np.asarray(i["x_sample"][0]),
        "cache_k": np.asarray(i["cache_k"][0, 0]).reshape(PAST, NAW), "cache_v": np.asarray(i["cache_v"][0, 0]).reshape(PAST, NAW),
    }
    for n in ("w_mod", "w_in", "w_oa", "w_pool", "w_ob", "w_oc", "w_out", "w_gu", "w_down"):
        a[n] = np.asarray(i[n][0])
    return a


def kernel(**inputs):
    import concourse.bacc as bacc
    from concourse.bass_utils import run_bass_kernel_spmd

    arrays = lay_out(inputs)
    nc = bacc.Bacc("TRN2", target_bir_lowering=False, num_devices=1)
    build(nc, arrays)
    r = run_bass_kernel_spmd(nc, [{n + "_dram": a for n, a in arrays.items()}], core_ids=[0]).results[0]
    shape = (1, 1, CTX, HEADS, DH)
    return (r["y_prompt_dram"].reshape(1, CTX, D), r["y_sample_dram"].reshape(1, LAT, D),
            r["new_k_dram"].reshape(shape), r["new_v_dram"].reshape(shape))
```

```python
from contextlib import ExitStack

import numpy as np
import concourse.bass as bass
from concourse import mybir

F32 = mybir.dt.float32
FR = mybir.dt.float32r
ACT = mybir.ActivationFunctionType
ALU = mybir.AluOpType
AX = mybir.AxisListType.X

P = 128
D = 1024
KD = D // P
LAT, CTX, PAST = 1024, 256, 256
T = LAT + CTX
NT = T // P
CHUNKS = ((0, 448), (448, 896), (896, 1280))
C2 = LAT - CHUNKS[2][0]
HEADS, DH = 8, 64
NAW = HEADS * DH
KH, KW, GW = 8, 16, 64
ROWS = LAT // GW
PW = CW = D // 4
CONV_K = 31
HALF = CONV_K // 2
HID = 2816
BLOCKS = HID // (2 * P)
EPS = 1e-6
NEG = -1e30
N_IN = 3 * NAW + PW + 2 * CW + 3 * D
P_COL, A_COL, G_COL, GATE_COL = 3 * NAW, 3 * NAW + PW, 3 * NAW + PW + CW, 3 * NAW + PW + 2 * CW
OFF = {}
_at = 0
for _name, _n in (("c", 2 * KD), ("b_mod", 6 * KD), ("norm1_g", KD), ("norm2_g", KD), ("final_g", KD),
                  ("b_gate", 3 * KD), ("pool_scale", 2), ("b_dw", 2), ("cn_g", 2), ("cn_b", 2),
                  ("w_dw", 2 * CONV_K)):
    OFF[_name] = _at
    _at += _n
NCOLS = _at
CB = HALF + LAT + HALF + CTX + HALF
CV = LAT + HALF + CTX
CCTX = LAT + HALF
PB = 8 + LAT + 16 + CTX + 8
PCTX = 8 + LAT + 16
SLOTS = 14
WIN = 10


class Ctx:
    pass


def chunk_views(ps, sbuf_row):
    n = CHUNKS[0][1]
    return ((ps[:, 0:2, 0:n], sbuf_row[:, 0:2 * n].rearrange("p (c n) -> p c n", c=2)),
            (ps[:, 2, 0:T - 2 * n], sbuf_row[:, 2 * n:T]))


def gemm(nc, ps, wh, wl, ah, al, ktiles, first=True, last=True):
    for n, (w0, k) in enumerate(ktiles):
        for part, (w, a) in enumerate(((wh, ah), (wh, al), (wl, ah))):
            for c, (c0, c1) in enumerate(CHUNKS):
                mm = nc.tensor.matmul(ps[:, c, 0:c1 - c0], w[:, w0:w0 + P], a[:, k, c0:c1],
                                      start=(first and n == 0 and part == 0),
                                      stop=(last and n == len(ktiles) - 1 and part == 2))
    return mm


def phase_input(g):
    nc = g.nc
    with ExitStack() as ctx:
        sb = lambda name, shape, dt=F32: ctx.enter_context(nc.sbuf_tensor(name, shape, dt))
        sem = lambda name: ctx.enter_context(nc.semaphore(name))
        XT = sb("XT0", [P, KD, T])
        x_rows = sb("x_rows", [P, NT, D])
        w_mod_sb = sb("w_mod_sb", [P, 4, KD * P])
        square = sb("square0", [P, 2, 512])
        sumsq = sb("sumsq0", [P, T])
        rstd = sb("rstd0", [P, T])
        normed = sb("normed0", [P, 2, T])
        const_in, x_in0, x_in1, x_in2 = sem("const_in"), sem("x_in0"), sem("x_in1"), sem("x_in2")
        x_in = (x_in0, x_in1, x_in2)
        w_in = [sem(f"wmod_in{b}") for b in range(4)]
        w_used, mod_done, mod_ready = sem("wmod_used"), sem("mod_done"), sem("mod_ready")
        ones_ready, silu_ready, turned, xt_ready = sem("ones_ready"), sem("silu_ready"), sem("turned"), sem("xt_ready")
        sq_ready, sq_added, stat_done, root_ready = sem("sq_ready"), sem("sq_added"), sem("stat_done"), sem("root_ready")
        rstd_ready, scaled, t_ready, ah_ready, al_ready = (sem("rstd_ready"), sem("scaled"), sem("t_ready"),
                                                           sem("ah_ready"), sem("al_ready"))
        acc_zero, mod_step, spilled = sem("acc_zero"), sem("mod_step"), sem("spilled")
        groups = [(0, 4), (4, 8), (8, 10)]
        banks = [g.ps[:, n // 3, n % 3, :] for n in range(6)]
        EARLY = 2 * KD
        with nc.Block() as block:

            @block.sync
            def _(sp):
                sp.dma_start(g.cols[:, :], g.d["cols"]).then_inc(const_in, 16)
                sp.dma_start(g.ident[:, :], g.d["ident"]).then_inc(const_in, 16)
                for n, (a, b) in enumerate(groups[:2]):
                    sp.dma_start(x_rows[:, a:b, :], g.d["x_sample"][a * P:b * P, :].rearrange("(t p) n -> p t n", p=P)).then_inc(x_in[n], 16)
                sp.dma_start(x_rows[:, 8:10, :], g.d["x_prompt"].rearrange("(t p) n -> p t n", p=P)).then_inc(x_in[2], 16)
                wv = g.d["w_mod"].rearrange("(k p) n -> p k n", p=P)

                def load(b, col):
                    sp.dma_start(w_mod_sb[:, b, :].rearrange("p (k n) -> p k n", k=KD), wv[:, :, bass.ds(col, P)]).then_inc(w_in[b], 16)

                for b in range(4):
                    load(b, b * P)
                with sp.Fori(1, (EARLY + KD) // 4) as i:
                    for b in range(4):
                        sp.wait_ge(w_used, i * 4 + (b - 3))
                        load(b, i * (4 * P) + b * P)
                sp.wait_ge(spilled, 16)

            @block.tensor
            def _(pe):
                pe.wait_ge(const_in, 32)
                for n in range(24):
                    gi, f = n // KD, n % KD
                    a, b = groups[gi]
                    if f == 0:
                        pe.wait_ge(x_in[gi], 16)
                    if n >= 6:
                        pe.wait_ge(xt_ready, n - 5)
                    for t in range(a, b):
                        mm = nc.tensor.transpose(banks[n % 6][:, (t - a) * P:(t - a + 1) * P],
                                                 x_rows[:, t, f * P:(f + 1) * P], g.ident[:, :])
                    mm.then_inc(turned, 1)
                pe.wait_ge(silu_ready, 1)

                def modulation(bank, tiles):
                    with pe.Fori(0, tiles // 4) as i:
                        for b in range(4):
                            pe.wait_ge(w_in[b], i * 16 + (16 + bank * 4 * EARLY))
                            for k in range(KD):
                                mm = nc.tensor.matmul(g.aux[:, bank, bass.ds(i * 8 + b * 2, 2)], w_mod_sb[:, b, k * P:(k + 1) * P],
                                                      g.cs[:, 2 * k:2 * k + 2], start=(k == 0), stop=(k == KD - 1))
                            mm.then_inc(w_used, 1)

                modulation(0, EARLY)
                pe.wait_ge(xt_ready, 24)
                pe.wait_ge(sq_added, 24)
                pe.wait_ge(ones_ready, 1)
                for c, (c0, c1) in enumerate(CHUNKS):
                    mm = nc.tensor.matmul(g.ps[:, 0, c, 0:c1 - c0], g.ones[:, :], sumsq[:, c0:c1], start=True, stop=True)
                mm.then_inc(stat_done, 1)
                modulation(1, KD)

            @block.scalar
            def _(act):
                act.wait_ge(const_in, 32)
                nc.scalar.activation(g.cs[:, :], g.cols[:, 0:2 * KD], ACT.Silu).then_inc(silu_ready, 1)
                for n in range(24):
                    gi, f = n // KD, n % KD
                    t0, t1 = groups[gi][0] * P, groups[gi][1] * P
                    act.wait_ge(xt_ready, n + 1)
                    if n >= 2:
                        act.wait_ge(sq_added, n - 1)
                    nc.scalar.activation(square[:, n % 2, 0:t1 - t0], XT[:, f, t0:t1], ACT.Square).then_inc(sq_ready, 1)
                act.wait_ge(xt_ready, 24)
                act.dma_start(g.d["xT"].rearrange("k p t -> p k t"), XT[:, :, :]).then_inc(spilled, 16)
                act.wait_ge(stat_done, 1)
                root(g, act, rstd, root_ready)
                copies(g, act, normed, t_ready, ah_ready)

            @block.vector
            def _(dve):
                nc.vector.memset(g.ones[:, :], 1.0)
                nc.vector.memset(g.eps[:, :], EPS).then_inc(ones_ready, 1)
                for n in range(24):
                    gi, f = n // KD, n % KD
                    t0, t1 = groups[gi][0] * P, groups[gi][1] * P
                    dve.wait_ge(turned, n + 1)
                    nc.vector.tensor_copy(XT[:, f, t0:t1], banks[n % 6][:, 0:t1 - t0]).then_inc(xt_ready, 1)
                dve.wait_ge(w_used, EARLY)
                mod_bias(g, 0, 2, g.aux[:, 0, 0:2 * EARLY], mod_step)
                dve.wait_ge(mod_step, 1)
                mod_gain(g, 0, "norm1_g", 1, mod_step)
                dve.wait_ge(mod_step, 2)
                dve.wait_ge(root_ready, 2)
                nc.vector.reciprocal(rstd[:, :], rstd[:, :]).then_inc(rstd_ready, 1)
                dve.wait_ge(rstd_ready, 1)
                scale_shift(g, dve, XT, rstd, normed, 0, 0, scaled, t_ready, al_ready)
                dve.wait_ge(w_used, EARLY + KD)
                mod_bias(g, 2, 3, g.aux[:, 1, 0:2 * KD], mod_step)

            @block.gpsimd
            def _(pool):
                nc.gpsimd.memset(sumsq[:, :], 0.0).then_inc(acc_zero, 1)
                pool.wait_ge(acc_zero, 1)
                for n in range(24):
                    t0, t1 = groups[n // KD][0] * P, groups[n // KD][1] * P
                    pool.wait_ge(sq_ready, n + 1)
                    if n:
                        pool.wait_ge(sq_added, n)
                    nc.gpsimd.tensor_tensor(sumsq[:, t0:t1], sumsq[:, t0:t1], square[:, n % 2, 0:t1 - t0], ALU.add).then_inc(sq_added, 1)
                rests(g, pool, normed, ah_ready, al_ready)


def mod_bias(g, a, b, source, done):
    bm = g.cols[:, OFF["b_mod"] + a * KD:OFF["b_mod"] + b * KD]
    g.nc.vector.tensor_tensor(g.mod[:, a * KD:b * KD, :], source.rearrange("p (m j) -> p m j", j=2),
                              bm.rearrange("p (m j) -> p m j", j=1).broadcast_to([P, (b - a) * KD, 2]), ALU.add).then_inc(done, 1)


def mod_gain(g, n, gain, part, done):
    gv = g.cols[:, OFF[gain]:OFF[gain] + KD].rearrange("p (m j) -> p m j", j=1).broadcast_to([P, KD, 2])
    g.nc.vector.scalar_tensor_tensor(g.gain[:, n, :, :], g.mod[:, part * KD:(part + 1) * KD, :], 1.0, gv,
                                     ALU.add, ALU.mult).then_inc(done, 1)


def root(g, act, rstd, root_ready):
    for ps, sb in chunk_views(g.ps[:, 0], rstd):
        g.nc.scalar.activation(sb, ps, ACT.Sqrt, bias=g.eps[:, 0:1], scale=1.0 / D).then_inc(root_ready, 1)


def scale_shift(g, dve, XT, rstd, normed, gain, shift_part, scaled, t_ready, al_ready):
    for f in range(KD):
        if f >= 2:
            dve.wait_ge(al_ready, f - 1)
        nc = g.nc
        nc.vector.tensor_tensor(normed[:, f % 2, :], XT[:, f, :], rstd[:, :], ALU.mult).then_inc(scaled, 1)
        dve.wait_ge(scaled, f + 1)
        for j, (a, b) in enumerate(((0, LAT), (LAT, T))):
            nc.vector.tensor_scalar(normed[:, f % 2, a:b], normed[:, f % 2, a:b], g.gain[:, gain, f, j:j + 1],
                                    g.mod[:, shift_part * KD + f, j:j + 1], ALU.mult, ALU.add).then_inc(t_ready, 1)


def copies(g, act, normed, t_ready, ah_ready):
    for f in range(KD):
        act.wait_ge(t_ready, 2 * (f + 1))
        g.nc.scalar.activation(g.AH[:, f, :], normed[:, f % 2, :], ACT.Copy).then_inc(ah_ready, 1)


def rests(g, pool, normed, ah_ready, al_ready):
    for f in range(KD):
        pool.wait_ge(ah_ready, f + 1)
        g.nc.gpsimd.tensor_tensor(g.AL[:, f, :], normed[:, f % 2, :], g.AH[:, f, :].bitcast(F32), ALU.subtract).then_inc(al_ready, 1)


class Weights:

    def __init__(self, g, ctx, tag):
        nc = g.nc
        self.g = g
        self.raw = ctx.enter_context(nc.sbuf_tensor(f"w_raw{tag}", [P, 2, KD * P], F32))
        self.hi = ctx.enter_context(nc.sbuf_tensor(f"w_hi{tag}", [P, 2, KD * P], FR))
        self.lo = ctx.enter_context(nc.sbuf_tensor(f"w_lo{tag}", [P, 2, KD * P], FR))
        self.raw_in = [ctx.enter_context(nc.semaphore(f"w_raw_in{b}{tag}")) for b in range(2)]
        self.hi_ready = ctx.enter_context(nc.semaphore(f"w_hi_ready{tag}"))
        self.lo_ready = ctx.enter_context(nc.semaphore(f"w_lo_ready{tag}"))
        self.used = ctx.enter_context(nc.semaphore(f"w_used{tag}"))

    def columns(self, slot, width):
        return self.raw[:, slot, :].rearrange("p (k n) -> p k n", n=width)


PIECES = ((0, 0, 448, 0), (1, 0, 448, 448), (2, 0, C2, 896), (2, C2, CTX, LAT))


def padded(tok, lead, ctx_at):
    return lead + tok if tok < LAT else ctx_at


def phase_mixers(g):
    nc = g.nc
    with ExitStack() as ctx:
        sb = lambda name, shape, dt=F32: ctx.enter_context(nc.sbuf_tensor(name, shape, dt))
        sem = lambda name: ctx.enter_context(nc.semaphore(name))
        W = Weights(g, ctx, "m")
        glu = sb("glu", [P, 2, CB])
        ppad = sb("pool_in", [P, 2, PB])
        summed = sb("summed", [P, 2, PB])
        conv = sb("conv", [P, 2, CV])
        sig = sb("sig", [P, T])
        square = sb("ln_square", [P, T])
        evac = sb("evac", [P, 2, T])
        vt = sb("vt", [P, NT, P])
        kt_ctx = sb("kt_ctx", [P, 2, P])
        cached_k = vt[:, 0:8, :].rearrange("p (t a) n -> p t (a n)", t=2)
        cached_kT = sb("cached_kT", [P, 4, PAST])
        wp = sb("wp", [P, 2, P])
        inv = sb("inv", [P, T])
        w_mod_sb = sb("w_mod_late", [P, 2, KD * 2 * P])
        free = (sem("set_free0"), sem("set_free1"))
        done = sem("small_products_done")
        ck_in, inv_in, inv_used, zeroed, wp_in = sem("ck_in"), sem("inv_in"), sem("inv_used"), sem("zeroed"), sem("wp_in")
        ck_turned, ck_out = sem("ck_turned"), sem("ck_out")
        pool_step, pooled, branch_ready = sem("pool_step"), sem("pooled"), sem("pool_branch_ready")
        glu_ready, conv_step = sem("glu_ready"), sem("conv_step")
        centred, sq_ready, root_ready, ln_step, silu_ready = sem("centred"), sem("ln_sq"), sem("ln_root"), sem("ln_step"), sem("ln_silu")
        turned, tok_ready = sem("kv_turned"), sem("kv_token_major")
        stored = (sem("evac_stored0"), sem("evac_stored1"))
        tok_stored, ck_stored, branch_stored = sem("tok_stored"), sem("ck_stored"), sem("mixer_branches_stored")
        mod_in = (sem("late_wmod_in0"), sem("late_wmod_in1"))
        mod_used, mod_out, mod_step = sem("late_wmod_used"), sem("late_mod_out"), sem("late_mod_step")
        wv = g.d["w_in"].rearrange("(k p) n -> p k n", p=P)
        wmv = g.d["w_mod"].rearrange("(k p) n -> p k n", p=P)
        FIRST = [G_COL, A_COL, G_COL + P, A_COL + P, P_COL, P_COL + P]
        U_Q, U_K, U_V, UNITS = 6, 10, 14, 18
        PLAN = (2, 1, 1, 2, 1, 1)
        NG = 3 * D // (2 * P)
        modp = g.aux[:, 1, 0:2 * 3 * KD]
        USE_Q, USE_K, USE_V, USE_POOL = 3, (6, 5), 8, 10

        with nc.Block() as block:

            @block.sync
            def _(sp):
                def load(b, col):
                    sp.dma_start(W.columns(b, P), wv[:, :, bass.ds(col, P)]).then_inc(W.raw_in[b], 16)

                def load_mod(n):
                    if n >= 2:
                        sp.wait_ge(mod_used, n - 1)
                    sp.dma_start(w_mod_sb[:, n % 2, :].rearrange("p (k n) -> p k n", k=KD),
                                 wmv[:, :, 3 * D + n * 2 * P:3 * D + (n + 1) * 2 * P]).then_inc(mod_in[n % 2], 16)

                def store(b, dst, use):
                    sp.wait_ge(free[b], use)
                    sp.dma_start(dst.rearrange("a p t -> p (a t)"), evac[:, b, :]).then_inc(stored[b], 16)

                def load_inv(t):
                    for half in range(2):
                        sp.dma_start(inv[half * 64:(half + 1) * 64, :],
                                     g.d["inv_count"][2 * t + half:2 * t + half + 1, :].broadcast_to([64, T])).then_inc(inv_in, 16)

                load(0, FIRST[0])
                load(1, FIRST[1])
                sp.dma_start(cached_k, g.d["cache_k"].rearrange("(t p) n -> p t n", p=P)).then_inc(ck_in, 16)
                load_mod(0)
                load_mod(1)
                load_inv(0)
                sp.wait_ge(zeroed, 2)
                for q in range(4):
                    r = 64 * (q % 2)
                    sp.dma_start(wp[r:r + 64, q // 2, r:r + 64], g.d["w_pool"][q, :, :]).then_inc(wp_in, 16)
                n = 2
                for u in range(2, U_Q + 2):
                    sp.wait_ge(W.lo_ready, u - 1)
                    load(u % 2, FIRST[u] if u < U_Q else (u - U_Q) * P)
                    for _ in range(PLAN[u - 2]):
                        load_mod(n)
                        n += 1
                    if u == 3:
                        sp.wait_ge(ck_out, 2)
                        sp.dma_start(g.d["kT"][:, :, T:T + PAST].rearrange("a p t -> p a t"), cached_kT[:, :, :]).then_inc(ck_stored, 16)
                for i in range(2):
                    for b in range(2):
                        sp.wait_ge(W.lo_ready, U_Q + 2 * i + b + 1)
                        load(b, (2 * i + 2 + b) * P)
                        if i == 0:
                            load_mod(n)
                            n += 1
                    for b in range(2):
                        store(b, g.d["qT"][2 * i + b:2 * i + b + 1, :, :], USE_Q + i + 1)
                for i in range(2):
                    for b in range(2):
                        sp.wait_ge(W.lo_ready, U_K + 2 * i + b + 1)
                        load(b, (6 + 2 * i + b) * P)
                    for b in range(2):
                        store(b, g.d["kT"][2 * i + b:2 * i + b + 1, :, 0:T], USE_K[b] + i + 1)
                    for b in range(2):
                        col = (2 * i + b) * P
                        sp.wait_ge(tok_ready, 2 * i + b + 2)
                        sp.dma_start(g.d["new_k"][:, col:col + P].rearrange("(t p) n -> p t n", p=P),
                                     kt_ctx[:, :, :]).then_inc(tok_stored, 16)
                    if i == 0:
                        sp.wait_ge(inv_used, 2)
                        load_inv(1)
                for b in range(2):
                    sp.wait_ge(W.lo_ready, UNITS - 2 + b - 1)
                    load(b, (10 + b) * P)
                for i in range(2):
                    for b in range(2):
                        col = (2 * i + b) * P
                        sp.wait_ge(tok_ready, 6 * i + 5 + 3 * b + 3)
                        sp.dma_start(g.d["v"][:, col:col + P].rearrange("(t p) n -> p t n", p=P), vt[:, :, :]).then_inc(tok_stored, 16)
                        sp.dma_start(g.d["new_v"][:, col:col + P].rearrange("(t p) n -> p t n", p=P), vt[:, 8:10, :]).then_inc(tok_stored, 16)
                    if i == 0:
                        for t in range(2):
                            for part, (a, b, at) in enumerate(((0, LAT, 0), (LAT, T, CCTX))):
                                sp.wait_ge(silu_ready, 2 * t + part + 1)
                                sp.dma_start(g.d["branch"][6 + t, :, a:b], conv[:, t, at:at + b - a]).then_inc(branch_stored, 16)
                for t in range(2):
                    sp.wait_ge(branch_ready, t + 1)
                    sp.dma_start(g.d["branch"][4 + t, :, :], ppad[:, t, 0:T]).then_inc(branch_stored, 16)
                sp.wait_ge(ck_stored, 16)
                sp.wait_ge(tok_stored, 16 * 12)
                sp.wait_ge(branch_stored, 16 * 6)
                for b in range(2):
                    sp.wait_ge(stored[b], 16 * 4)

            @block.tensor
            def _(pe):
                pe.wait_ge(ck_in, 16)
                for hp in range(4):
                    for t in range(2):
                        mm = nc.tensor.transpose(g.aux[:, hp // 2, (hp % 2) * 256 + t * P:(hp % 2) * 256 + (t + 1) * P],
                                                 cached_k[:, t, hp * P:(hp + 1) * P], g.ident[:, :])
                mm.then_inc(ck_turned, 1)

                def unit(s, w_count, uses):
                    pe.wait_ge(W.lo_ready, w_count)
                    pe.wait_ge(free[s], uses)
                    gemm(nc, g.ps[:, s], W.hi[:, s, :], W.lo[:, s, :], g.AH, g.AL,
                         [(k * P, k) for k in range(KD)]).then_inc(W.used, 1)

                def modulation(b, raw, column):
                    pe.wait_ge(mod_in[b], raw)
                    for m in range(2):
                        for k in range(KD):
                            mm = nc.tensor.matmul(modp[:, bass.ds(column + 2 * m, 2)], w_mod_sb[:, b, (2 * k + m) * P:(2 * k + m + 1) * P],
                                                  g.cs[:, 2 * k:2 * k + 2], start=(k == 0), stop=(k == KD - 1))
                    mm.then_inc(mod_used, 1)

                def channel_sums(s, tiles):
                    for bank, c0, n, tok in PIECES:
                        for t, (x, ctx_at) in enumerate(tiles):
                            at = padded(tok, 0, ctx_at)
                            mm = nc.tensor.matmul(g.ps[:, s, bank, c0:c0 + n], g.ones[:, :], x[:, at:at + n], start=(t == 0), stop=(t == 1))
                    mm.then_inc(done, 1)

                n = 0
                for u in range(U_Q):
                    unit(u % 2, u + 1, u // 2)
                    for _ in range(PLAN[u]):
                        if n == 0:
                            pe.wait_ge(ck_out, 2)
                        modulation(n % 2, 16 * (n // 2 + 1), n * 4)
                        n += 1
                with pe.Fori(0, 2) as i:
                    for s in range(2):
                        unit(s, i * 2 + (U_Q + s + 1), i + USE_Q)
                        modulation(s, i * 16 + 16 * (n // 2 + 1), i * 8 + (n + s) * 4)
                pe.wait_ge(conv_step, 2 * CONV_K)
                pe.wait_ge(free[0], USE_Q + 2)
                channel_sums(0, [(conv[:, t, :], CCTX) for t in range(2)])
                with pe.Fori(0, 2) as i:
                    for s in range(2):
                        unit(s, i * 2 + (U_K + s + 1), i + USE_K[s])
                    for s in range(2):
                        pe.wait_ge(free[s], i + (USE_K[s] + 1))
                        pe.wait_ge(tok_ready, i * 2 + (s + 1))
                        for t in range(2):
                            mm = nc.tensor.transpose(g.aux[:, 0, t * P:(t + 1) * P], evac[:, s, LAT + t * P:LAT + (t + 1) * P], g.ident[:, :])
                        mm.then_inc(turned, 1)
                pe.wait_ge(sq_ready, 2)
                channel_sums(1, [(sig, LAT), (square, LAT)])
                pe.wait_ge(mod_out, 1)
                with pe.Fori(0, 2) as i:
                    for s in range(2):
                        unit(s, i * 2 + (U_V + s + 1), i + USE_V)
                    for s in range(2):
                        pe.wait_ge(free[s], i + (USE_V + 1))
                        for part, (a, b) in enumerate(V_PARTS):
                            pe.wait_ge(tok_ready, i * 6 + (5 + 3 * s + (1 if part == 2 else 0)))
                            for t in range(a, b):
                                mm = nc.tensor.transpose(g.aux[:, part % 2, (t - a) * P:(t - a + 1) * P], evac[:, s, t * P:(t + 1) * P], g.ident[:, :])
                            mm.then_inc(turned, 1)
                pe.wait_ge(wp_in, 64)
                pe.wait_ge(pooled, 2)
                for t in range(2):
                    pe.wait_ge(free[t], USE_POOL)
                    for bank, c0, n, tok in PIECES:
                        at = padded(tok, 8, PCTX)
                        mm = nc.tensor.matmul(g.ps[:, t, bank, c0:c0 + n], wp[:, t, :], summed[:, t, at:at + n], start=True, stop=True)
                    mm.then_inc(done, 1)

            @block.scalar
            def _(act):
                def split(slot, raw_count, used=None):
                    act.wait_ge(W.raw_in[slot], raw_count)
                    if used is not None:
                        act.wait_ge(W.used, used)
                    nc.scalar.activation(W.hi[:, slot, :], W.raw[:, slot, :], ACT.Copy).then_inc(W.hi_ready, 1)

                def copy_out(s):
                    for ps, out in chunk_views(g.ps[:, s], evac[:, s, :]):
                        last = nc.scalar.activation(out, ps, ACT.Copy)
                    last.then_inc(free[s], 1)

                act.sem_inc(tok_ready, 1)
                split(0, 16)
                split(1, 16)
                act.wait_ge(ck_turned, 1)
                for h in range(2):
                    nc.scalar.activation(cached_kT[:, 2 * h:2 * h + 2, :], g.aux[:, h, :].rearrange("p (a t) -> p a t", a=2), ACT.Copy).then_inc(ck_out, 1)
                act.wait_ge(zeroed, 1)
                for u in range(U_Q):
                    if u in (0, 2):
                        act.wait_ge(W.used, u + 1)
                        if u == 2:
                            act.wait_ge(glu_ready, 1)
                        for ps, out in chunk_views(g.ps[:, 0], sig):
                            last = nc.scalar.activation(out, ps, ACT.Sigmoid)
                        last.then_inc(free[0], 1)
                    elif u in (4, 5):
                        act.wait_ge(W.used, u + 1)
                        for bank, c0, n, tok in PIECES:
                            at = padded(tok, 8, PCTX)
                            last = nc.scalar.activation(ppad[:, u - 4, at:at + n], g.ps[:, u % 2, bank, c0:c0 + n], ACT.Copy)
                        last.then_inc(free[u % 2], 1)
                    split(u % 2, 16 * (u // 2 + 2), u + 1)
                for i in range(2):
                    for s in range(2):
                        act.wait_ge(W.used, 2 * i + U_Q + s + 1)
                        if i:
                            act.wait_ge(stored[s], 16 * i)
                        copy_out(s)
                        split(s, 16 * (i + U_Q // 2 + 2), 2 * i + U_Q + s + 1)
                act.wait_ge(mod_used, NG)
                nc.scalar.activation(g.mod[:, 3 * KD:6 * KD, :], modp.rearrange("p (m j) -> p m j", j=2), ACT.Copy).then_inc(mod_out, 1)
                for i in range(2):
                    for s in range(2):
                        act.wait_ge(W.used, 2 * i + U_K + s + 1)
                        act.wait_ge(stored[s], 16 * i + 32)
                        if i:
                            act.wait_ge(turned, 2 * i)
                        copy_out(s)
                        split(s, 16 * (i + U_K // 2 + 2), 2 * i + U_K + s + 1)
                    for s in range(2):
                        act.wait_ge(turned, 2 * i + s + 1)
                        if i or s:
                            act.wait_ge(tok_stored, 32 * i + 16 * s)
                        nc.scalar.activation(kt_ctx[:, :, :], g.aux[:, 0, 0:256].rearrange("p (t n) -> p t n", t=2), ACT.Copy).then_inc(tok_ready, 1)
                    if i == 0:
                        act.wait_ge(centred, 6)
                        for t, x in enumerate((sig, square)):
                            for a, b, at in ((0, LAT, 0), (LAT, T, CCTX)):
                                last = nc.scalar.activation(x[:, a:b], conv[:, t, at:at + b - a], ACT.Square)
                            last.then_inc(sq_ready, 1)
                act.wait_ge(done, 2)
                for ps, out in chunk_views(g.ps[:, 1], sig):
                    last = nc.scalar.activation(out, ps, ACT.Sqrt, bias=g.eps[:, 0:1], scale=1.0 / CW)
                last.then_inc(free[1], 1)
                for i in range(2):
                    for s in range(2):
                        act.wait_ge(W.used, 2 * i + U_V + s + 1)
                        act.wait_ge(stored[s], 16 * 4)
                        act.wait_ge(turned, 4 + 6 * i)
                        copy_out(s)
                        if i == 0:
                            split(s, 16 * (U_V // 2 + 2), U_V + s + 1)
                    for s in range(2):
                        for part, (a, b) in enumerate(V_PARTS):
                            act.wait_ge(turned, 4 + 6 * i + 3 * s + part + 1)
                            if part == 0:
                                act.wait_ge(tok_stored, 64 + 64 * i + 32 * s)
                            nc.scalar.activation(vt[:, a:b, :], g.aux[:, part % 2, 0:(b - a) * P].rearrange("p (t n) -> p t n", n=P), ACT.Copy).then_inc(tok_ready, 1)
                    if i == 0:
                        for t in range(2):
                            act.wait_ge(ln_step, 1 + 2 * (t + 1))
                            for n, at in ((LAT, 0), (CTX, CCTX)):
                                x = conv[:, t, at:at + n]
                                nc.scalar.activation(x, x, ACT.Silu, bias=g.cols[:, OFF["cn_b"] + t:OFF["cn_b"] + t + 1],
                                                     scale=g.cols[:, OFF["cn_g"] + t:OFF["cn_g"] + t + 1]).then_inc(silu_ready, 1)
                for t in range(2):
                    act.wait_ge(done, t + 3)
                    for ps, out in chunk_views(g.ps[:, t], ppad[:, t, 0:T]):
                        last = nc.scalar.activation(out, ps, ACT.Copy, scale=g.cols[:, OFF["pool_scale"] + t:OFF["pool_scale"] + t + 1])
                    last.then_inc(branch_ready, 1)

            @block.gpsimd
            def _(pool):
                with pool.Fori(0, UNITS // 2) as i:
                    for b in range(2):
                        pool.wait_ge(W.hi_ready, i * 2 + (b + 1))
                        nc.gpsimd.tensor_tensor(W.lo[:, b, :], W.raw[:, b, :], W.hi[:, b, :].bitcast(F32), ALU.subtract).then_inc(W.lo_ready, 1)

            @block.vector
            def _(dve):
                nc.vector.memset(ppad[:, :, :], 0.0).then_inc(zeroed, 1)
                nc.vector.memset(wp[:, :, :], 0.0).then_inc(zeroed, 1)
                for a in (0, HALF + LAT, CB - HALF):
                    nc.vector.memset(glu[:, :, a:a + HALF], 0.0)
                for t in range(2):
                    dve.wait_ge(W.used, 2 + 2 * t)
                    dve.wait_ge(free[0], t + 1)
                    for bank, c0, n, tok in PIECES:
                        at = padded(tok, HALF, HALF + LAT + HALF)
                        last = nc.vector.tensor_tensor(glu[:, t, at:at + n], g.ps[:, 1, bank, c0:c0 + n], sig[:, tok:tok + n], ALU.mult)
                    last.then_inc(free[1], 1)
                    dve.wait_ge(free[1], t + 1)
                    dve.sem_inc(glu_ready, 1)
                wd, bd = OFF["w_dw"], OFF["b_dw"]
                for t in range(2):
                    nc.vector.tensor_scalar(conv[:, t, :], glu[:, t, 0:CV], g.cols[:, wd + t * CONV_K:wd + t * CONV_K + 1],
                                            g.cols[:, bd + t:bd + t + 1], ALU.mult, ALU.add).then_inc(conv_step, 1)
                with dve.Fori(1, CONV_K) as k:
                    for t in range(2):
                        dve.wait_ge(conv_step, k * 2 + (t - 1))
                        nc.vector.scalar_tensor_tensor(conv[:, t, :], glu[:, t, bass.ds(k, CV)], g.cols[:, bass.ds(k + (wd + t * CONV_K), 1)],
                                                       conv[:, t, :], ALU.mult, ALU.add).then_inc(conv_step, 1)
                dve.wait_ge(done, 1)
                for t in range(2):
                    w = conv[:, t, :]
                    for ps, x in ((g.ps[:, 0, 0:2, 0:448], w[:, 0:896].rearrange("p (c n) -> p c n", c=2)),
                                  (g.ps[:, 0, 2, 0:C2], w[:, 896:LAT]), (g.ps[:, 0, 2, C2:C2 + CTX], w[:, CCTX:CCTX + CTX])):
                        nc.vector.scalar_tensor_tensor(x, ps, -1.0 / CW, x, ALU.mult, ALU.add).then_inc(centred, 1)
                dve.wait_ge(centred, 6)
                dve.sem_inc(free[0], 1)

                def window_sum(out, a, b):
                    nc.vector.tensor_tensor(out, a, b, ALU.add).then_inc(pool_step, 1)

                for s in range(2):
                    dve.wait_ge(free[s], 3)
                window_sum(summed[:, :, 1:PB], ppad[:, :, 0:PB - 1], ppad[:, :, 1:PB])
                dve.wait_ge(pool_step, 1)
                window_sum(glu[:, :, 2:PB - 1], summed[:, :, 1:PB - 2], summed[:, :, 3:PB])
                dve.wait_ge(pool_step, 2)
                window_sum(summed[:, 1, 4:PB - 3], glu[:, 1, 2:PB - 5], glu[:, 1, 6:PB - 1])
                dve.wait_ge(pool_step, 3)
                window_sum(glu[64:P, 1, 8:PB - 7], summed[64:P, 1, 4:PB - 11], summed[64:P, 1, 12:PB - 3])
                dve.wait_ge(pool_step, 4)
                for t in range(2):
                    dve.wait_ge(inv_in, 32 * (t + 1))
                    for src, r in ((summed, 0), (glu, 64)):
                        for a, b, at in ((0, LAT, 8), (LAT, T, PCTX)):
                            nc.vector.tensor_tensor(summed[r:r + 64, t, at:at + b - a], src[r:r + 64, t, at:at + b - a], inv[r:r + 64, a:b], ALU.mult).then_inc(inv_used if a == LAT else pool_step, 1)
                    dve.wait_ge(inv_used, 2 * (t + 1))
                    nc.vector.tensor_tensor(summed[:, t, 8:PCTX + CTX], summed[:, t, 8:PCTX + CTX], ppad[:, t, 8:PCTX + CTX], ALU.subtract).then_inc(pooled, 1)
                dve.wait_ge(mod_out, 1)
                late = g.mod[:, 3 * KD:6 * KD, :]
                nc.vector.tensor_tensor(late, late, g.cols[:, OFF["b_mod"] + 3 * KD:OFF["b_mod"] + 6 * KD].rearrange("p (m j) -> p m j", j=1).broadcast_to([P, 3 * KD, 2]),
                                        ALU.add).then_inc(mod_step, 1)
                dve.wait_ge(mod_step, 1)
                mod_gain(g, 1, "norm2_g", 4, mod_step)
                dve.wait_ge(free[1], USE_V)
                nc.vector.reciprocal(sig[:, :], sig[:, :]).then_inc(ln_step, 1)
                dve.wait_ge(ln_step, 1)
                for t in range(2):
                    for a, n, at in ((0, LAT, 0), (LAT, CTX, CCTX)):
                        nc.vector.tensor_tensor(conv[:, t, at:at + n], conv[:, t, at:at + n], sig[:, a:a + n], ALU.mult).then_inc(ln_step, 1)


V_PARTS = ((0, 4), (4, 8), (8, 10))


QT = NT
LOCAL = WIN * GW
PCOLS = LOCAL + PAST


def tile_plan(n):
    if n >= LAT // P:
        return None
    start = min(max(2 * n - KH // 2, 0), ROWS - KH)
    inner = 0 < 2 * n + 1 - KH // 2 < ROWS - KH
    return start * GW, (LOCAL if inner else KH * GW), start - 2 * n + KH - 2, inner


def blocks(n):
    plan = tile_plan(n)
    if plan is None:
        return [], [(5, 8), (6, 9)]
    v0 = plan[0] // P
    return [(j, v0 + j) for j in range(4)], ([(4, v0 + 4)] if plan[3] else []) + [(5, NT), (6, NT + 1)]


def phase_attention(g):
    nc = g.nc
    with ExitStack() as ctx:
        sb = lambda name, shape, dt=F32: ctx.enter_context(nc.sbuf_tensor(name, shape, dt))
        sem = lambda name: ctx.enter_context(nc.semaphore(name))
        KW_ = T + PAST
        q_src = sb("q_src", [P, T])
        k_src = sb("k_src", [P, KW_])
        v_src = sb("v_src", [P, NT + 2, DH])
        b_src = sb("b_src", [P, SLOTS, GW])
        QS = sb("QS", [P, 2, T], FR)
        KA = sb("KA", [P, 2, KW_], FR)
        KB = sb("KB", [P, 2, KW_], FR)
        VV = sb("VV", [P, 2, NT + 2, 2 * DH], FR)
        bias = sb("bias", [P, 2, SLOTS + WIN, GW])
        col_mask = sb("col_mask", [P, GW])
        prob = sb("prob", [P, 4, PCOLS])
        PT = sb("PT", [P, 2, 7, 2 * P], FR)
        OT = sb("OT", [P, T])
        OLO = sb("OLO", [64, T])
        OUT = sb("OUT", [64, T])
        st = sb("softmax_cols", [P, 4, 6])
        psS = g.ps_all[:, 0:4, :].rearrange("p (s b) n -> p s (b n)", s=2)
        psT = g.ps_all[:, 4:6, :].rearrange("p b n -> p (b n)")
        psV = g.ps_all[:, 6:8, :]
        q_in, k_in, v_in, b_in, mask_in = sem("q_in"), sem("k_in"), sem("v_in"), sem("b_in"), sem("mask_in")
        q_hi, q_lo, k_hi, k_lo, v_hi, v_lo = sem("q_hi"), sem("q_lo"), sem("k_hi"), sem("k_lo"), sem("v_hi"), sem("v_lo")
        table, table_ready = sem("bias_table"), sem("bias_ready")
        scored, max_step, max_ready, exp_ready, sum_step, sum_ready, normal = (
            sem("scored"), sem("max_step"), sem("max_ready"), sem("exp_ready"), sem("sum_step"), sem("sum_ready"), sem("normalised"))
        t_done, p_hi, p_lo = (sem("t_done0"), sem("t_done1")), (sem("p_hi0"), sem("p_hi1")), (sem("p_lo0"), sem("p_lo1"))
        times_v, summed_v, olo_ready, out_ready, out_stored = (sem("times_v"), sem("summed_v"), sem("olo_ready"),
                                                               sem("out_ready"), sem("out_stored"))
        passed = sem("pool_wait_passed")
        NL = LAT // P
        LAST = 2 * QT
        TURN, TIMES = 3, 4

        def tile(i, s):
            return None if isinstance(i, int) and i * LAST + s < 0 else (i, s)

        def b0(gs2, s):
            return gs2 * (2 * NL) + (s // QT) * NL + min(s % QT, NL)

        def wait(eng, semaphore, value):
            if not isinstance(value, int) or value > 0:
                eng.wait_ge(semaphore, value)

        q_rows = g.d["qT"].rearrange("a p t -> (a p) t")
        k_rows = g.d["kT"].rearrange("a p t -> (a p) t")
        out_rows = g.d["branch"].rearrange("a p t -> (a p) t")

        def head_pairs(eng, body):
            body(0, True)
            with eng.Fori(1, HEADS // 2 - 1) as i:
                body(i, True)
            body(HEADS // 2 - 1, False)

        with nc.Block() as block:

            @block.sync
            def _(sp):
                def load(h, i, b):
                    sp.wait_ge(k_lo, h)
                    for half in range(2):
                        sp.dma_start(k_src[half * 64:half * 64 + 64, :], k_rows[bass.ds(i * P + b * 64, 64), :]).then_inc(k_in, 16)
                    sp.wait_ge(q_lo, h)
                    for half in range(2):
                        sp.dma_start(q_src[half * 64:half * 64 + 64, :], q_rows[bass.ds(i * P + b * 64, 64), :]).then_inc(q_in, 16)
                    sp.wait_ge(v_lo, h)
                    sp.dma_start(v_src[:, 0:NT, :], g.d["v"][:, bass.ds(i * P + b * 64, 64)].rearrange("(t p) n -> p t n", p=P)).then_inc(v_in, 16)
                    sp.dma_start(v_src[:, NT:NT + 2, :], g.d["cache_v"][:, bass.ds(i * P + b * 64, 64)].rearrange("(t p) n -> p t n", p=P)).then_inc(v_in, 16)
                    sp.wait_ge(table, h)
                    for half in range(2):
                        sp.dma_start(b_src[half * 64:half * 64 + 64, :, :], rpb_window(g, i, b, 1 - half)).then_inc(b_in, 16)

                sp.dma_start(col_mask[:, :], g.d["col_mask"]).then_inc(mask_in, 16)
                load(0, 0, 0)
                load(1, 0, 1)

                def pair(i, more):
                    for b in range(2):
                        if more:
                            load(i * 2 + (b + 2), i + 1, b)
                        sp.wait_ge(out_ready, i * 2 + (b + 1))
                        sp.dma_start(out_rows[bass.ds(i * P + b * 64, 64), :], OUT[:, :]).then_inc(out_stored, 16)

                for i in range(HEADS // 2):
                    pair(i, i < HEADS // 2 - 1)
                sp.wait_ge(out_stored, 16 * HEADS)

            @block.tensor
            def _(pe):
                def scores(i, s):
                    b, n = s // QT % 2, s % QT
                    if n == 0:
                        pe.wait_ge(q_lo, i * 2 + (b + 1))
                        pe.wait_ge(k_lo, i * 2 + (b + 1))
                    wait(pe, exp_ready, i * LAST + (s - 1))
                    q = QS[:, b, n * P:(n + 1) * P]
                    plan = tile_plan(n)
                    regions = [(LOCAL, LOCAL + PAST, T if plan else LAT)]
                    if plan:
                        regions.insert(0, (0, 512, plan[0]))
                        if plan[3]:
                            regions.insert(1, (512, LOCAL, plan[0] + 512))
                    for c0, c1, k0 in regions:
                        for m, K in enumerate((KA, KB)):
                            mm = nc.tensor.matmul(psS[:, s % 2, c0:c1], q, K[:, b, k0:k0 + c1 - c0], start=(m == 0), stop=(m == 1))
                    mm.then_inc(scored, 1)

                def turn(i, s):
                    n = s % QT
                    pe.wait_ge(normal, i * LAST + (s + 1))
                    for bank, bl in enumerate(blocks(n)):
                        if bl:
                            wait(pe, p_lo[bank], b0(i, s) if bank == 0 else i * LAST + s)
                            for j, _ in bl:
                                mm = nc.tensor.transpose(psT[:, j * P:(j + 1) * P], prob[:, s % 4, j * P:(j + 1) * P], g.ident[:, :])
                            mm.then_inc(t_done[bank], 1)

                def value(i, s):
                    b, n = s // QT % 2, s % QT
                    if n == 0:
                        pe.wait_ge(v_lo, i * 2 + (s // QT + 1))
                    if n < NL:
                        pe.wait_ge(p_lo[0], b0(i, s) + 1)
                    pe.wait_ge(p_lo[1], i * LAST + (s + 1))
                    wait(pe, summed_v, i * LAST + (s - 1))
                    both = sum(blocks(n), [])
                    for m, (j, v) in enumerate(both):
                        mm = nc.tensor.matmul(psV[:, s % 2, 0:2 * P], VV[:, b, v, :], PT[:, s % 2, j, :], start=(m == 0), stop=(m == len(both) - 1))
                    mm.then_inc(times_v, 1)

                def pair(i, more):
                    for s in range(LAST if more else LAST + TIMES):
                        if s < LAST:
                            scores(i, s)
                        if tile(i, s - TURN) and s - TURN < LAST:
                            turn(i, s - TURN)
                        if tile(i, s - TIMES):
                            value(i, s - TIMES)

                head_pairs(pe, pair)

            @block.scalar
            def _(act):
                def prepare(what, h, b):
                    if what == "k":
                        act.wait_ge(k_in, h * 32 + 32)
                        nc.scalar.activation(KA[:, b, :], k_src[:, :], ACT.Copy).then_inc(k_hi, 1)
                    elif what == "q":
                        act.wait_ge(q_in, h * 32 + 32)
                        nc.scalar.activation(QS[:, b, :], q_src[:, :], ACT.Copy, scale=DH ** -0.5).then_inc(q_hi, 1)
                    elif what == "v":
                        act.wait_ge(v_in, h * 32 + 32)
                        nc.scalar.activation(VV[:, b, :, 0:DH], v_src[:, :, :], ACT.Copy).then_inc(v_hi, 1)

                def exponential(i, s):
                    plan = tile_plan(s % QT)
                    act.wait_ge(max_ready, i * LAST + (s + 1))
                    c = st[:, s % 4, :]
                    pr = prob[:, s % 4, :]
                    if plan:
                        nc.scalar.activation(pr[:, 0:plan[1]], pr[:, 0:plan[1]], ACT.Exp, bias=c[:, 2:3], accum_out=c[:, 3:4])
                    nc.scalar.activation(pr[:, LOCAL:PCOLS], psS[:, s % 2, LOCAL:PCOLS], ACT.Exp, bias=c[:, 2:3], accum_out=c[:, 4:5]).then_inc(exp_ready, 1)

                def upper(i, s):
                    n = s % QT
                    wait(act, times_v, i * LAST + (s - 1))
                    for bank, bl in enumerate(blocks(n)):
                        if bl:
                            act.wait_ge(t_done[bank], (b0(i, s) if bank == 0 else i * LAST + s) + 1)
                            j0, j1 = bl[0][0], bl[-1][0] + 1
                            nc.scalar.activation(PT[:, s % 2, j0:j1, 0:P], psT[:, j0 * P:j1 * P].rearrange("p (j n) -> p j n", n=P), ACT.Copy).then_inc(p_hi[bank], 1)

                def pair(i, more):
                    for s in range(LAST if more else LAST + TIMES):
                        if tile(i, s - TURN) and s - TURN < LAST:
                            upper(i, s - TURN)
                        if s < LAST:
                            exponential(i, s)
                        if s in (5, 6, 7):
                            prepare("kqv"[s - 5], i * 2 + 1, 1)
                        if more and s - QT in (5, 6, 7):
                            prepare("kqv"[s - QT - 5], i * 2 + 2, 0)
                        done = tile(i, s - TIMES - QT + 1)
                        if done and (s - TIMES - QT + 1) % QT == 0:
                            h = (s - TIMES - QT + 1) // QT
                            act.wait_ge(summed_v, i * LAST + QT * (h + 1))
                            wait(act, out_ready, i * 2 + h)
                            nc.scalar.activation(OLO[:, :], OT[64:P, :], ACT.Copy).then_inc(olo_ready, 1)

                for w in "kqv":
                    prepare(w, 0, 0)
                head_pairs(act, pair)

            @block.vector
            def _(dve):
                def prepare(what, h, b):
                    if what == "q":
                        dve.wait_ge(q_hi, h + 1)
                        r = 64 if b == 0 else 0
                        nc.vector.scalar_tensor_tensor(QS[r:r + 64, b, :], q_src[r:r + 64, :], DH ** -0.5, QS[r:r + 64, b, :].bitcast(F32),
                                                       ALU.mult, ALU.subtract).then_inc(q_lo, 1)
                    else:
                        dve.wait_ge(b_in, h * 32 + 32)
                        nc.vector.tensor_tensor(bias[:, b, 0:SLOTS, :], b_src[:, :, ::-1],
                                                col_mask[:, :].rearrange("p (a n) -> p a n", a=1).broadcast_to([P, SLOTS, GW]), ALU.add).then_inc(table, 1)
                        nc.vector.memset(bias[0:64, b, SLOTS + KH:SLOTS + WIN, :], NEG)
                        nc.vector.memset(bias[64:P, b, SLOTS:SLOTS + 1, :], NEG)
                        nc.vector.memset(bias[64:P, b, SLOTS + KH + 1:SLOTS + WIN, :], NEG)
                        dve.wait_ge(table, h + 1)
                        nc.vector.tensor_copy(bias[0:64, b, SLOTS:SLOTS + KH, :], bias[0:64, b, KH // 2 - 2:KH // 2 - 2 + KH, :])
                        nc.vector.tensor_copy(bias[64:P, b, SLOTS + 1:SLOTS + KH + 1, :], bias[64:P, b, KH // 2 - 1:KH // 2 - 1 + KH, :]).then_inc(table_ready, 1)

                def maximum(i, s):
                    b, n = s // QT % 2, s % QT
                    plan = tile_plan(n)
                    dve.wait_ge(scored, i * LAST + (s + 1))
                    wait(dve, t_done[1], i * LAST + (s - 3))
                    c = st[:, s % 4, :]
                    if not plan:
                        nc.vector.tensor_reduce(c[:, 2:3], psS[:, s % 2, LOCAL:PCOLS], AX, ALU.max, negate=True).then_inc(max_ready, 1)
                        return
                    if n == 0:
                        dve.wait_ge(table_ready, i * 2 + (b + 1))
                    slot = SLOTS if plan[3] else plan[2]
                    nc.vector.tensor_reduce(c[:, 1:2], psS[:, s % 2, LOCAL:PCOLS], AX, ALU.max).then_inc(max_step, 1)
                    nc.vector.tensor_tensor_reduce(prob[:, s % 4, 0:plan[1]], psS[:, s % 2, 0:plan[1]],
                                                   bias[:, b, slot:slot + plan[1] // GW, :].rearrange("p a n -> p (a n)"),
                                                   1.0, -3.0e38, ALU.add, ALU.max, c[:, 0:1]).then_inc(max_step, 1)
                    dve.wait_ge(max_step, 2 * (b0(i, s) + 1))
                    nc.vector.tensor_scalar(c[:, 2:3], c[:, 0:1], c[:, 1:2], -1.0, ALU.max, ALU.mult).then_inc(max_ready, 1)

                def total(i, s):
                    c = st[:, s % 4, :]
                    dve.wait_ge(exp_ready, i * LAST + (s + 1))
                    if tile_plan(s % QT):
                        nc.vector.tensor_tensor(c[:, 4:5], c[:, 3:4], c[:, 4:5], ALU.add).then_inc(sum_step, 1)
                        dve.wait_ge(sum_step, b0(i, s) + 1)
                    nc.vector.reciprocal(c[:, 5:6], c[:, 4:5]).then_inc(sum_ready, 1)

                def lower(i, s):
                    for bank, bl in enumerate(blocks(s % QT)):
                        if bl:
                            dve.wait_ge(p_hi[bank], (b0(i, s) if bank == 0 else i * LAST + s) + 1)
                            j0, j1 = bl[0][0], bl[-1][0] + 1
                            nc.vector.tensor_tensor(PT[:, s % 2, j0:j1, P:2 * P], psT[:, j0 * P:j1 * P].rearrange("p (j n) -> p j n", n=P),
                                                    PT[:, s % 2, j0:j1, 0:P].bitcast(F32), ALU.subtract).then_inc(p_lo[bank], 1)

                def gather(i, s):
                    n = s % QT
                    dve.wait_ge(times_v, i * LAST + (s + 1))
                    if n == 0:
                        wait(dve, out_ready, i * 2 + s // QT)
                    nc.vector.tensor_reduce(OT[:, n * P:(n + 1) * P], psV[:, s % 2, 0:2 * P].rearrange("p (a q) -> p q a", a=2), AX, ALU.add).then_inc(summed_v, 1)

                def pair(i, more):
                    for s in range(LAST if more else LAST + TIMES):
                        if s < LAST:
                            maximum(i, s)
                        if tile(i, s - 1) and s - 1 < LAST:
                            total(i, s - 1)
                        if tile(i, s - TURN) and s - TURN < LAST:
                            lower(i, s - TURN)
                        if tile(i, s - TIMES):
                            gather(i, s - TIMES)
                        if s in (6, 7):
                            prepare("qb"[s - 6], i * 2 + 1, 1)
                        if more and s - QT in (6, 7):
                            prepare("qb"[s - QT - 6], i * 2 + 2, 0)
                        if tile(i, s - TIMES - QT + 1) and (s - TIMES - QT + 1) % QT == 0:
                            h = (s - TIMES - QT + 1) // QT
                            dve.wait_ge(olo_ready, i * 2 + (h + 1))
                            wait(dve, out_stored, i * 32 + 16 * h)
                            nc.vector.tensor_tensor(OUT[:, :], OT[0:64, :], OLO[:, :], ALU.add).then_inc(out_ready, 1)

                dve.wait_ge(mask_in, 16)
                for w in "qb":
                    prepare(w, 0, 0)
                head_pairs(dve, pair)

            @block.gpsimd
            def _(pool):
                def prepare(what, h, b):
                    if what == "k":
                        pool.wait_ge(k_hi, h + 1)
                        nc.gpsimd.tensor_tensor(KB[:, b, :], k_src[:, :], KA[:, b, :].bitcast(F32), ALU.subtract).then_inc(k_lo, 1)
                    elif what == "v":
                        pool.wait_ge(v_hi, h + 1)
                        nc.gpsimd.tensor_tensor(VV[:, b, :, DH:2 * DH], v_src[:, :, :], VV[:, b, :, 0:DH].bitcast(F32), ALU.subtract).then_inc(v_lo, 1)

                def normalise(i, s):
                    plan = tile_plan(s % QT)
                    pool.wait_ge(sum_ready, i * LAST + (s + 1))
                    pool.sem_inc(passed, 1)
                    c, pr = st[:, s % 4, :], prob[:, s % 4, :]
                    if plan and not plan[3]:
                        nc.gpsimd.tensor_scalar(pr[:, 0:plan[1]], pr[:, 0:plan[1]], c[:, 5:6], 1.0, ALU.mult, ALU.mult)
                    a = 0 if plan and plan[3] else LOCAL
                    nc.gpsimd.tensor_scalar(pr[:, a:PCOLS], pr[:, a:PCOLS], c[:, 5:6], 1.0, ALU.mult, ALU.mult).then_inc(normal, 1)

                def pair(i, more):
                    for s in range(LAST if more else LAST + 1):
                        if tile(i, s - 1):
                            normalise(i, s - 1)
                        if s in (5, 7):
                            prepare("k" if s == 5 else "v", i * 2 + 1, 1)
                        if more and s - QT in (5, 7):
                            prepare("k" if s - QT == 5 else "v", i * 2 + 2, 0)

                for w in "kv":
                    prepare(w, 0, 0)
                head_pairs(pool, pair)


def rpb_window(g, i, b, first):
    rpb = g.d["rpb"]
    rows, width = 2 * KH - 1, 2 * GW - 1
    return bass.AP(tensor=rpb.tensor, offset=rpb.offset + ((2 * i + b) * rows + first) * width,
                   ap=[[1, GW], [width, SLOTS], [1, GW]])


def phase_merge(g):
    nc = g.nc
    with ExitStack() as ctx:
        sb = lambda name, shape, dt=F32: ctx.enter_context(nc.sbuf_tensor(name, shape, dt))
        sem = lambda name: ctx.enter_context(nc.semaphore(name))
        W = Weights(g, ctx, "g")
        BH = sb("BH", [P, KD, T], FR)
        BL = sb("BL", [P, KD, T], FR)
        stage = sb("branch_stage", [P, T])
        gate = sb("gate", [P, T])
        total = sb("total", [P, T])
        part = sb("part", [P, T])
        b_in, b_hi, b_lo = sem("b_in"), sem("b_hi"), sem("b_lo")
        gate_ready, free0, free1 = sem("gate_ready"), sem("merge_free0"), sem("merge_free1")
        part_ready, part_added, stored = sem("part_ready"), sem("part_added"), sem("merged_stored")
        passed = sem("sync_wait_passed")
        wv = g.d["w_in"].rearrange("(k p) n -> p k n", p=P)
        proj = {0: ("w_oa", 4, 0), 1: ("w_ob", 2, 4), 2: ("w_oc", 2, 6)}
        kts = [KD, 4, KD, 2, KD, 2]

        with nc.Block() as block:

            @block.sync
            def _(sp):
                def load(i, j):
                    b = j % 2
                    if b == 0:
                        src = wv[:, :, bass.ds(i * P + (GATE_COL + (j // 2) * D), P)]
                    else:
                        name = proj[j // 2][0]
                        src = g.d[name].rearrange("(k p) n -> p k n", p=P)[:, :, bass.ds(i * P, P)]
                    sp.dma_start(W.raw[:, b, 0:kts[j] * P].rearrange("p (k n) -> p k n", n=P), src).then_inc(W.raw_in[b], 16)

                load(0, 0)
                load(0, 1)
                for k in range(KD):
                    sp.wait_ge(b_lo, k)
                    sp.dma_start(stage[:, :], g.d["branch"][k, :, :]).then_inc(b_in, 16)
                    if k in (3, 7):
                        sp.wait_ge(W.lo_ready, 1 if k == 3 else 2)
                        load(0, 2 if k == 3 else 3)
                for j in (4, 5):
                    sp.wait_ge(W.lo_ready, j - 1)
                    load(0, j)
                with sp.Fori(0, KD - 1) as i:
                    for j in range(6):
                        sp.wait_ge(W.lo_ready, i * 6 + (j + 5))
                        if j % 2:
                            sp.sem_inc(passed, 1)
                        load(i + 1, j)
                    sp.wait_ge(part_added, i * 2 + 2)
                    sp.dma_start(g.d["merged"][bass.ds(i, 1), :, :].rearrange("a p t -> p (a t)"), total[:, :]).then_inc(stored, 16)
                sp.wait_ge(part_added, 2 * KD)
                sp.dma_start(g.d["merged"][KD - 1, :, :], total[:, :]).then_inc(stored, 16)
                sp.wait_ge(stored, 16 * KD)

            @block.tensor
            def _(pe):
                def tile(i, skip):
                    for j in range(6):
                        s = j % 2
                        pe.wait_ge(W.lo_ready, i * 6 + (j + 1))
                        pe.wait_ge((free0, free1)[s], i * 3 + j // 2)
                        if s == 0:
                            ah, al, k0 = g.AH, g.AL, 0
                        else:
                            ah, al, k0 = BH, BL, proj[j // 2][2]
                            if skip:
                                pe.wait_ge(b_lo, k0 + kts[j])
                        gemm(nc, g.ps[:, s], W.hi[:, s, :], W.lo[:, s, :], ah, al,
                             [(k * P, k0 + k) for k in range(kts[j])]).then_inc(W.used, 1)

                tile(0, True)
                with pe.Fori(1, KD) as i:
                    tile(i, False)

            @block.scalar
            def _(act):
                def split(i, j, first=False):
                    b, n = j % 2, kts[j] * P
                    act.wait_ge(W.raw_in[b], i * 48 + 16 * (j // 2 + 1))
                    if not first:
                        act.wait_ge(W.used, i * 6 + (j - 1))
                    nc.scalar.activation(W.hi[:, b, 0:n], W.raw[:, b, 0:n], ACT.Copy).then_inc(W.hi_ready, 1)

                def gate_out(i, j):
                    act.wait_ge(W.used, i * 6 + (j + 1))
                    if not isinstance(i, int) or 3 * i + j:
                        act.wait_ge(free1, i * 3 + j // 2)
                    c = OFF["b_gate"] + (j // 2) * KD
                    for ps, out in chunk_views(g.ps[:, 0], gate):
                        last = nc.scalar.activation(out, ps, ACT.Sigmoid, bias=g.cols[:, bass.ds(i + c, 1)])
                    last.then_inc(free0, 1)

                def tile(i, following):
                    for j in range(6):
                        if j % 2 == 0:
                            gate_out(i, j)
                        if j + 2 < 6:
                            split(i, j + 2)
                        elif following:
                            split(i + 1, j - 4)

                split(0, 0, True)
                split(0, 1, True)
                for k in range(KD):
                    act.wait_ge(b_in, 16 * (k + 1))
                    nc.scalar.activation(BH[:, k, :], stage[:, :], ACT.Copy).then_inc(b_hi, 1)
                tile(0, True)
                with act.Fori(1, KD - 1) as i:
                    tile(i, True)
                tile(KD - 1, False)

            @block.gpsimd
            def _(pool):
                def lower(i, j):
                    b, n = j % 2, kts[j] * P
                    pool.wait_ge(W.hi_ready, i * 6 + (j + 1))
                    nc.gpsimd.tensor_tensor(W.lo[:, b, 0:n], W.raw[:, b, 0:n], W.hi[:, b, 0:n].bitcast(F32), ALU.subtract).then_inc(W.lo_ready, 1)

                lower(0, 0)
                lower(0, 1)
                for k in range(KD):
                    pool.wait_ge(b_hi, k + 1)
                    nc.gpsimd.tensor_tensor(BL[:, k, :], stage[:, :], BH[:, k, :].bitcast(F32), ALU.subtract).then_inc(b_lo, 1)
                for j in range(2, 6):
                    lower(0, j)
                with pool.Fori(1, KD) as i:
                    for j in range(6):
                        lower(i, j)

            @block.vector
            def _(dve):
                def tile(i):
                    for b in range(3):
                        dve.wait_ge(free0, i * 3 + (b + 1))
                        dve.wait_ge(W.used, i * 6 + (2 * b + 2))
                        if b == 0:
                            if not isinstance(i, int):
                                dve.wait_ge(stored, i * 16)
                        elif b == 2:
                            dve.wait_ge(part_added, i * 2 + 1)
                        out = total if b == 0 else part
                        for (ps, o), (_, x) in zip(chunk_views(g.ps[:, 1], out), chunk_views(g.ps[:, 1], gate)):
                            last = nc.vector.tensor_tensor(o, ps, x, ALU.mult)
                        last.then_inc(free1, 1)
                        if b:
                            dve.wait_ge(free1, i * 3 + (b + 1))
                            nc.vector.tensor_tensor(total[:, :], total[:, :], part[:, :], ALU.add).then_inc(part_added, 1)

                tile(0)
                with dve.Fori(1, KD) as i:
                    tile(i)


def residual(g, dve, XT, m, gate_part, s, free):
    nc = g.nc
    ps, x = g.ps[:, s], XT[:, m, :]
    for p, o, j in ((ps[:, 0:2, 0:448], x[..., 0:896].rearrange("p (c n) -> p c n", c=2), 0),
                    (ps[:, 2, 0:C2], x[..., 896:LAT], 0), (ps[:, 2, C2:C2 + CTX], x[..., LAT:T], 1)):
        last = nc.vector.scalar_tensor_tensor(o, p, g.mod[:, gate_part * KD + m, j:j + 1], o, ALU.mult, ALU.add)
    last.then_inc(free, 1)


def phase_output(g):
    nc = g.nc
    with ExitStack() as ctx:
        sb = lambda name, shape, dt=F32: ctx.enter_context(nc.sbuf_tensor(name, shape, dt))
        sem = lambda name: ctx.enter_context(nc.semaphore(name))
        XT = g.XT
        W = Weights(g, ctx, "o")
        stage = sb("merged_stage", [P, 2, T])
        square = sb("square1", [P, 2, T])
        sumsq = sb("sumsq1", [P, T])
        rstd = sb("rstd1", [P, T])
        normed = sb("normed1", [P, 2, T])
        m_in = (sem("merged_in0"), sem("merged_in1"))
        m_hi, m_lo, x_in = sem("m_hi"), sem("m_lo"), sem("x_back")
        free = (sem("out_free0"), sem("out_free1"))
        zero, sq_ready, sq_added, stat_done = sem("out_zero"), sem("out_sq"), sem("out_sq_added"), sem("out_stat")
        root_ready, rstd_ready, scaled, t_ready, ah_ready, al_ready = (
            sem("out_root"), sem("out_rstd"), sem("out_scaled"), sem("out_t"), sem("out_ah"), sem("out_al"))
        wv = g.d["w_out"].rearrange("(k p) n -> p k n", p=P)
        with nc.Block() as block:

            @block.sync
            def _(sp):
                for m in range(2):
                    sp.dma_start(W.columns(m, P), wv[:, :, m * P:(m + 1) * P]).then_inc(W.raw_in[m], 16)
                for k in range(KD):
                    if k >= 2:
                        sp.wait_ge(m_lo, k - 1)
                    sp.dma_start(stage[:, k % 2, :], g.d["merged"][k, :, :]).then_inc(m_in[k % 2], 16)
                sp.dma_start(XT[:, :, :], g.d["xT"].rearrange("k p t -> p k t")).then_inc(x_in, 16)
                with sp.Fori(1, KD // 2) as i:
                    for b in range(2):
                        sp.wait_ge(W.lo_ready, i * 2 + (b - 1))
                        sp.dma_start(W.columns(b, P), wv[:, :, bass.ds(i * (2 * P) + b * P, P)]).then_inc(W.raw_in[b], 16)

            @block.tensor
            def _(pe):
                for m in range(2):
                    pe.wait_ge(W.lo_ready, m + 1)
                for k in range(KD):
                    pe.wait_ge(m_lo, k + 1)
                    for m in range(2):
                        mm = gemm(nc, g.ps[:, m], W.hi[:, m, :], W.lo[:, m, :], g.AH, g.AL, [(k * P, k)], first=k == 0, last=k == KD - 1)
                        if k == KD - 1:
                            mm.then_inc(W.used, 1)
                with pe.Fori(1, KD // 2) as i:
                    for s in range(2):
                        pe.wait_ge(W.lo_ready, i * 2 + (s + 1))
                        pe.wait_ge(free[s], i)
                        gemm(nc, g.ps[:, s], W.hi[:, s, :], W.lo[:, s, :], g.AH, g.AL, [(k * P, k) for k in range(KD)]).then_inc(W.used, 1)
                pe.wait_ge(sq_added, KD)
                pe.wait_ge(free[0], KD // 2)
                for c, (c0, c1) in enumerate(CHUNKS):
                    mm = nc.tensor.matmul(g.ps[:, 0, c, 0:c1 - c0], g.ones[:, :], sumsq[:, c0:c1], start=True, stop=True)
                mm.then_inc(stat_done, 1)

            @block.scalar
            def _(act):
                def split(m):
                    act.wait_ge(W.raw_in[m % 2], 16 * (m // 2 + 1))
                    if m >= 2:
                        act.wait_ge(W.used, m - 1)
                    nc.scalar.activation(W.hi[:, m % 2, :], W.raw[:, m % 2, :], ACT.Copy).then_inc(W.hi_ready, 1)

                split(0)
                split(1)
                for k in range(KD):
                    act.wait_ge(m_in[k % 2], 16 * (k // 2 + 1))
                    nc.scalar.activation(g.AH[:, k, :], stage[:, k % 2, :], ACT.Copy).then_inc(m_hi, 1)
                for m in range(KD):
                    if m + 2 < KD:
                        split(m + 2)
                    act.wait_ge(free[m % 2], m // 2 + 1)
                    if m >= 2:
                        act.wait_ge(sq_added, m - 1)
                    nc.scalar.activation(square[:, m % 2, :], XT[:, m, :], ACT.Square).then_inc(sq_ready, 1)
                act.wait_ge(stat_done, 1)
                root(g, act, rstd, root_ready)
                copies(g, act, normed, t_ready, ah_ready)

            @block.vector
            def _(dve):
                dve.wait_ge(x_in, 16)
                for m in range(KD):
                    dve.wait_ge(W.used, m + 1)
                    residual(g, dve, XT, m, 2, m % 2, free[m % 2])
                dve.wait_ge(root_ready, 2)
                nc.vector.reciprocal(rstd[:, :], rstd[:, :]).then_inc(rstd_ready, 1)
                dve.wait_ge(rstd_ready, 1)
                dve.wait_ge(free[0], KD // 2)
                dve.wait_ge(free[1], KD // 2)
                scale_shift(g, dve, XT, rstd, normed, 1, 3, scaled, t_ready, al_ready)

            @block.gpsimd
            def _(pool):
                nc.gpsimd.memset(sumsq[:, :], 0.0).then_inc(zero, 1)
                for m in range(2):
                    pool.wait_ge(W.hi_ready, m + 1)
                    nc.gpsimd.tensor_tensor(W.lo[:, m, :], W.raw[:, m, :], W.hi[:, m, :].bitcast(F32), ALU.subtract).then_inc(W.lo_ready, 1)
                for k in range(KD):
                    pool.wait_ge(m_hi, k + 1)
                    nc.gpsimd.tensor_tensor(g.AL[:, k, :], stage[:, k % 2, :], g.AH[:, k, :].bitcast(F32), ALU.subtract).then_inc(m_lo, 1)
                pool.wait_ge(zero, 1)
                for m in range(KD):
                    if m + 2 < KD:
                        pool.wait_ge(W.hi_ready, m + 3)
                        b = m % 2
                        nc.gpsimd.tensor_tensor(W.lo[:, b, :], W.raw[:, b, :], W.hi[:, b, :].bitcast(F32), ALU.subtract).then_inc(W.lo_ready, 1)
                    pool.wait_ge(sq_ready, m + 1)
                    if m:
                        pool.wait_ge(sq_added, m)
                    nc.gpsimd.tensor_tensor(sumsq[:, :], sumsq[:, :], square[:, m % 2, :], ALU.add).then_inc(sq_added, 1)
                rests(g, pool, normed, ah_ready, al_ready)


def phase_ffn(g):
    nc = g.nc
    with ExitStack() as ctx:
        sb = lambda name, shape, dt=F32: ctx.enter_context(nc.sbuf_tensor(name, shape, dt))
        sem = lambda name: ctx.enter_context(nc.semaphore(name))
        XT = g.XT
        W = Weights(g, ctx, "f")
        gated = sb("silu_a", [P, T])
        act32 = sb("act32", [P, 2, T])
        actH = sb("actH", [P, 2, T], FR)
        actL = sb("actL", [P, 2, T], FR)
        free = (sem("ffn_free0"), sem("ffn_free1"))
        hid_done, out_done = sem("hidden_done"), sem("down_done")
        a_ready, b_ready, h_hi, h_lo = sem("a_ready"), sem("b_ready"), sem("h_hi"), sem("h_lo")
        gu = g.d["w_gu"].rearrange("(k p) n -> p k n", p=P)
        down = g.d["w_down"].rearrange("(k p) n -> p k n", p=P)
        kinds = ("a0", "b0", "d0", "d1", "a1", "b1")
        with nc.Block() as block:

            def wcount(j, n):
                return j * 6 + (n - 1)

            @block.sync
            def _(sp):
                def load(j, kind):
                    b = int(kind in ("b0", "d1", "b1"))
                    if kind[0] == "d":
                        raw = W.raw[:, b, :].rearrange("p (k n) -> p k n", n=512)
                        src = down[:, bass.ds(j * 2 - 2, 2), b * 512:(b + 1) * 512]
                    else:
                        raw = W.columns(b, P)
                        src = gu[:, :, bass.ds(j * (2 * P) + (int(kind[1]) * P + (HID if kind[0] == "b" else 0)), P)]
                    sp.dma_start(raw, src).then_inc(W.raw_in[b], 16)

                for n, kind in enumerate(("a0", "b0", "a1", "b1")):
                    if n >= 2:
                        sp.wait_ge(W.lo_ready, n - 1)
                    load(0, kind)
                with sp.Fori(1, BLOCKS) as j:
                    for n, kind in enumerate(kinds):
                        sp.wait_ge(W.lo_ready, wcount(j, n) - 2)
                        load(j, kind)
                for b in range(2):
                    sp.wait_ge(W.lo_ready, wcount(BLOCKS, b) - 2)
                    load(BLOCKS, ("d0", "d1")[b])

            @block.tensor
            def _(pe):
                def hidden(s, w, uses):
                    pe.wait_ge(W.lo_ready, w)
                    pe.wait_ge(free[s], uses)
                    gemm(nc, g.ps[:, s], W.hi[:, s, :], W.lo[:, s, :], g.AH, g.AL, [(k * P, k) for k in range(KD)]).then_inc(W.used, 1)

                def output(j, w0, uses):
                    pe.wait_ge(h_lo, j * 2)
                    for m in range(KD):
                        s, ws = m % 2, m // 4
                        if m % 4 == 0:
                            pe.wait_ge(W.lo_ready, w0 + ws + 1)
                        pe.wait_ge(free[s], uses + m // 2)
                        mm = gemm(nc, g.ps[:, s], W.hi[:, ws, :], W.lo[:, ws, :], actH, actL, [(k * 512 + (m % 4) * P, k) for k in range(2)])
                        mm.then_inc(out_done, 1)
                        if m % 4 == 3:
                            pe.wait_ge(out_done, j * KD - KD + (m + 1))
                            pe.sem_inc(W.used, 1)

                for u in range(4):
                    hidden(u % 2, u + 1, u // 2)
                with pe.Fori(1, BLOCKS) as j:
                    for s in range(2):
                        hidden(s, wcount(j, s), j * 6 - 4)
                    output(j, j * 6, j * 6 - 3)
                    for s in range(2):
                        hidden(s, wcount(j, 4 + s), j * 6 + 1)
                output(BLOCKS, wcount(BLOCKS, -1), BLOCKS * 6 - 4)

            @block.scalar
            def _(act):
                def split(b, raw, used=None):
                    act.wait_ge(W.raw_in[b], raw)
                    if used is not None:
                        act.wait_ge(W.used, used)
                    nc.scalar.activation(W.hi[:, b, :], W.raw[:, b, :], ACT.Copy).then_inc(W.hi_ready, 1)

                def silu(w, hid):
                    act.wait_ge(W.used, w)
                    act.wait_ge(b_ready, hid)
                    for ps, out in chunk_views(g.ps[:, 0], gated):
                        last = nc.scalar.activation(out, ps, ACT.Silu)
                    last.then_inc(free[0], 1)

                def upper(t, hid):
                    act.wait_ge(b_ready, hid)
                    nc.scalar.activation(actH[:, t, :], act32[:, t, :], ACT.Copy).then_inc(h_hi, 1)

                split(0, 16)
                split(1, 16)
                for t in range(2):
                    silu(2 * t + 1, t)
                    split(0, 16 * (t + 2), 2 * t + 1)
                    split(1, 16 * (t + 2), 2 * t + 2)
                    upper(t, t + 1)
                with act.Fori(1, BLOCKS) as j:
                    w = j * 6 - 2
                    r = j * 48 - 16
                    silu(w + 1, j * 2)
                    split(0, r + 32, w + 1)
                    split(1, r + 32, w + 2)
                    split(0, r + 48, w + 3)
                    split(1, r + 48, w + 4)
                    act.wait_ge(out_done, j * KD)
                    upper(0, j * 2 + 1)
                    silu(w + 5, j * 2 + 1)
                    split(0, r + 64, w + 5)
                    split(1, r + 64, w + 6)
                    upper(1, j * 2 + 2)

            @block.vector
            def _(dve):
                def product(t, w, uses0, hid):
                    dve.wait_ge(W.used, w)
                    dve.wait_ge(free[0], uses0)
                    dve.wait_ge(h_lo, hid)
                    for (ps, o), (_, x) in zip(chunk_views(g.ps[:, 1], act32[:, t, :]), chunk_views(g.ps[:, 1], gated)):
                        last = nc.vector.tensor_tensor(o, ps, x, ALU.mult)
                    last.then_inc(free[1], 1)
                    dve.wait_ge(free[1], uses0)
                    dve.sem_inc(b_ready, 1)

                def add_output(j):
                    for m in range(KD):
                        dve.wait_ge(out_done, j * KD - KD + (m + 1))
                        residual(g, dve, XT, m, 5, m % 2, free[m % 2])

                for t in range(2):
                    product(t, 2 * t + 2, t + 1, 0)
                with dve.Fori(1, BLOCKS) as j:
                    product(0, j * 6, j * 6 - 3, j * 2 - 1)
                    add_output(j)
                    product(1, j * 6 + 4, j * 6 + 2, j * 2)
                add_output(BLOCKS)

            @block.gpsimd
            def _(pool):
                def lower(b, count):
                    pool.wait_ge(W.hi_ready, count)
                    nc.gpsimd.tensor_tensor(W.lo[:, b, :], W.raw[:, b, :], W.hi[:, b, :].bitcast(F32), ALU.subtract).then_inc(W.lo_ready, 1)

                def rest(t, count):
                    pool.wait_ge(h_hi, count)
                    nc.gpsimd.tensor_tensor(actL[:, t, :], act32[:, t, :], actH[:, t, :].bitcast(F32), ALU.subtract).then_inc(h_lo, 1)

                lower(0, 1)
                lower(1, 2)
                for t in range(2):
                    lower(0, 2 * t + 3)
                    lower(1, 2 * t + 4)
                    rest(t, t + 1)
                with pool.Fori(1, BLOCKS) as j:
                    for n in range(4):
                        lower(n % 2, j * 6 + (n + 1))
                    rest(0, j * 2 + 1)
                    for n in range(2):
                        lower(n % 2, j * 6 + (n + 5))
                    rest(1, j * 2 + 2)


def phase_final(g):
    nc = g.nc
    with ExitStack() as ctx:
        sb = lambda name, shape, dt=F32: ctx.enter_context(nc.sbuf_tensor(name, shape, dt))
        sem = lambda name: ctx.enter_context(nc.semaphore(name))
        XT = g.XT
        square = sb("square2", [P, 2, T])
        sumsq = sb("sumsq2", [P, T])
        rstd = sb("rstd2", [P, T])
        rows = sb("y_rows", [P, 2, D])
        zero, sq_ready, sq_added, stat_done, root_ready = sem("fin_zero"), sem("fin_sq"), sem("fin_sq_added"), sem("fin_stat"), sem("fin_root")
        rstd_ready, y_ready, turned, copied = sem("fin_rstd"), sem("y_ready"), sem("fin_turned"), sem("fin_copied")
        stored = (sem("y_stored0"), sem("y_stored1"))
        with nc.Block() as block:

            @block.sync
            def _(sp):
                for t in range(NT):
                    sp.wait_ge(copied, 2 * t + 2)
                    dst = g.d["y_sample"][t * P:(t + 1) * P, :] if t < LAT // P else g.d["y_prompt"][t * P - LAT:(t + 1) * P - LAT, :]
                    sp.dma_start(dst, rows[:, t % 2, :]).then_inc(stored[t % 2], 16)
                for b in range(2):
                    sp.wait_ge(stored[b], 16 * NT // 2)

            @block.tensor
            def _(pe):
                pe.wait_ge(sq_added, KD)
                for c, (c0, c1) in enumerate(CHUNKS):
                    mm = nc.tensor.matmul(g.ps_all[:, c, 0:c1 - c0], g.ones[:, :], sumsq[:, c0:c1], start=True, stop=True)
                mm.then_inc(stat_done, 1)
                pe.wait_ge(y_ready, KD)
                pe.wait_ge(root_ready, 2)
                for t in range(NT):
                    for h in range(2):
                        n = 2 * t + h
                        if n >= 8:
                            pe.wait_ge(copied, n - 7)
                        for f in range(4):
                            mm = nc.tensor.transpose(g.ps_all[:, n % 8, f * P:(f + 1) * P], XT[:, 4 * h + f, t * P:(t + 1) * P], g.ident[:, :])
                        mm.then_inc(turned, 1)

            @block.scalar
            def _(act):
                for m in range(KD):
                    if m >= 2:
                        act.wait_ge(sq_added, m - 1)
                    nc.scalar.activation(square[:, m % 2, :], XT[:, m, :], ACT.Square).then_inc(sq_ready, 1)
                act.wait_ge(stat_done, 1)
                root(g, act, rstd, root_ready)
                for n in range(2 * NT):
                    t = n // 2
                    act.wait_ge(turned, n + 1)
                    if t >= 2 and n % 2 == 0:
                        act.wait_ge(stored[t % 2], 16 * (t // 2))
                    nc.scalar.activation(rows[:, t % 2, (n % 2) * 512:(n % 2 + 1) * 512], g.ps_all[:, n % 8, :], ACT.Copy).then_inc(copied, 1)

            @block.vector
            def _(dve):
                dve.wait_ge(root_ready, 2)
                nc.vector.reciprocal(rstd[:, :], rstd[:, :]).then_inc(rstd_ready, 1)
                dve.wait_ge(rstd_ready, 1)
                for m in range(KD):
                    c = OFF["final_g"] + m
                    nc.vector.scalar_tensor_tensor(XT[:, m, :], XT[:, m, :], g.cols[:, c:c + 1], rstd[:, :], ALU.mult, ALU.mult).then_inc(y_ready, 1)

            @block.gpsimd
            def _(pool):
                nc.gpsimd.memset(sumsq[:, :], 0.0).then_inc(zero, 1)
                pool.wait_ge(zero, 1)
                for m in range(KD):
                    pool.wait_ge(sq_ready, m + 1)
                    if m:
                        pool.wait_ge(sq_added, m)
                    nc.gpsimd.tensor_tensor(sumsq[:, :], sumsq[:, :], square[:, m % 2, :], ALU.add).then_inc(sq_added, 1)


PHASES = (phase_input, phase_mixers, phase_attention, phase_merge, phase_output, phase_ffn, phase_final)


_OUTS = (("y_prompt", (CTX, D)), ("y_sample", (LAT, D)), ("new_k", (CTX, NAW)), ("new_v", (CTX, NAW)))
_SCRATCH = (("xT", (KD, P, T)), ("qT", (4, P, T)), ("kT", (4, P, T + PAST)), ("v", (T, NAW)),
            ("branch", (KD, P, T)), ("merged", (KD, P, T)))


def build(nc, arrays, phases=9, scratch_kind="Internal"):
    g = Ctx()
    g.nc = nc
    g.d = {n: nc.dram_tensor(n + "_dram", a.shape, F32, kind="ExternalInput").ap() for n, a in arrays.items()}
    for n, shape in _OUTS:
        g.d[n] = nc.dram_tensor(n + "_dram", shape, F32, kind="ExternalOutput").ap()
    for n, shape in _SCRATCH:
        g.d[n] = nc.dram_tensor(n + "_dram", shape, F32, kind=scratch_kind).ap()
    with ExitStack() as ctx:
        sb = lambda name, shape, dt=F32: ctx.enter_context(nc.sbuf_tensor(name, shape, dt))
        g.cols = sb("cols", [P, NCOLS])
        g.mod = sb("mod", [P, 6 * KD, 2])
        g.gain = sb("gain", [P, 2, KD, 2])
        g.cs = sb("silu_c", [P, 2 * KD])
        g.ident = sb("ident", [P, P])
        g.ones = sb("ones", [P, P])
        g.eps = sb("eps", [P, 1])
        g.AH = sb("AH", [P, KD, T], FR)
        g.AL = sb("AL", [P, KD, T], FR)
        g.ps_all = ctx.enter_context(nc.psum_tensor("ps_all", [P, 8, 512], F32))
        g.ps = g.ps_all[:, 0:6, :].rearrange("p (s c) n -> p s c n", s=2)
        g.aux = g.ps_all[:, 6:8, :]
        for n, phase in enumerate(PHASES):
            if n < phases:
                if phase is phase_output:
                    g.XT = sb("XT", [P, KD, T])
                phase(g)


def columns(v):
    return np.asarray(v).reshape(-1, P).T


def lay_out(i):
    both = np.stack([columns(i["c"][0]), columns(i["c_ctx"])], axis=2).reshape(P, 2 * KD)
    w_dw = np.asarray(i["w_dw"][0]).T.reshape(2, P, CONV_K).transpose(1, 0, 2).reshape(P, 2 * CONV_K)
    packed = [both] + [columns(v) for v in (i["b_mod"][0], i["norm1_g"][0], i["norm2_g"][0], i["final_g"], i["b_gate"][0],
                                            i["pool_scale"][0], i["b_dw"][0], i["conv_norm_g"][0], i["conv_norm_b"][0])] + [w_dw]
    rpb = np.zeros((HEADS, 2 * KH - 1, 2 * GW - 1), np.float32)
    side = GW - KW
    rpb[:, :, side:side + 2 * KW - 1] = np.asarray(i["rpb"][0])[:, :, ::-1]
    start = np.clip(np.arange(GW) - KW // 2, 0, GW - KW)
    inside = (np.arange(GW)[None] >= start[:, None]) & (np.arange(GW)[None] < start[:, None] + KW)
    inv = []
    for w in (2, 4, 8, 16):
        row = []
        for n in (LAT, CTX):
            t = np.arange(n)
            row.append(1.0 / (np.clip(t - w // 2 + w, 0, n) - np.clip(t - w // 2, 0, n)))
        inv.append(np.concatenate(row))
    a = {
        "cols": np.ascontiguousarray(np.concatenate(packed, axis=1)),
        "ident": np.eye(P, dtype=np.float32),
        "col_mask": np.tile(np.where(inside, 0.0, NEG), (2, 1)).astype(np.float32),
        "inv_count": np.stack(inv).astype(np.float32),
        "rpb": rpb,
        "x_prompt": np.asarray(i["x_prompt"][0]), "x_sample": np.asarray(i["x_sample"][0]),
        "cache_k": np.asarray(i["cache_k"][0, 0]).reshape(PAST, NAW), "cache_v": np.asarray(i["cache_v"][0, 0]).reshape(PAST, NAW),
    }
    for n in ("w_mod", "w_in", "w_oa", "w_pool", "w_ob", "w_oc", "w_out", "w_gu", "w_down"):
        a[n] = np.asarray(i[n][0])
    return a


def kernel(**inputs):
    import concourse.bacc as bacc
    from concourse.bass_utils import run_bass_kernel_spmd

    arrays = lay_out(inputs)
    nc = bacc.Bacc("TRN2", target_bir_lowering=False, num_devices=1)
    build(nc, arrays)
    r = run_bass_kernel_spmd(nc, [{n + "_dram": a for n, a in arrays.items()}], core_ids=[0]).results[0]
    shape = (1, 1, CTX, HEADS, DH)
    return (r["y_prompt_dram"].reshape(1, CTX, D), r["y_sample_dram"].reshape(1, LAT, D),
            r["new_k_dram"].reshape(shape), r["new_v_dram"].reshape(shape))
```

```python
from contextlib import ExitStack

import numpy as np
import concourse.bass as bass
from concourse import mybir

F32 = mybir.dt.float32
FR = mybir.dt.float32r
ACT = mybir.ActivationFunctionType
ALU = mybir.AluOpType
AX = mybir.AxisListType.X

P = 128
D = 1024
KD = D // P
LAT, CTX, PAST = 1024, 256, 256
T = LAT + CTX
NT = T // P
CHUNKS = ((0, 448), (448, 896), (896, 1280))
C2 = LAT - CHUNKS[2][0]
HEADS, DH = 8, 64
NAW = HEADS * DH
KH, KW, GW = 8, 16, 64
ROWS = LAT // GW
PW = CW = D // 4
CONV_K = 31
HALF = CONV_K // 2
HID = 2816
BLOCKS = HID // (2 * P)
EPS = 1e-6
NEG = -1e30
N_IN = 3 * NAW + PW + 2 * CW + 3 * D
P_COL, A_COL, G_COL, GATE_COL = 3 * NAW, 3 * NAW + PW, 3 * NAW + PW + CW, 3 * NAW + PW + 2 * CW
OFF = {}
_at = 0
for _name, _n in (("c", 2 * KD), ("b_mod", 6 * KD), ("norm1_g", KD), ("norm2_g", KD), ("b_gate", 3 * KD),
                  ("pool_scale", 2), ("b_dw", 2), ("cn_g", 2), ("cn_b", 2), ("w_dw", 2 * CONV_K)):
    OFF[_name] = _at
    _at += _n
NCOLS = _at
CB = HALF + LAT + HALF + CTX + HALF
CV = LAT + HALF + CTX
CCTX = LAT + HALF
PB = 8 + LAT + 16 + CTX + 8
PCTX = 8 + LAT + 16
SLOTS = 14
WIN = 10


class Ctx:
    pass


def chunk_views(ps, sbuf_row):
    n = CHUNKS[0][1]
    return ((ps[:, 0:2, 0:n], sbuf_row[:, 0:2 * n].rearrange("p (c n) -> p c n", c=2)),
            (ps[:, 2, 0:T - 2 * n], sbuf_row[:, 2 * n:T]))


def gemm(nc, ps, wh, wl, ah, al, ktiles, first=True, last=True):
    for n, (w0, k) in enumerate(ktiles):
        for part, (w, a) in enumerate(((wh, ah), (wh, al), (wl, ah))):
            for c, (c0, c1) in enumerate(CHUNKS):
                mm = nc.tensor.matmul(ps[:, c, 0:c1 - c0], w[:, w0:w0 + P], a[:, k, c0:c1],
                                      start=(first and n == 0 and part == 0),
                                      stop=(last and n == len(ktiles) - 1 and part == 2))
    return mm


def phase_input(g):
    nc = g.nc
    with ExitStack() as ctx:
        sb = lambda name, shape, dt=F32: ctx.enter_context(nc.sbuf_tensor(name, shape, dt))
        sem = lambda name: ctx.enter_context(nc.semaphore(name))
        XT = sb("XT0", [P, KD, T])
        x_rows = sb("x_rows", [P, NT, D])
        w_mod_sb = sb("w_mod_sb", [P, 4, KD * P])
        square = sb("square0", [P, 2, 512])
        sumsq = sb("sumsq0", [P, T])
        rstd = sb("rstd0", [P, T])
        normed = sb("normed0", [P, 2, T])
        const_in, x_in0, x_in1, x_in2 = sem("const_in"), sem("x_in0"), sem("x_in1"), sem("x_in2")
        x_in = (x_in0, x_in1, x_in2)
        w_in = [sem(f"wmod_in{b}") for b in range(4)]
        w_used, mod_done, mod_ready = sem("wmod_used"), sem("mod_done"), sem("mod_ready")
        ones_ready, silu_ready, turned, xt_ready = sem("ones_ready"), sem("silu_ready"), sem("turned"), sem("xt_ready")
        sq_ready, sq_added, stat_done, root_ready = sem("sq_ready"), sem("sq_added"), sem("stat_done"), sem("root_ready")
        rstd_ready, scaled, t_ready, ah_ready, al_ready = (sem("rstd_ready"), sem("scaled"), sem("t_ready"),
                                                           sem("ah_ready"), sem("al_ready"))
        acc_zero, mod_step, spilled = sem("acc_zero"), sem("mod_step"), sem("spilled")
        groups = [(0, 4), (4, 8), (8, 10)]
        banks = [g.ps[:, n // 3, n % 3, :] for n in range(6)]
        EARLY = 2 * KD
        FRONT = KD
        with nc.Block() as block:

            @block.sync
            def _(sp):
                sp.dma_start(g.cols[:, :], g.d["cols"]).then_inc(const_in, 16)
                sp.dma_start(g.ident[:, :], g.d["ident"]).then_inc(const_in, 16)
                for n, (a, b) in enumerate(groups[:2]):
                    sp.dma_start(x_rows[:, a:b, :], g.d["x_sample"][a * P:b * P, :].rearrange("(t p) n -> p t n", p=P)).then_inc(x_in[n], 16)
                sp.dma_start(x_rows[:, 8:10, :], g.d["x_prompt"].rearrange("(t p) n -> p t n", p=P)).then_inc(x_in[2], 16)
                wv = g.d["w_mod"].rearrange("(k p) n -> p k n", p=P)

                def load(b, col):
                    sp.dma_start(w_mod_sb[:, b, :].rearrange("p (k n) -> p k n", k=KD), wv[:, :, bass.ds(col, P)]).then_inc(w_in[b], 16)

                for b in range(4):
                    load(b, b * P)
                with sp.Fori(1, (EARLY + KD) // 4) as i:
                    for b in range(4):
                        sp.wait_ge(w_used, i * 4 + (b - 3))
                        load(b, i * (4 * P) + b * P)
                sp.wait_ge(spilled, 16)

            @block.tensor
            def _(pe):
                pe.wait_ge(const_in, 32)
                for n in range(24):
                    gi, f = n // KD, n % KD
                    a, b = groups[gi]
                    if f == 0:
                        pe.wait_ge(x_in[gi], 16)
                    if n >= 6:
                        pe.wait_ge(xt_ready, n - 5)
                    for t in range(a, b):
                        mm = nc.tensor.transpose(banks[n % 6][:, (t - a) * P:(t - a + 1) * P],
                                                 x_rows[:, t, f * P:(f + 1) * P], g.ident[:, :])
                    mm.then_inc(turned, 1)
                pe.wait_ge(silu_ready, 1)

                def modulation(bank, first, tiles):
                    with pe.Fori(0, tiles // 4) as i:
                        for b in range(4):
                            pe.wait_ge(w_in[b], i * 16 + (16 + 4 * (bank * EARLY + first)))
                            for k in range(KD):
                                mm = nc.tensor.matmul(g.aux[:, bank, bass.ds(i * 8 + (first + b) * 2, 2)], w_mod_sb[:, b, k * P:(k + 1) * P],
                                                      g.cs[:, 2 * k:2 * k + 2], start=(k == 0), stop=(k == KD - 1))
                            mm.then_inc(w_used, 1)

                modulation(0, 0, FRONT)
                pe.wait_ge(xt_ready, 24)
                pe.wait_ge(sq_added, 24)
                pe.wait_ge(ones_ready, 1)
                for c, (c0, c1) in enumerate(CHUNKS):
                    mm = nc.tensor.matmul(g.ps[:, 0, c, 0:c1 - c0], g.ones[:, :], sumsq[:, c0:c1], start=True, stop=True)
                mm.then_inc(stat_done, 1)
                modulation(0, FRONT, EARLY - FRONT)
                modulation(1, 0, KD)

            @block.scalar
            def _(act):
                act.wait_ge(const_in, 32)
                nc.scalar.activation(g.cs[:, :], g.cols[:, 0:2 * KD], ACT.Silu).then_inc(silu_ready, 1)
                for n in range(24):
                    gi, f = n // KD, n % KD
                    t0, t1 = groups[gi][0] * P, groups[gi][1] * P
                    act.wait_ge(xt_ready, n + 1)
                    if n >= 2:
                        act.wait_ge(sq_added, n - 1)
                    nc.scalar.activation(square[:, n % 2, 0:t1 - t0], XT[:, f, t0:t1], ACT.Square).then_inc(sq_ready, 1)
                act.wait_ge(xt_ready, 24)
                act.dma_start(g.d["xT"].rearrange("k p t -> p k t"), XT[:, :, :]).then_inc(spilled, 16)
                act.wait_ge(stat_done, 1)
                root(g, act, rstd, root_ready)
                copies(g, act, normed, t_ready, ah_ready)

            @block.vector
            def _(dve):
                nc.vector.memset(g.ones[:, :], 1.0)
                nc.vector.memset(g.eps[:, :], EPS).then_inc(ones_ready, 1)
                for n in range(24):
                    gi, f = n // KD, n % KD
                    t0, t1 = groups[gi][0] * P, groups[gi][1] * P
                    dve.wait_ge(turned, n + 1)
                    nc.vector.tensor_copy(XT[:, f, t0:t1], banks[n % 6][:, 0:t1 - t0]).then_inc(xt_ready, 1)
                dve.wait_ge(root_ready, 2)
                nc.vector.reciprocal(rstd[:, :], rstd[:, :]).then_inc(rstd_ready, 1)
                dve.wait_ge(rstd_ready, 1)
                dve.wait_ge(w_used, EARLY)
                mod_bias(g, 0, 2, g.aux[:, 0, 0:2 * EARLY], mod_step)
                dve.wait_ge(mod_step, 1)
                mod_gain(g, 0, "norm1_g", 1, mod_step)
                dve.wait_ge(mod_step, 2)
                scale_shift(g, dve, XT, rstd, normed, 0, 0, scaled, t_ready, al_ready)
                dve.wait_ge(w_used, EARLY + KD)
                mod_bias(g, 2, 3, g.aux[:, 1, 0:2 * KD], mod_step)

            @block.gpsimd
            def _(pool):
                nc.gpsimd.memset(sumsq[:, :], 0.0).then_inc(acc_zero, 1)
                pool.wait_ge(acc_zero, 1)
                for n in range(24):
                    t0, t1 = groups[n // KD][0] * P, groups[n // KD][1] * P
                    pool.wait_ge(sq_ready, n + 1)
                    if n:
                        pool.wait_ge(sq_added, n)
                    nc.gpsimd.tensor_tensor(sumsq[:, t0:t1], sumsq[:, t0:t1], square[:, n % 2, 0:t1 - t0], ALU.add).then_inc(sq_added, 1)
                rests(g, pool, normed, ah_ready, al_ready)


def mod_bias(g, a, b, source, done):
    bm = g.cols[:, OFF["b_mod"] + a * KD:OFF["b_mod"] + b * KD]
    g.nc.vector.tensor_tensor(g.mod[:, a * KD:b * KD, :], source.rearrange("p (m j) -> p m j", j=2),
                              bm.rearrange("p (m j) -> p m j", j=1).broadcast_to([P, (b - a) * KD, 2]), ALU.add).then_inc(done, 1)


def mod_gain(g, n, gain, part, done):
    gv = g.cols[:, OFF[gain]:OFF[gain] + KD].rearrange("p (m j) -> p m j", j=1).broadcast_to([P, KD, 2])
    g.nc.vector.scalar_tensor_tensor(g.gain[:, n, :, :], g.mod[:, part * KD:(part + 1) * KD, :], 1.0, gv,
                                     ALU.add, ALU.mult).then_inc(done, 1)


def root(g, act, rstd, root_ready):
    for ps, sb in chunk_views(g.ps[:, 0], rstd):
        g.nc.scalar.activation(sb, ps, ACT.Sqrt, bias=g.eps[:, 0:1], scale=1.0 / D).then_inc(root_ready, 1)


def scale_shift(g, dve, XT, rstd, normed, gain, shift_part, scaled, t_ready, al_ready):
    for f in range(KD):
        if f >= 2:
            dve.wait_ge(al_ready, f - 1)
        nc = g.nc
        nc.vector.tensor_tensor(normed[:, f % 2, :], XT[:, f, :], rstd[:, :], ALU.mult).then_inc(scaled, 1)
        dve.wait_ge(scaled, f + 1)
        for j, (a, b) in enumerate(((0, LAT), (LAT, T))):
            nc.vector.tensor_scalar(normed[:, f % 2, a:b], normed[:, f % 2, a:b], g.gain[:, gain, f, j:j + 1],
                                    g.mod[:, shift_part * KD + f, j:j + 1], ALU.mult, ALU.add).then_inc(t_ready, 1)


def copies(g, act, normed, t_ready, ah_ready):
    for f in range(KD):
        act.wait_ge(t_ready, 2 * (f + 1))
        g.nc.scalar.activation(g.AH[:, f, :], normed[:, f % 2, :], ACT.Copy).then_inc(ah_ready, 1)


def rests(g, pool, normed, ah_ready, al_ready):
    for f in range(KD):
        pool.wait_ge(ah_ready, f + 1)
        g.nc.gpsimd.tensor_tensor(g.AL[:, f, :], normed[:, f % 2, :], g.AH[:, f, :].bitcast(F32), ALU.subtract).then_inc(al_ready, 1)


class Weights:

    def __init__(self, g, ctx, tag):
        nc = g.nc
        self.g = g
        self.raw = ctx.enter_context(nc.sbuf_tensor(f"w_raw{tag}", [P, 2, KD * P], F32))
        self.hi = ctx.enter_context(nc.sbuf_tensor(f"w_hi{tag}", [P, 2, KD * P], FR))
        self.lo = ctx.enter_context(nc.sbuf_tensor(f"w_lo{tag}", [P, 2, KD * P], FR))
        self.raw_in = [ctx.enter_context(nc.semaphore(f"w_raw_in{b}{tag}")) for b in range(2)]
        self.hi_ready = ctx.enter_context(nc.semaphore(f"w_hi_ready{tag}"))
        self.lo_ready = ctx.enter_context(nc.semaphore(f"w_lo_ready{tag}"))
        self.used = ctx.enter_context(nc.semaphore(f"w_used{tag}"))

    def columns(self, slot, width):
        return self.raw[:, slot, :].rearrange("p (k n) -> p k n", n=width)


PIECES = ((0, 0, 448, 0), (1, 0, 448, 448), (2, 0, C2, 896), (2, C2, CTX, LAT))


def padded(tok, lead, ctx_at):
    return lead + tok if tok < LAT else ctx_at


def phase_mixers(g):
    nc = g.nc
    with ExitStack() as ctx:
        sb = lambda name, shape, dt=F32: ctx.enter_context(nc.sbuf_tensor(name, shape, dt))
        sem = lambda name: ctx.enter_context(nc.semaphore(name))
        W = Weights(g, ctx, "m")
        glu = sb("glu", [P, 2, CB])
        ppad = sb("pool_in", [P, 2, PB])
        summed = sb("summed", [P, 2, PB])
        conv = sb("conv", [P, 2, CV])
        sig = sb("sig", [P, T])
        square = sb("ln_square", [P, T])
        evac = sb("evac", [P, 2, T])
        vt = sb("vt", [P, NT, P])
        kt_ctx = sb("kt_ctx", [P, 2, P])
        cached_k = vt[:, 0:8, :].rearrange("p (t a) n -> p t (a n)", t=2)
        cached_kT = sb("cached_kT", [P, 4, PAST])
        wp = sb("wp", [P, 2, P])
        inv = sb("inv", [P, T])
        w_mod_sb = sb("w_mod_late", [P, 2, KD * 2 * P])
        mod_acc = sb("mod_acc", [P, 2, 2, 2 * P])
        free = (sem("set_free0"), sem("set_free1"))
        done = sem("small_products_done")
        ck_in, inv_in, inv_used, zeroed, wp_in = sem("ck_in"), sem("inv_in"), sem("inv_used"), sem("zeroed"), sem("wp_in")
        ck_turned, ck_out = sem("ck_turned"), sem("ck_out")
        pool_step, pooled, branch_ready = sem("pool_step"), sem("pooled"), sem("pool_branch_ready")
        glu_ready, conv_step = sem("glu_ready"), sem("conv_step")
        centred, sq_ready, root_ready, ln_step, silu_ready = sem("centred"), sem("ln_sq"), sem("ln_root"), sem("ln_step"), sem("ln_silu")
        turned, tok_ready = sem("kv_turned"), sem("kv_token_major")
        stored = (sem("evac_stored0"), sem("evac_stored1"))
        tok_stored, ck_stored, branch_stored = sem("tok_stored"), sem("ck_stored"), sem("mixer_branches_stored")
        mod_in = (sem("late_wmod_in0"), sem("late_wmod_in1"))
        acc_step, mod_used, mod_out, mod_step = sem("mod_acc_step"), sem("mod_acc_used"), sem("late_mod_out"), sem("late_mod_step")
        wv = g.d["w_in"].rearrange("(k p) n -> p k n", p=P)
        wmv = g.d["w_mod"].rearrange("(k p) n -> p k n", p=P)
        FIRST = [G_COL, A_COL, G_COL + P, A_COL + P, P_COL, P_COL + P]
        U_Q, U_K, U_V, UNITS = 6, 10, 14, 18
        NG = 3 * D // (2 * P)
        STEPS = 2 * KD
        modp = g.aux[:, 1, 0:2 * 3 * KD]
        USE_Q, USE_K, USE_V, USE_POOL = 3, (5, 5), 8, 10

        with nc.Block() as block:

            @block.sync
            def _(sp):
                def load(b, col):
                    sp.dma_start(W.columns(b, P), wv[:, :, bass.ds(col, P)]).then_inc(W.raw_in[b], 16)

                def load_mod(n):
                    if n >= 2:
                        sp.wait_ge(acc_step, STEPS * (n - 1))
                    sp.dma_start(w_mod_sb[:, n % 2, :].rearrange("p (k n) -> p k n", k=KD),
                                 wmv[:, :, 3 * D + n * 2 * P:3 * D + (n + 1) * 2 * P]).then_inc(mod_in[n % 2], 16)

                def store(b, dst, use):
                    sp.wait_ge(free[b], use)
                    sp.dma_start(dst.rearrange("a p t -> p (a t)"), evac[:, b, :]).then_inc(stored[b], 16)

                def load_inv(t):
                    for half in range(2):
                        sp.dma_start(inv[half * 64:(half + 1) * 64, :],
                                     g.d["inv_count"][2 * t + half:2 * t + half + 1, :].broadcast_to([64, T])).then_inc(inv_in, 16)

                load(0, FIRST[0])
                load(1, FIRST[1])
                sp.dma_start(cached_k, g.d["cache_k"].rearrange("(t p) n -> p t n", p=P)).then_inc(ck_in, 16)
                load_mod(0)
                load_mod(1)
                load_inv(0)
                sp.wait_ge(zeroed, 2)
                for q in range(4):
                    r = 64 * (q % 2)
                    sp.dma_start(wp[r:r + 64, q // 2, r:r + 64], g.d["w_pool"][q, :, :]).then_inc(wp_in, 16)
                for u in range(2, U_Q + 2):
                    sp.wait_ge(W.lo_ready, u - 1)
                    load(u % 2, FIRST[u] if u < U_Q else (u - U_Q) * P)
                    if u in (3, 4, 5):
                        load_mod(2 * u - 4)
                        load_mod(2 * u - 3)
                    if u == 3:
                        sp.wait_ge(ck_out, 2)
                        sp.dma_start(g.d["kT"][:, :, T:T + PAST].rearrange("a p t -> p a t"), cached_kT[:, :, :]).then_inc(ck_stored, 16)
                for i in range(2):
                    for b in range(2):
                        sp.wait_ge(W.lo_ready, U_Q + 2 * i + b + 1)
                        load(b, (2 * i + 2 + b) * P)
                    for b in range(2):
                        store(b, g.d["qT"][2 * i + b:2 * i + b + 1, :, :], USE_Q + i + 1)
                for i in range(2):
                    for b in range(2):
                        sp.wait_ge(W.lo_ready, U_K + 2 * i + b + 1)
                        load(b, (6 + 2 * i + b) * P)
                    for b in range(2):
                        load_mod(8 + 2 * i + b)
                    for b in range(2):
                        store(b, g.d["kT"][2 * i + b:2 * i + b + 1, :, 0:T], USE_K[b] + 1 + (i if b else 2 * i))
                    for b in range(2):
                        col = (2 * i + b) * P
                        sp.wait_ge(tok_ready, 2 * i + b + 2)
                        sp.dma_start(g.d["new_k"][:, col:col + P].rearrange("(t p) n -> p t n", p=P),
                                     kt_ctx[:, :, :]).then_inc(tok_stored, 16)
                for b in range(2):
                    sp.wait_ge(W.lo_ready, UNITS - 2 + b - 1)
                    load(b, (10 + b) * P)
                sp.wait_ge(inv_used, 2)
                load_inv(1)
                for i in range(2):
                    for b in range(2):
                        col = (2 * i + b) * P
                        sp.wait_ge(tok_ready, 6 * i + 5 + 3 * b + 3)
                        sp.dma_start(g.d["v"][:, col:col + P].rearrange("(t p) n -> p t n", p=P), vt[:, :, :]).then_inc(tok_stored, 16)
                        sp.dma_start(g.d["new_v"][:, col:col + P].rearrange("(t p) n -> p t n", p=P), vt[:, 8:10, :]).then_inc(tok_stored, 16)
                    if i == 0:
                        for t in range(2):
                            for part, (a, b, at) in enumerate(((0, LAT, 0), (LAT, T, CCTX))):
                                sp.wait_ge(silu_ready, 2 * t + part + 1)
                                sp.dma_start(g.d["branch"][6 + t, :, a:b], conv[:, t, at:at + b - a]).then_inc(branch_stored, 16)
                for t in range(2):
                    sp.wait_ge(branch_ready, t + 1)
                    sp.dma_start(g.d["branch"][4 + t, :, :], ppad[:, t, 0:T]).then_inc(branch_stored, 16)
                sp.wait_ge(ck_stored, 16)
                sp.wait_ge(tok_stored, 16 * 12)
                sp.wait_ge(branch_stored, 16 * 6)
                for b in range(2):
                    sp.wait_ge(stored[b], 16 * 4)

            @block.tensor
            def _(pe):
                pe.wait_ge(ck_in, 16)
                for hp in range(4):
                    for t in range(2):
                        mm = nc.tensor.transpose(g.aux[:, hp // 2, (hp % 2) * 256 + t * P:(hp % 2) * 256 + (t + 1) * P],
                                                 cached_k[:, t, hp * P:(hp + 1) * P], g.ident[:, :])
                mm.then_inc(ck_turned, 1)

                def unit(s, w_count, uses):
                    pe.wait_ge(W.lo_ready, w_count)
                    pe.wait_ge(free[s], uses)
                    gemm(nc, g.ps[:, s], W.hi[:, s, :], W.lo[:, s, :], g.AH, g.AL,
                         [(k * P, k) for k in range(KD)]).then_inc(W.used, 1)

                def modulation(n):
                    pe.wait_ge(acc_step, STEPS * (n + 1))
                    for m in range(2):
                        for j in range(2):
                            c = 4 * n + 2 * m + j
                            mm = nc.tensor.matmul(modp[:, c:c + 1], mod_acc[:, n % 2, j, m * P:(m + 1) * P],
                                                  g.ones[:, 0:1], start=True, stop=True)
                    mm.then_inc(mod_used, 1)

                def channel_sums(s, tiles):
                    for bank, c0, n, tok in PIECES:
                        for t, (x, ctx_at) in enumerate(tiles):
                            at = padded(tok, 0, ctx_at)
                            mm = nc.tensor.matmul(g.ps[:, s, bank, c0:c0 + n], g.ones[:, :], x[:, at:at + n], start=(t == 0), stop=(t == 1))
                    mm.then_inc(done, 1)

                for u in range(U_Q):
                    unit(u % 2, u + 1, u // 2)
                    if u == 2:
                        pe.wait_ge(ck_out, 2)
                    if u in (2, 3, 5):
                        n = {2: 0, 3: 2, 5: 4}[u]
                        modulation(n)
                        modulation(n + 1)
                with pe.Fori(0, 2) as i:
                    for s in range(2):
                        unit(s, i * 2 + (U_Q + s + 1), i + USE_Q)
                for i in range(2):
                    for s in range(2):
                        unit(s, i * 2 + (U_K + s + 1), USE_K[s] + (i if s else 2 * i))
                        if i == 0 and s == 1:
                            pe.wait_ge(conv_step, 2 * CONV_K)
                            pe.wait_ge(free[0], USE_K[0] + 1)
                            channel_sums(0, [(conv[:, t, :], CCTX) for t in range(2)])
                        if i or s:
                            n = 4 + 2 * (2 * i + s)
                            modulation(n)
                            modulation(n + 1)
                    for s in range(2):
                        pe.wait_ge(free[s], USE_K[s] + 1 + (i if s else 2 * i))
                        pe.wait_ge(tok_ready, i * 2 + (s + 1))
                        for t in range(2):
                            mm = nc.tensor.transpose(g.aux[:, 0, t * P:(t + 1) * P], evac[:, s, LAT + t * P:LAT + (t + 1) * P], g.ident[:, :])
                        mm.then_inc(turned, 1)
                pe.wait_ge(sq_ready, 2)
                channel_sums(1, [(sig, LAT), (square, LAT)])
                pe.wait_ge(mod_out, 1)
                with pe.Fori(0, 2) as i:
                    for s in range(2):
                        unit(s, i * 2 + (U_V + s + 1), i + USE_V)
                    for s in range(2):
                        pe.wait_ge(free[s], i + (USE_V + 1))
                        for part, (a, b) in enumerate(V_PARTS):
                            pe.wait_ge(tok_ready, i * 6 + (5 + 3 * s + (1 if part == 2 else 0)))
                            for t in range(a, b):
                                mm = nc.tensor.transpose(g.aux[:, part % 2, (t - a) * P:(t - a + 1) * P], evac[:, s, t * P:(t + 1) * P], g.ident[:, :])
                            mm.then_inc(turned, 1)
                pe.wait_ge(wp_in, 64)
                pe.wait_ge(pooled, 2)
                for t in range(2):
                    pe.wait_ge(free[t], USE_POOL)
                    for bank, c0, n, tok in PIECES:
                        at = padded(tok, 8, PCTX)
                        mm = nc.tensor.matmul(g.ps[:, t, bank, c0:c0 + n], wp[:, t, :], summed[:, t, at:at + n], start=True, stop=True)
                    mm.then_inc(done, 1)

            @block.scalar
            def _(act):
                def split(slot, raw_count, used=None):
                    act.wait_ge(W.raw_in[slot], raw_count)
                    if used is not None:
                        act.wait_ge(W.used, used)
                    nc.scalar.activation(W.hi[:, slot, :], W.raw[:, slot, :], ACT.Copy).then_inc(W.hi_ready, 1)

                def copy_out(s):
                    for ps, out in chunk_views(g.ps[:, s], evac[:, s, :]):
                        last = nc.scalar.activation(out, ps, ACT.Copy)
                    last.then_inc(free[s], 1)

                act.sem_inc(tok_ready, 1)
                split(0, 16)
                split(1, 16)
                act.wait_ge(ck_turned, 1)
                for h in range(2):
                    nc.scalar.activation(cached_kT[:, 2 * h:2 * h + 2, :], g.aux[:, h, :].rearrange("p (a t) -> p a t", a=2), ACT.Copy).then_inc(ck_out, 1)
                act.wait_ge(zeroed, 1)
                for u in range(U_Q):
                    if u in (0, 2):
                        act.wait_ge(W.used, u + 1)
                        if u == 2:
                            act.wait_ge(glu_ready, 1)
                        for ps, out in chunk_views(g.ps[:, 0], sig):
                            last = nc.scalar.activation(out, ps, ACT.Sigmoid)
                        last.then_inc(free[0], 1)
                    elif u in (4, 5):
                        act.wait_ge(W.used, u + 1)
                        for bank, c0, n, tok in PIECES:
                            at = padded(tok, 8, PCTX)
                            last = nc.scalar.activation(ppad[:, u - 4, at:at + n], g.ps[:, u % 2, bank, c0:c0 + n], ACT.Copy)
                        last.then_inc(free[u % 2], 1)
                    split(u % 2, 16 * (u // 2 + 2), u + 1)
                for i in range(2):
                    for s in range(2):
                        act.wait_ge(W.used, 2 * i + U_Q + s + 1)
                        if i:
                            act.wait_ge(stored[s], 16 * i)
                        copy_out(s)
                        split(s, 16 * (i + U_Q // 2 + 2), 2 * i + U_Q + s + 1)
                for i in range(2):
                    for s in range(2):
                        act.wait_ge(W.used, 2 * i + U_K + s + 1)
                        act.wait_ge(stored[s], 16 * i + 32)
                        if i:
                            act.wait_ge(turned, 2 * i)
                        copy_out(s)
                        split(s, 16 * (i + U_K // 2 + 2), 2 * i + U_K + s + 1)
                    for s in range(2):
                        act.wait_ge(turned, 2 * i + s + 1)
                        if i or s:
                            act.wait_ge(tok_stored, 32 * i + 16 * s)
                        nc.scalar.activation(kt_ctx[:, :, :], g.aux[:, 0, 0:256].rearrange("p (t n) -> p t n", t=2), ACT.Copy).then_inc(tok_ready, 1)
                    if i == 0:
                        act.wait_ge(centred, 6)
                        for t, x in enumerate((sig, square)):
                            for a, b, at in ((0, LAT, 0), (LAT, T, CCTX)):
                                last = nc.scalar.activation(x[:, a:b], conv[:, t, at:at + b - a], ACT.Square)
                            last.then_inc(sq_ready, 1)
                act.wait_ge(mod_used, NG)
                nc.scalar.activation(g.mod[:, 3 * KD:6 * KD, :], modp.rearrange("p (m j) -> p m j", j=2), ACT.Copy).then_inc(mod_out, 1)
                act.wait_ge(done, 2)
                for ps, out in chunk_views(g.ps[:, 1], sig):
                    last = nc.scalar.activation(out, ps, ACT.Sqrt, bias=g.eps[:, 0:1], scale=1.0 / CW)
                last.then_inc(free[1], 1)
                for i in range(2):
                    for s in range(2):
                        act.wait_ge(W.used, 2 * i + U_V + s + 1)
                        act.wait_ge(stored[s], 16 * 4)
                        act.wait_ge(turned, 4 + 6 * i)
                        copy_out(s)
                        if i == 0:
                            split(s, 16 * (U_V // 2 + 2), U_V + s + 1)
                    for s in range(2):
                        for part, (a, b) in enumerate(V_PARTS):
                            act.wait_ge(turned, 4 + 6 * i + 3 * s + part + 1)
                            if part == 0:
                                act.wait_ge(tok_stored, 64 + 64 * i + 32 * s)
                            nc.scalar.activation(vt[:, a:b, :], g.aux[:, part % 2, 0:(b - a) * P].rearrange("p (t n) -> p t n", n=P), ACT.Copy).then_inc(tok_ready, 1)
                    if i == 0:
                        for t in range(2):
                            act.wait_ge(ln_step, 1 + 2 * (t + 1))
                            for n, at in ((LAT, 0), (CTX, CCTX)):
                                x = conv[:, t, at:at + n]
                                nc.scalar.activation(x, x, ACT.Silu, bias=g.cols[:, OFF["cn_b"] + t:OFF["cn_b"] + t + 1],
                                                     scale=g.cols[:, OFF["cn_g"] + t:OFF["cn_g"] + t + 1]).then_inc(silu_ready, 1)
                for t in range(2):
                    act.wait_ge(done, t + 3)
                    for ps, out in chunk_views(g.ps[:, t], ppad[:, t, 0:T]):
                        last = nc.scalar.activation(out, ps, ACT.Copy, scale=g.cols[:, OFF["pool_scale"] + t:OFF["pool_scale"] + t + 1])
                    last.then_inc(branch_ready, 1)

            @block.gpsimd
            def _(pool):
                with pool.Fori(0, UNITS // 2) as i:
                    for b in range(2):
                        pool.wait_ge(W.hi_ready, i * 2 + (b + 1))
                        nc.gpsimd.tensor_tensor(W.lo[:, b, :], W.raw[:, b, :], W.hi[:, b, :].bitcast(F32), ALU.subtract).then_inc(W.lo_ready, 1)

            @block.vector
            def _(dve):
                nc.vector.memset(ppad[:, :, :], 0.0).then_inc(zeroed, 1)
                nc.vector.memset(wp[:, :, :], 0.0).then_inc(zeroed, 1)
                for a in (0, HALF + LAT, CB - HALF):
                    nc.vector.memset(glu[:, :, a:a + HALF], 0.0)

                def modulation(first, last):
                    for n in range(first, last):
                        b = n % 2
                        dve.wait_ge(mod_in[b], 16 * (n // 2 + 1))
                        if n >= 2:
                            dve.wait_ge(mod_used, n - 1)
                        for k in range(KD):
                            for j in range(2):
                                w, c, acc = w_mod_sb[:, b, k * 2 * P:(k + 1) * 2 * P], g.cs[:, 2 * k + j:2 * k + j + 1], mod_acc[:, b, j, :]
                                if k == 0:
                                    nc.vector.tensor_scalar(acc, w, c, None, ALU.mult).then_inc(acc_step, 1)
                                else:
                                    dve.wait_ge(acc_step, STEPS * n + 2 * k + j - 1)
                                    nc.vector.scalar_tensor_tensor(acc, w, c, acc, ALU.mult, ALU.add).then_inc(acc_step, 1)

                modulation(0, 2)
                for t in range(2):
                    dve.wait_ge(W.used, 2 + 2 * t)
                    dve.wait_ge(free[0], t + 1)
                    for bank, c0, n, tok in PIECES:
                        at = padded(tok, HALF, HALF + LAT + HALF)
                        last = nc.vector.tensor_tensor(glu[:, t, at:at + n], g.ps[:, 1, bank, c0:c0 + n], sig[:, tok:tok + n], ALU.mult)
                    last.then_inc(free[1], 1)
                    dve.wait_ge(free[1], t + 1)
                    dve.sem_inc(glu_ready, 1)
                    if t == 0:
                        modulation(2, 4)
                modulation(4, 6)
                wd, bd = OFF["w_dw"], OFF["b_dw"]
                for t in range(2):
                    nc.vector.tensor_scalar(conv[:, t, :], glu[:, t, 0:CV], g.cols[:, wd + t * CONV_K:wd + t * CONV_K + 1],
                                            g.cols[:, bd + t:bd + t + 1], ALU.mult, ALU.add).then_inc(conv_step, 1)
                with dve.Fori(1, CONV_K) as k:
                    for t in range(2):
                        dve.wait_ge(conv_step, k * 2 + (t - 1))
                        nc.vector.scalar_tensor_tensor(conv[:, t, :], glu[:, t, bass.ds(k, CV)], g.cols[:, bass.ds(k + (wd + t * CONV_K), 1)],
                                                       conv[:, t, :], ALU.mult, ALU.add).then_inc(conv_step, 1)
                modulation(6, 8)
                dve.wait_ge(done, 1)
                for t in range(2):
                    w = conv[:, t, :]
                    for ps, x in ((g.ps[:, 0, 0:2, 0:448], w[:, 0:896].rearrange("p (c n) -> p c n", c=2)),
                                  (g.ps[:, 0, 2, 0:C2], w[:, 896:LAT]), (g.ps[:, 0, 2, C2:C2 + CTX], w[:, CCTX:CCTX + CTX])):
                        nc.vector.scalar_tensor_tensor(x, ps, -1.0 / CW, x, ALU.mult, ALU.add).then_inc(centred, 1)
                dve.wait_ge(centred, 6)
                dve.sem_inc(free[0], 1)
                modulation(8, NG)

                def window_sum(out, a, b):
                    nc.vector.tensor_tensor(out, a, b, ALU.add).then_inc(pool_step, 1)

                for s in range(2):
                    dve.wait_ge(free[s], 3)
                window_sum(summed[:, :, 1:PB], ppad[:, :, 0:PB - 1], ppad[:, :, 1:PB])
                dve.wait_ge(pool_step, 1)
                window_sum(glu[:, :, 2:PB - 1], summed[:, :, 1:PB - 2], summed[:, :, 3:PB])
                dve.wait_ge(pool_step, 2)
                window_sum(summed[:, 1, 4:PB - 3], glu[:, 1, 2:PB - 5], glu[:, 1, 6:PB - 1])
                dve.wait_ge(pool_step, 3)
                window_sum(glu[64:P, 1, 8:PB - 7], summed[64:P, 1, 4:PB - 11], summed[64:P, 1, 12:PB - 3])
                dve.wait_ge(pool_step, 4)
                for t in range(2):
                    dve.wait_ge(inv_in, 32 * (t + 1))
                    for src, r in ((summed, 0), (glu, 64)):
                        for a, b, at in ((0, LAT, 8), (LAT, T, PCTX)):
                            nc.vector.tensor_tensor(summed[r:r + 64, t, at:at + b - a], src[r:r + 64, t, at:at + b - a], inv[r:r + 64, a:b], ALU.mult).then_inc(inv_used if a == LAT else pool_step, 1)
                    dve.wait_ge(inv_used, 2 * (t + 1))
                    nc.vector.tensor_tensor(summed[:, t, 8:PCTX + CTX], summed[:, t, 8:PCTX + CTX], ppad[:, t, 8:PCTX + CTX], ALU.subtract).then_inc(pooled, 1)
                dve.wait_ge(mod_out, 1)
                late = g.mod[:, 3 * KD:6 * KD, :]
                nc.vector.tensor_tensor(late, late, g.cols[:, OFF["b_mod"] + 3 * KD:OFF["b_mod"] + 6 * KD].rearrange("p (m j) -> p m j", j=1).broadcast_to([P, 3 * KD, 2]),
                                        ALU.add).then_inc(mod_step, 1)
                dve.wait_ge(mod_step, 1)
                mod_gain(g, 1, "norm2_g", 4, mod_step)
                dve.wait_ge(free[1], USE_V)
                nc.vector.reciprocal(sig[:, :], sig[:, :]).then_inc(ln_step, 1)
                dve.wait_ge(ln_step, 1)
                for t in range(2):
                    for a, n, at in ((0, LAT, 0), (LAT, CTX, CCTX)):
                        nc.vector.tensor_tensor(conv[:, t, at:at + n], conv[:, t, at:at + n], sig[:, a:a + n], ALU.mult).then_inc(ln_step, 1)


V_PARTS = ((0, 4), (4, 8), (8, 10))


QT = NT
LOCAL = WIN * GW
PCOLS = LOCAL + PAST


def tile_plan(n):
    if n >= LAT // P:
        return None
    start = min(max(2 * n - KH // 2, 0), ROWS - KH)
    inner = 0 < 2 * n + 1 - KH // 2 < ROWS - KH
    return start * GW, (LOCAL if inner else KH * GW), start - 2 * n + KH - 2, inner


def blocks(n):
    plan = tile_plan(n)
    if plan is None:
        return [], [(5, 8), (6, 9)]
    v0 = plan[0] // P
    return [(j, v0 + j) for j in range(4)], ([(4, v0 + 4)] if plan[3] else []) + [(5, NT), (6, NT + 1)]


def phase_attention(g):
    nc = g.nc
    with ExitStack() as ctx:
        sb = lambda name, shape, dt=F32: ctx.enter_context(nc.sbuf_tensor(name, shape, dt))
        sem = lambda name: ctx.enter_context(nc.semaphore(name))
        KW_ = T + PAST
        q_src = sb("q_src", [P, T])
        k_src = sb("k_src", [P, KW_])
        v_src = sb("v_src", [P, NT + 2, DH])
        b_src = sb("b_src", [P, SLOTS, GW])
        QS = sb("QS", [P, 2, T], FR)
        KA = sb("KA", [P, 2, KW_], FR)
        KB = sb("KB", [P, 2, KW_], FR)
        VV = sb("VV", [P, 2, NT + 2, 2 * DH], FR)
        bias = sb("bias", [P, 2, SLOTS + WIN, GW])
        col_mask = sb("col_mask", [P, GW])
        row_mask = sb("row_mask", [P, WIN])
        prob = sb("prob", [P, 4, PCOLS])
        PT = sb("PT", [P, 2, 7, 2 * P], FR)
        OT = sb("OT", [P, T])
        OLO = sb("OLO", [64, T])
        OUT = sb("OUT", [64, T])
        st = sb("softmax_cols", [P, 4, 6])
        psS = g.ps_all[:, 0:4, :].rearrange("p (s b) n -> p s (b n)", s=2)
        psT = g.ps_all[:, 4:6, :].rearrange("p b n -> p (b n)")
        psV = g.ps_all[:, 6:8, :]
        q_in, k_in, v_in, b_in, mask_in = sem("q_in"), sem("k_in"), sem("v_in"), sem("b_in"), sem("mask_in")
        q_hi, q_lo, k_hi, k_lo, v_hi, v_lo = sem("q_hi"), sem("q_lo"), sem("k_hi"), sem("k_lo"), sem("v_hi"), sem("v_lo")
        table, table_ready = sem("bias_table"), sem("bias_ready")
        scored, max_step, max_ready, exp_ready, sum_step, sum_ready, normal = (
            sem("scored"), sem("max_step"), sem("max_ready"), sem("exp_ready"), sem("sum_step"), sem("sum_ready"), sem("normalised"))
        t_done, p_hi, p_lo = (sem("t_done0"), sem("t_done1")), (sem("p_hi0"), sem("p_hi1")), (sem("p_lo0"), sem("p_lo1"))
        times_v, summed_v, olo_ready, out_ready, out_stored = (sem("times_v"), sem("summed_v"), sem("olo_ready"),
                                                               sem("out_ready"), sem("out_stored"))
        passed = sem("pool_wait_passed")
        NL = LAT // P
        LAST = 2 * QT
        TURN, TIMES = 3, 4
        HI_AT, LO_AT, Q_LO_AT = {2: "k", 4: "q", 6: "v"}, {3: "k", 5: "b", 7: "v"}, 5

        def tile(i, s):
            return None if isinstance(i, int) and i * LAST + s < 0 else (i, s)

        def b0(gs2, s):
            return gs2 * (2 * NL) + (s // QT) * NL + min(s % QT, NL)

        def wait(eng, semaphore, value):
            if not isinstance(value, int) or value > 0:
                eng.wait_ge(semaphore, value)

        q_rows = g.d["qT"].rearrange("a p t -> (a p) t")
        k_rows = g.d["kT"].rearrange("a p t -> (a p) t")
        out_rows = g.d["branch"].rearrange("a p t -> (a p) t")

        def head_pairs(eng, body):
            body(0, True)
            with eng.Fori(1, HEADS // 2 - 1) as i:
                body(i, True)
            body(HEADS // 2 - 1, False)

        with nc.Block() as block:

            @block.sync
            def _(sp):
                def load(h, i, b):
                    sp.wait_ge(k_lo, h)
                    for half in range(2):
                        sp.dma_start(k_src[half * 64:half * 64 + 64, :], k_rows[bass.ds(i * P + b * 64, 64), :]).then_inc(k_in, 16)
                    sp.wait_ge(q_lo, h)
                    for half in range(2):
                        sp.dma_start(q_src[half * 64:half * 64 + 64, :], q_rows[bass.ds(i * P + b * 64, 64), :]).then_inc(q_in, 16)
                    sp.wait_ge(table, h)
                    for half in range(2):
                        sp.dma_start(b_src[half * 64:half * 64 + 64, :, :], rpb_window(g, i, b, 1 - half)).then_inc(b_in, 16)
                    sp.wait_ge(v_lo, h)
                    sp.dma_start(v_src[:, 0:NT, :], g.d["v"][:, bass.ds(i * P + b * 64, 64)].rearrange("(t p) n -> p t n", p=P)).then_inc(v_in, 16)
                    sp.dma_start(v_src[:, NT:NT + 2, :], g.d["cache_v"][:, bass.ds(i * P + b * 64, 64)].rearrange("(t p) n -> p t n", p=P)).then_inc(v_in, 16)

                sp.dma_start(col_mask[:, :], g.d["col_mask"]).then_inc(mask_in, 16)
                sp.dma_start(row_mask[:, :], g.d["row_mask"]).then_inc(mask_in, 16)
                load(0, 0, 0)
                load(1, 0, 1)

                def pair(i, more):
                    for b in range(2):
                        if more:
                            load(i * 2 + (b + 2), i + 1, b)
                        sp.wait_ge(out_ready, i * 2 + (b + 1))
                        sp.dma_start(out_rows[bass.ds(i * P + b * 64, 64), :], OUT[:, :]).then_inc(out_stored, 16)

                for i in range(HEADS // 2):
                    pair(i, i < HEADS // 2 - 1)
                sp.wait_ge(out_stored, 16 * HEADS)

            @block.tensor
            def _(pe):
                def scores(i, s):
                    b, n = s // QT % 2, s % QT
                    if n == 0:
                        pe.wait_ge(q_lo, i * 2 + (b + 1))
                        pe.wait_ge(k_lo, i * 2 + (b + 1))
                    wait(pe, exp_ready, i * LAST + (s - 1))
                    q = QS[:, b, n * P:(n + 1) * P]
                    plan = tile_plan(n)
                    regions = [(LOCAL, LOCAL + PAST, T if plan else LAT)]
                    if plan:
                        regions.insert(0, (0, 512, plan[0]))
                        if plan[3]:
                            regions.insert(1, (512, LOCAL, plan[0] + 512))
                    for c0, c1, k0 in regions:
                        for m, K in enumerate((KA, KB)):
                            mm = nc.tensor.matmul(psS[:, s % 2, c0:c1], q, K[:, b, k0:k0 + c1 - c0], start=(m == 0), stop=(m == 1))
                    mm.then_inc(scored, 1)

                def turn(i, s):
                    n = s % QT
                    pe.wait_ge(normal, i * LAST + (s + 1))
                    for bank, bl in enumerate(blocks(n)):
                        if bl:
                            wait(pe, p_lo[bank], b0(i, s) if bank == 0 else i * LAST + s)
                            for j, _ in bl:
                                mm = nc.tensor.transpose(psT[:, j * P:(j + 1) * P], prob[:, s % 4, j * P:(j + 1) * P], g.ident[:, :])
                            mm.then_inc(t_done[bank], 1)

                def value(i, s):
                    b, n = s // QT % 2, s % QT
                    if n == 0:
                        pe.wait_ge(v_lo, i * 2 + (s // QT + 1))
                    if n < NL:
                        pe.wait_ge(p_lo[0], b0(i, s) + 1)
                    pe.wait_ge(p_lo[1], i * LAST + (s + 1))
                    wait(pe, summed_v, i * LAST + (s - 1))
                    both = sum(blocks(n), [])
                    for m, (j, v) in enumerate(both):
                        mm = nc.tensor.matmul(psV[:, s % 2, 0:2 * P], VV[:, b, v, :], PT[:, s % 2, j, :], start=(m == 0), stop=(m == len(both) - 1))
                    mm.then_inc(times_v, 1)

                def pair(i, more):
                    for s in range(LAST if more else LAST + TIMES):
                        if s < LAST:
                            scores(i, s)
                        if tile(i, s - TURN) and s - TURN < LAST:
                            turn(i, s - TURN)
                        if tile(i, s - TIMES):
                            value(i, s - TIMES)

                head_pairs(pe, pair)

            @block.scalar
            def _(act):
                def prepare(what, h, b):
                    if what == "k":
                        act.wait_ge(k_in, h * 32 + 32)
                        nc.scalar.activation(KA[:, b, :], k_src[:, :], ACT.Copy).then_inc(k_hi, 1)
                    elif what == "q":
                        act.wait_ge(q_in, h * 32 + 32)
                        nc.scalar.activation(QS[:, b, :], q_src[:, :], ACT.Copy, scale=DH ** -0.5).then_inc(q_hi, 1)
                    elif what == "v":
                        act.wait_ge(v_in, h * 32 + 32)
                        nc.scalar.activation(VV[:, b, :, 0:DH], v_src[:, :, :], ACT.Copy).then_inc(v_hi, 1)

                def exponential(i, s):
                    plan = tile_plan(s % QT)
                    act.wait_ge(max_ready, i * LAST + (s + 1))
                    c = st[:, s % 4, :]
                    pr = prob[:, s % 4, :]
                    if plan:
                        nc.scalar.activation(pr[:, 0:plan[1]], pr[:, 0:plan[1]], ACT.Exp, bias=c[:, 2:3], accum_out=c[:, 3:4])
                    nc.scalar.activation(pr[:, LOCAL:PCOLS], psS[:, s % 2, LOCAL:PCOLS], ACT.Exp, bias=c[:, 2:3], accum_out=c[:, 4:5]).then_inc(exp_ready, 1)

                def upper(i, s):
                    n = s % QT
                    wait(act, times_v, i * LAST + (s - 1))
                    for bank, bl in enumerate(blocks(n)):
                        if bl:
                            act.wait_ge(t_done[bank], (b0(i, s) if bank == 0 else i * LAST + s) + 1)
                            j0, j1 = bl[0][0], bl[-1][0] + 1
                            nc.scalar.activation(PT[:, s % 2, j0:j1, 0:P], psT[:, j0 * P:j1 * P].rearrange("p (j n) -> p j n", n=P), ACT.Copy).then_inc(p_hi[bank], 1)

                def pair(i, more):
                    for s in range(LAST if more else LAST + TIMES):
                        if tile(i, s - TURN) and s - TURN < LAST:
                            upper(i, s - TURN)
                        if s < LAST:
                            exponential(i, s)
                        if s in HI_AT:
                            prepare(HI_AT[s], i * 2 + 1, 1)
                        if more and s - QT in HI_AT:
                            prepare(HI_AT[s - QT], i * 2 + 2, 0)
                        done = tile(i, s - TIMES - QT + 1)
                        if done and (s - TIMES - QT + 1) % QT == 0:
                            h = (s - TIMES - QT + 1) // QT
                            act.wait_ge(summed_v, i * LAST + QT * (h + 1))
                            wait(act, out_ready, i * 2 + h)
                            nc.scalar.activation(OLO[:, :], OT[64:P, :], ACT.Copy).then_inc(olo_ready, 1)

                for w in "kqv":
                    prepare(w, 0, 0)
                head_pairs(act, pair)

            @block.vector
            def _(dve):
                def prepare(h, b):
                    dve.wait_ge(q_hi, h + 1)
                    r = 64 if b == 0 else 0
                    nc.vector.scalar_tensor_tensor(QS[r:r + 64, b, :], q_src[r:r + 64, :], DH ** -0.5, QS[r:r + 64, b, :].bitcast(F32),
                                                   ALU.mult, ALU.subtract).then_inc(q_lo, 1)

                def maximum(i, s):
                    b, n = s // QT % 2, s % QT
                    plan = tile_plan(n)
                    dve.wait_ge(scored, i * LAST + (s + 1))
                    wait(dve, t_done[1], i * LAST + (s - 3))
                    c = st[:, s % 4, :]
                    if not plan:
                        nc.vector.tensor_reduce(c[:, 2:3], psS[:, s % 2, LOCAL:PCOLS], AX, ALU.max, negate=True).then_inc(max_ready, 1)
                        return
                    if n == 0:
                        dve.wait_ge(table_ready, i * 2 + (b + 1))
                    slot = SLOTS if plan[3] else plan[2]
                    nc.vector.tensor_reduce(c[:, 1:2], psS[:, s % 2, LOCAL:PCOLS], AX, ALU.max).then_inc(max_step, 1)
                    nc.vector.tensor_tensor_reduce(prob[:, s % 4, 0:plan[1]], psS[:, s % 2, 0:plan[1]],
                                                   bias[:, b, slot:slot + plan[1] // GW, :].rearrange("p a n -> p (a n)"),
                                                   1.0, -3.0e38, ALU.add, ALU.max, c[:, 0:1]).then_inc(max_step, 1)
                    dve.wait_ge(max_step, 2 * (b0(i, s) + 1))
                    nc.vector.tensor_scalar(c[:, 2:3], c[:, 0:1], c[:, 1:2], -1.0, ALU.max, ALU.mult).then_inc(max_ready, 1)

                def total(i, s):
                    c = st[:, s % 4, :]
                    dve.wait_ge(exp_ready, i * LAST + (s + 1))
                    if tile_plan(s % QT):
                        nc.vector.tensor_tensor(c[:, 4:5], c[:, 3:4], c[:, 4:5], ALU.add).then_inc(sum_step, 1)
                        dve.wait_ge(sum_step, b0(i, s) + 1)
                    nc.vector.reciprocal(c[:, 5:6], c[:, 4:5]).then_inc(sum_ready, 1)

                def lower(i, s):
                    for bank, bl in enumerate(blocks(s % QT)):
                        if bl:
                            dve.wait_ge(p_hi[bank], (b0(i, s) if bank == 0 else i * LAST + s) + 1)
                            j0, j1 = bl[0][0], bl[-1][0] + 1
                            nc.vector.tensor_tensor(PT[:, s % 2, j0:j1, P:2 * P], psT[:, j0 * P:j1 * P].rearrange("p (j n) -> p j n", n=P),
                                                    PT[:, s % 2, j0:j1, 0:P].bitcast(F32), ALU.subtract).then_inc(p_lo[bank], 1)

                def gather(i, s):
                    n = s % QT
                    dve.wait_ge(times_v, i * LAST + (s + 1))
                    if n == 0:
                        wait(dve, out_ready, i * 2 + s // QT)
                    nc.vector.tensor_reduce(OT[:, n * P:(n + 1) * P], psV[:, s % 2, 0:2 * P].rearrange("p (a q) -> p q a", a=2), AX, ALU.add).then_inc(summed_v, 1)

                def pair(i, more):
                    for s in range(LAST if more else LAST + TIMES + 1):
                        if s < LAST:
                            maximum(i, s)
                        if tile(i, s - 1) and s - 1 < LAST:
                            total(i, s - 1)
                        if tile(i, s - TURN) and s - TURN < LAST:
                            lower(i, s - TURN)
                        if tile(i, s - TIMES - QT) and (s - TIMES - QT) % QT == 0:
                            h = (s - TIMES - QT) // QT
                            dve.wait_ge(olo_ready, i * 2 + (h + 1))
                            wait(dve, out_stored, i * 32 + 16 * h)
                            nc.vector.tensor_tensor(OUT[:, :], OT[0:64, :], OLO[:, :], ALU.add).then_inc(out_ready, 1)
                        if tile(i, s - TIMES) and s - TIMES < LAST:
                            gather(i, s - TIMES)
                        if s == Q_LO_AT:
                            prepare(i * 2 + 1, 1)
                        if more and s - QT == Q_LO_AT:
                            prepare(i * 2 + 2, 0)

                prepare(0, 0)
                head_pairs(dve, pair)

            @block.gpsimd
            def _(pool):
                def prepare(what, h, b):
                    if what == "k":
                        pool.wait_ge(k_hi, h + 1)
                        nc.gpsimd.tensor_tensor(KB[:, b, :], k_src[:, :], KA[:, b, :].bitcast(F32), ALU.subtract).then_inc(k_lo, 1)
                    elif what == "v":
                        pool.wait_ge(v_hi, h + 1)
                        nc.gpsimd.tensor_tensor(VV[:, b, :, DH:2 * DH], v_src[:, :, :], VV[:, b, :, 0:DH].bitcast(F32), ALU.subtract).then_inc(v_lo, 1)
                    elif what == "b":
                        pool.wait_ge(b_in, h * 32 + 32)
                        nc.gpsimd.tensor_tensor(bias[:, b, 0:SLOTS, :], b_src[:, :, ::-1],
                                                col_mask[:, :].rearrange("p (a n) -> p a n", a=1).broadcast_to([P, SLOTS, GW]), ALU.add).then_inc(table, 1)
                        pool.wait_ge(table, h + 1)
                        nc.gpsimd.tensor_tensor(bias[:, b, SLOTS:SLOTS + WIN, :], bias[:, b, KH // 2 - 2:KH // 2 - 2 + WIN, :],
                                                row_mask[:, :].rearrange("p (a n) -> p a n", n=1).broadcast_to([P, WIN, GW]), ALU.add).then_inc(table_ready, 1)

                def normalise(i, s):
                    plan = tile_plan(s % QT)
                    pool.wait_ge(sum_ready, i * LAST + (s + 1))
                    pool.sem_inc(passed, 1)
                    c, pr = st[:, s % 4, :], prob[:, s % 4, :]
                    if plan and not plan[3]:
                        nc.gpsimd.tensor_scalar(pr[:, 0:plan[1]], pr[:, 0:plan[1]], c[:, 5:6], 1.0, ALU.mult, ALU.mult)
                    a = 0 if plan and plan[3] else LOCAL
                    nc.gpsimd.tensor_scalar(pr[:, a:PCOLS], pr[:, a:PCOLS], c[:, 5:6], 1.0, ALU.mult, ALU.mult).then_inc(normal, 1)

                def pair(i, more):
                    for s in range(LAST if more else LAST + 1):
                        if tile(i, s - 1):
                            normalise(i, s - 1)
                        if s in LO_AT:
                            prepare(LO_AT[s], i * 2 + 1, 1)
                        if more and s - QT in LO_AT:
                            prepare(LO_AT[s - QT], i * 2 + 2, 0)

                pool.wait_ge(mask_in, 32)
                for w in "kbv":
                    prepare(w, 0, 0)
                head_pairs(pool, pair)


def rpb_window(g, i, b, first):
    rpb = g.d["rpb"]
    rows, width = 2 * KH - 1, 2 * GW - 1
    return bass.AP(tensor=rpb.tensor, offset=rpb.offset + ((2 * i + b) * rows + first) * width,
                   ap=[[1, GW], [width, SLOTS], [1, GW]])


def phase_merge(g):
    nc = g.nc
    with ExitStack() as ctx:
        sb = lambda name, shape, dt=F32: ctx.enter_context(nc.sbuf_tensor(name, shape, dt))
        sem = lambda name: ctx.enter_context(nc.semaphore(name))
        W = Weights(g, ctx, "g")
        BH = sb("BH", [P, KD, T], FR)
        BL = sb("BL", [P, KD, T], FR)
        stage = sb("branch_stage", [P, T])
        gate = sb("gate", [P, T])
        total = sb("total", [P, T])
        part = sb("part", [P, T])
        b_in, b_hi, b_lo = sem("b_in"), sem("b_hi"), sem("b_lo")
        gate_ready, free0, free1 = sem("gate_ready"), sem("merge_free0"), sem("merge_free1")
        part_ready, part_added, stored = sem("part_ready"), sem("part_added"), sem("merged_stored")
        passed = sem("sync_wait_passed")
        wv = g.d["w_in"].rearrange("(k p) n -> p k n", p=P)
        proj = (("w_oc", 2, 6), ("w_ob", 2, 4), ("w_oa", 4, 0))
        kts = [KD, 2, KD, 2, KD, 4]
        STAGED = (6, 7, 4, 5, 0, 1, 2, 3)
        NEW = (1, 2, 1, 2, 0, 0)

        with nc.Block() as block:

            @block.sync
            def _(sp):
                def load(i, j):
                    b = j % 2
                    if b == 0:
                        src = wv[:, :, bass.ds(i * P + (GATE_COL + (2 - j // 2) * D), P)]
                    else:
                        name = proj[j // 2][0]
                        src = g.d[name].rearrange("(k p) n -> p k n", p=P)[:, :, bass.ds(i * P, P)]
                    sp.dma_start(W.raw[:, b, 0:kts[j] * P].rearrange("p (k n) -> p k n", n=P), src).then_inc(W.raw_in[b], 16)

                load(0, 0)
                load(0, 1)
                n = 0
                for j in range(-1, 4):
                    if j >= 0:
                        sp.wait_ge(W.lo_ready, j + 1)
                        load(0, j + 2)
                    for _ in range(2 if j < 0 else NEW[j]):
                        if n:
                            sp.wait_ge(b_lo, n)
                        sp.dma_start(stage[:, :], g.d["branch"][STAGED[n], :, :]).then_inc(b_in, 16)
                        n += 1
                with sp.Fori(0, KD - 1) as i:
                    for j in range(6):
                        sp.wait_ge(W.lo_ready, i * 6 + (j + 5))
                        if j % 2:
                            sp.sem_inc(passed, 1)
                        load(i + 1, j)
                    sp.wait_ge(part_added, i * 2 + 2)
                    sp.dma_start(g.d["merged"][bass.ds(i, 1), :, :].rearrange("a p t -> p (a t)"), total[:, :]).then_inc(stored, 16)
                sp.wait_ge(part_added, 2 * KD)
                sp.dma_start(g.d["merged"][KD - 1, :, :], total[:, :]).then_inc(stored, 16)
                sp.wait_ge(stored, 16 * KD)

            @block.tensor
            def _(pe):
                def tile(i, skip):
                    for j in range(6):
                        s = j % 2
                        pe.wait_ge(W.lo_ready, i * 6 + (j + 1))
                        pe.wait_ge((free0, free1)[s], i * 3 + j // 2)
                        if s == 0:
                            ah, al, k0 = g.AH, g.AL, 0
                        else:
                            ah, al, k0 = BH, BL, proj[j // 2][2]
                            if skip:
                                pe.wait_ge(b_lo, (2, 4, 8)[j // 2])
                        gemm(nc, g.ps[:, s], W.hi[:, s, :], W.lo[:, s, :], ah, al,
                             [(k * P, k0 + k) for k in range(kts[j])]).then_inc(W.used, 1)

                tile(0, True)
                with pe.Fori(1, KD) as i:
                    tile(i, False)

            @block.scalar
            def _(act):
                def split(i, j, first=False):
                    b, n = j % 2, kts[j] * P
                    act.wait_ge(W.raw_in[b], i * 48 + 16 * (j // 2 + 1))
                    if not first:
                        act.wait_ge(W.used, i * 6 + (j - 1))
                    nc.scalar.activation(W.hi[:, b, 0:n], W.raw[:, b, 0:n], ACT.Copy).then_inc(W.hi_ready, 1)

                def gate_out(i, j):
                    act.wait_ge(W.used, i * 6 + (j + 1))
                    if not isinstance(i, int) or 3 * i + j:
                        act.wait_ge(free1, i * 3 + j // 2)
                    c = OFF["b_gate"] + (2 - j // 2) * KD
                    for ps, out in chunk_views(g.ps[:, 0], gate):
                        last = nc.scalar.activation(out, ps, ACT.Sigmoid, bias=g.cols[:, bass.ds(i + c, 1)])
                    last.then_inc(free0, 1)

                def split_branch(n):
                    act.wait_ge(b_in, 16 * (n + 1))
                    nc.scalar.activation(BH[:, STAGED[n], :], stage[:, :], ACT.Copy).then_inc(b_hi, 1)

                def tile(i, following, first=False):
                    n = 2
                    for j in range(6):
                        if j + 2 < 6:
                            split(i, j + 2)
                        elif following:
                            split(i + 1, j - 4)
                        if j % 2 == 0:
                            gate_out(i, j)
                        if first:
                            for _ in range(NEW[j]):
                                split_branch(n)
                                n += 1

                split(0, 0, True)
                split(0, 1, True)
                split_branch(0)
                split_branch(1)
                tile(0, True, True)
                with act.Fori(1, KD - 1) as i:
                    tile(i, True)
                tile(KD - 1, False)

            @block.gpsimd
            def _(pool):
                def lower(i, j):
                    b, n = j % 2, kts[j] * P
                    pool.wait_ge(W.hi_ready, i * 6 + (j + 1))
                    nc.gpsimd.tensor_tensor(W.lo[:, b, 0:n], W.raw[:, b, 0:n], W.hi[:, b, 0:n].bitcast(F32), ALU.subtract).then_inc(W.lo_ready, 1)

                lower(0, 0)
                lower(0, 1)
                n = 0
                for j in range(-1, 4):
                    if j >= 0:
                        lower(0, j + 2)
                    for _ in range(2 if j < 0 else NEW[j]):
                        pool.wait_ge(b_hi, n + 1)
                        nc.gpsimd.tensor_tensor(BL[:, STAGED[n], :], stage[:, :], BH[:, STAGED[n], :].bitcast(F32), ALU.subtract).then_inc(b_lo, 1)
                        n += 1
                with pool.Fori(1, KD) as i:
                    for j in range(6):
                        lower(i, j)

            @block.vector
            def _(dve):
                def tile(i):
                    for b in range(3):
                        dve.wait_ge(free0, i * 3 + (b + 1))
                        dve.wait_ge(W.used, i * 6 + (2 * b + 2))
                        if b == 0:
                            if not isinstance(i, int):
                                dve.wait_ge(stored, i * 16)
                        elif b == 2:
                            dve.wait_ge(part_added, i * 2 + 1)
                        out = total if b == 0 else part
                        for (ps, o), (_, x) in zip(chunk_views(g.ps[:, 1], out), chunk_views(g.ps[:, 1], gate)):
                            last = nc.vector.tensor_tensor(o, ps, x, ALU.mult)
                        last.then_inc(free1, 1)
                        if b:
                            dve.wait_ge(free1, i * 3 + (b + 1))
                            nc.vector.tensor_tensor(total[:, :], total[:, :], part[:, :], ALU.add).then_inc(part_added, 1)

                tile(0)
                with dve.Fori(1, KD) as i:
                    tile(i)


def residual(g, dve, XT, m, gate_part, s, free):
    nc = g.nc
    ps, x = g.ps[:, s], XT[:, m, :]
    for p, o, j in ((ps[:, 0:2, 0:448], x[..., 0:896].rearrange("p (c n) -> p c n", c=2), 0),
                    (ps[:, 2, 0:C2], x[..., 896:LAT], 0), (ps[:, 2, C2:C2 + CTX], x[..., LAT:T], 1)):
        last = nc.vector.scalar_tensor_tensor(o, p, g.mod[:, gate_part * KD + m, j:j + 1], o, ALU.mult, ALU.add)
    last.then_inc(free, 1)


def phase_back(g):
    nc = g.nc
    with ExitStack() as ctx:
        sb = lambda name, shape, dt=F32: ctx.enter_context(nc.sbuf_tensor(name, shape, dt))
        sem = lambda name: ctx.enter_context(nc.semaphore(name))
        XT = sb("XT", [P, KD, T])
        W = Weights(g, ctx, "o")
        act32 = sb("act32", [P, 2, T])
        stage = square = act32
        sumsq = gated = sb("sumsq_silu_a", [P, T])
        rstd = sumsq2 = sb("rstd_sumsq2", [P, T])
        normed = sb("normed1", [P, 2, T])
        actH = sb("actH", [P, 2, T], FR)
        actL = sb("actL", [P, 2, T], FR)
        g_row = sb("final_g_row", [P, D])
        tok_rstd = sb("tok_rstd", [P, 2, NT])
        m_in = (sem("merged_in0"), sem("merged_in1"))
        m_hi, m_lo, g_in = sem("m_hi"), sem("m_lo"), sem("final_g_in")
        x_in = [sem(f"x_back{m}") for m in range(KD)]
        free = (sem("out_free0"), sem("out_free1"))
        zero, sq_ready, sq_added, stat_done = sem("out_zero"), sem("out_sq"), sem("out_sq_added"), sem("out_stat")
        root_ready, rstd_ready, scaled, t_ready, ah_ready, al_ready = (
            sem("out_root"), sem("out_rstd"), sem("out_scaled"), sem("out_t"), sem("out_ah"), sem("out_al"))
        out_done, b_ready, h_hi, h_lo = sem("down_done"), sem("b_ready"), sem("h_hi"), sem("h_lo")
        zero2, sq2_ready, sq2_added, stat2_done, root2_ready, rstd2_ready = (
            sem("fin_zero"), sem("fin_sq"), sem("fin_sq_added"), sem("fin_stat"), sem("fin_root"), sem("fin_rstd"))
        turned, y_ready, y_stored = sem("y_turned"), sem("y_ready"), sem("y_stored")
        wv = g.d["w_out"].rearrange("(k p) n -> p k n", p=P)
        gu = g.d["w_gu"].rearrange("(k p) n -> p k n", p=P)
        down = g.d["w_down"].rearrange("(k p) n -> p k n", p=P)
        W0, F0 = KD, KD // 2
        kinds = ("a0", "b0", "d0", "d1", "a1", "b1")
        LASTS = F0 + 6 * BLOCKS - 4

        def wcount(j, n):
            return j * 6 + (W0 + n - 1)

        with nc.Block() as block:

            @block.sync
            def _(sp):
                def load(j, kind):
                    b = int(kind in ("b0", "d1", "b1"))
                    if kind[0] == "d":
                        raw = W.raw[:, b, :].rearrange("p (k n) -> p k n", n=512)
                        src = down[:, bass.ds(j * 2 - 2, 2), b * 512:(b + 1) * 512]
                    else:
                        raw = W.columns(b, P)
                        src = gu[:, :, bass.ds(j * (2 * P) + (int(kind[1]) * P + (HID if kind[0] == "b" else 0)), P)]
                    sp.dma_start(raw, src).then_inc(W.raw_in[b], 16)

                for m in range(2):
                    sp.dma_start(W.columns(m, P), wv[:, :, m * P:(m + 1) * P]).then_inc(W.raw_in[m], 16)
                for k in range(KD):
                    if k >= 2:
                        sp.wait_ge(m_lo, k - 1)
                    sp.dma_start(stage[:, k % 2, :], g.d["merged"][k, :, :]).then_inc(m_in[k % 2], 16)
                    if k in (4, 5):
                        b = k - 4
                        sp.wait_ge(W.lo_ready, b + 1)
                        sp.dma_start(W.columns(b, P), wv[:, :, (2 + b) * P:(3 + b) * P]).then_inc(W.raw_in[b], 16)
                for m in range(KD):
                    sp.dma_start(XT[:, m, :], g.d["xT"][m, :, :]).then_inc(x_in[m], 16)
                with sp.Fori(2, KD // 2) as i:
                    for b in range(2):
                        sp.wait_ge(W.lo_ready, i * 2 + (b - 1))
                        sp.dma_start(W.columns(b, P), wv[:, :, bass.ds(i * (2 * P) + b * P, P)]).then_inc(W.raw_in[b], 16)
                sp.dma_start(g_row[:, :], g.d["final_g"].broadcast_to([P, D])).then_inc(g_in, 16)
                for n, kind in enumerate(("a0", "b0", "a1", "b1")):
                    sp.wait_ge(W.lo_ready, W0 + n - 1)
                    load(0, kind)
                with sp.Fori(1, BLOCKS) as j:
                    for n, kind in enumerate(kinds):
                        sp.wait_ge(W.lo_ready, wcount(j, n) - 2)
                        load(j, kind)
                for b in range(2):
                    sp.wait_ge(W.lo_ready, wcount(BLOCKS, b) - 2)
                    load(BLOCKS, ("d0", "d1")[b])
                for t in range(NT):
                    sp.wait_ge(y_ready, 2 * t + 2)
                    dst = g.d["y_sample"][t * P:(t + 1) * P, :] if t < LAT // P else g.d["y_prompt"][t * P - LAT:(t + 1) * P - LAT, :]
                    sp.dma_start(dst.rearrange("t (f n) -> t f n", n=P), XT[:, :, t * P:(t + 1) * P]).then_inc(y_stored, 16)
                sp.wait_ge(y_stored, 16 * NT)

            @block.tensor
            def _(pe):
                def paced(ready, w, wait_sets):
                    for m in range(2):
                        pe.wait_ge(W.lo_ready, w + m + 1)
                    wait_sets()
                    for k in range(KD):
                        pe.wait_ge(ready, k + 1)
                        for m in range(2):
                            mm = gemm(nc, g.ps[:, m], W.hi[:, m, :], W.lo[:, m, :], g.AH, g.AL, [(k * P, k)], first=k == 0, last=k == KD - 1)
                            if k == KD - 1:
                                mm.then_inc(W.used, 1)

                def unit(s, w, uses):
                    pe.wait_ge(W.lo_ready, w)
                    pe.wait_ge(free[s], uses)
                    gemm(nc, g.ps[:, s], W.hi[:, s, :], W.lo[:, s, :], g.AH, g.AL, [(k * P, k) for k in range(KD)]).then_inc(W.used, 1)

                def output(j, w0, uses):
                    pe.wait_ge(h_lo, j * 2)
                    for m in range(KD):
                        s, ws = m % 2, m // 4
                        if m % 4 == 0:
                            pe.wait_ge(W.lo_ready, w0 + ws + 1)
                        pe.wait_ge(free[s], uses + m // 2)
                        mm = gemm(nc, g.ps[:, s], W.hi[:, ws, :], W.lo[:, ws, :], actH, actL, [(k * 512 + (m % 4) * P, k) for k in range(2)])
                        mm.then_inc(out_done, 1)
                        if m % 4 == 3:
                            pe.wait_ge(out_done, j * KD - KD + (m + 1))
                            pe.sem_inc(W.used, 1)

                def turn(t):
                    for h in range(2):
                        n = 2 * t + h
                        if n >= 6:
                            pe.wait_ge(y_ready, n - 5)
                        for f in range(4):
                            mm = nc.tensor.transpose(g.ps_all[:, n % 6, f * P:(f + 1) * P], XT[:, 4 * h + f, t * P:(t + 1) * P], g.ident[:, :])
                        mm.then_inc(turned, 1)

                paced(m_lo, 0, lambda: None)
                with pe.Fori(1, KD // 2) as i:
                    for s in range(2):
                        unit(s, i * 2 + (s + 1), i)
                pe.wait_ge(sq_added, KD - 1)
                pe.wait_ge(free[0], F0)
                for last, x in enumerate((sumsq, square[:, 1, :])):
                    if last:
                        pe.wait_ge(sq_ready, KD)
                    for c, (c0, c1) in enumerate(CHUNKS):
                        mm = nc.tensor.matmul(g.ps[:, 0, c, 0:c1 - c0], g.ones[:, :], x[:, c0:c1], start=not last, stop=bool(last))
                mm.then_inc(stat_done, 1)

                def sets():
                    pe.wait_ge(root_ready, 2)
                    pe.wait_ge(free[1], F0)

                paced(al_ready, W0, sets)
                for s in range(2):
                    unit(s, W0 + 3 + s, F0 + 1)
                with pe.Fori(1, BLOCKS) as j:
                    for s in range(2):
                        unit(s, wcount(j, s), j * 6 + (F0 - 4))
                    output(j, j * 6 + W0, j * 6 + (F0 - 3))
                    for s in range(2):
                        unit(s, wcount(j, 4 + s), j * 6 + (F0 + 1))
                output(BLOCKS, wcount(BLOCKS, -1), LASTS)
                for s in range(2):
                    pe.wait_ge(free[s], LASTS + F0)
                for t in range(3):
                    turn(t)
                pe.wait_ge(sq2_added, KD - 1)
                pe.wait_ge(sq2_ready, KD)
                for t in range(NT):
                    for last, x in enumerate((sumsq2, square[:, 1, :])):
                        mm = nc.tensor.matmul(g.aux[:, 0, t:t + 1], x[:, t * P:(t + 1) * P], g.ones[:, 0:1], start=not last, stop=bool(last))
                mm.then_inc(stat2_done, 1)
                for t in range(3, NT):
                    turn(t)

            @block.scalar
            def _(act):
                def split(b, raw, used=None):
                    act.wait_ge(W.raw_in[b], raw)
                    if used is not None:
                        act.wait_ge(W.used, used)
                    nc.scalar.activation(W.hi[:, b, :], W.raw[:, b, :], ACT.Copy).then_inc(W.hi_ready, 1)

                def silu(w, hid):
                    act.wait_ge(W.used, w)
                    act.wait_ge(b_ready, hid)
                    for ps, out in chunk_views(g.ps[:, 0], gated):
                        last = nc.scalar.activation(out, ps, ACT.Silu)
                    last.then_inc(free[0], 1)

                def upper(t, hid):
                    act.wait_ge(b_ready, hid)
                    nc.scalar.activation(actH[:, t, :], act32[:, t, :], ACT.Copy).then_inc(h_hi, 1)

                split(0, 16)
                split(1, 16)
                for k in range(KD):
                    act.wait_ge(m_in[k % 2], 16 * (k // 2 + 1))
                    nc.scalar.activation(g.AH[:, k, :], stage[:, k % 2, :], ACT.Copy).then_inc(m_hi, 1)
                act.wait_ge(m_lo, KD)
                for m in range(KD):
                    split(m % 2, 16 * (m // 2 + 2), m + 1)
                    act.wait_ge(free[m % 2], m // 2 + 1)
                    if m >= 2:
                        act.wait_ge(sq_added, m - 1)
                    nc.scalar.activation(square[:, m % 2, :], XT[:, m, :], ACT.Square).then_inc(sq_ready, 1)
                act.wait_ge(stat_done, 1)
                root(g, act, rstd, root_ready)
                copies(g, act, normed, t_ready, ah_ready)
                R0 = 16 * F0
                for t in range(2):
                    silu(W0 + 2 * t + 1, t)
                    split(0, R0 + 16 * (t + 2), W0 + 2 * t + 1)
                    split(1, R0 + 16 * (t + 2), W0 + 2 * t + 2)
                    upper(t, t + 1)
                with act.Fori(1, BLOCKS) as j:
                    w = j * 6 + (W0 - 2)
                    r = j * 48 + (R0 - 16)
                    silu(w + 1, j * 2)
                    split(0, r + 32, w + 1)
                    split(1, r + 32, w + 2)
                    split(0, r + 48, w + 3)
                    split(1, r + 48, w + 4)
                    act.wait_ge(out_done, j * KD)
                    upper(0, j * 2 + 1)
                    silu(w + 5, j * 2 + 1)
                    split(0, r + 64, w + 5)
                    split(1, r + 64, w + 6)
                    upper(1, j * 2 + 2)
                act.wait_ge(h_lo, 2 * BLOCKS)
                for m in range(KD):
                    act.wait_ge(free[m % 2], LASTS + m // 2 + 1)
                    if m >= 2:
                        act.wait_ge(sq2_added, m - 1)
                    nc.scalar.activation(square[:, m % 2, :], XT[:, m, :], ACT.Square).then_inc(sq2_ready, 1)
                act.wait_ge(stat2_done, 1)
                nc.scalar.activation(tok_rstd[:, 0, :], g.aux[:, 0, 0:NT], ACT.Sqrt, bias=g.eps[:, 0:1], scale=1.0 / D).then_inc(root2_ready, 1)

            @block.vector
            def _(dve):
                def product(t, w, uses0, hid):
                    dve.wait_ge(W.used, w)
                    dve.wait_ge(free[0], uses0)
                    if hid is not None:
                        dve.wait_ge(h_lo, hid)
                    for (ps, o), (_, x) in zip(chunk_views(g.ps[:, 1], act32[:, t, :]), chunk_views(g.ps[:, 1], gated)):
                        last = nc.vector.tensor_tensor(o, ps, x, ALU.mult)
                    last.then_inc(free[1], 1)
                    dve.wait_ge(free[1], uses0)
                    dve.sem_inc(b_ready, 1)

                def add_output(j):
                    for m in range(KD):
                        dve.wait_ge(out_done, j * KD - KD + (m + 1))
                        residual(g, dve, XT, m, 5, m % 2, free[m % 2])

                for m in range(KD):
                    dve.wait_ge(x_in[m], 16)
                    dve.wait_ge(W.used, m + 1)
                    residual(g, dve, XT, m, 2, m % 2, free[m % 2])
                dve.wait_ge(root_ready, 2)
                nc.vector.reciprocal(rstd[:, :], rstd[:, :]).then_inc(rstd_ready, 1)
                dve.wait_ge(rstd_ready, 1)
                for s in range(2):
                    dve.wait_ge(free[s], F0)
                scale_shift(g, dve, XT, rstd, normed, 1, 3, scaled, t_ready, al_ready)
                for t in range(2):
                    product(t, W0 + 2 * t + 2, F0 + t + 1, None)
                with dve.Fori(1, BLOCKS) as j:
                    product(0, wcount(j, 1), j * 6 + (F0 - 3), j * 2 - 1)
                    add_output(j)
                    product(1, wcount(j, 5), j * 6 + (F0 + 2), j * 2)
                add_output(BLOCKS)
                dve.wait_ge(g_in, 16)
                dve.wait_ge(root2_ready, 1)
                nc.vector.reciprocal(tok_rstd[:, 1, :], tok_rstd[:, 0, :]).then_inc(rstd2_ready, 1)
                dve.wait_ge(rstd2_ready, 1)
                for n in range(2 * NT):
                    t, f = n // 2, (n % 2) * 4
                    dve.wait_ge(turned, n + 1)
                    nc.vector.scalar_tensor_tensor(XT[:, f:f + 4, t * P:(t + 1) * P], g.ps_all[:, n % 6, :].rearrange("p (f n) -> p f n", n=P),
                                                   tok_rstd[:, 1, t:t + 1], g_row[:, f * P:(f + 4) * P].rearrange("p (f n) -> p f n", n=P),
                                                   ALU.mult, ALU.mult).then_inc(y_ready, 1)

            @block.gpsimd
            def _(pool):
                def lower(b, count):
                    pool.wait_ge(W.hi_ready, count)
                    nc.gpsimd.tensor_tensor(W.lo[:, b, :], W.raw[:, b, :], W.hi[:, b, :].bitcast(F32), ALU.subtract).then_inc(W.lo_ready, 1)

                def rest(t, count):
                    pool.wait_ge(h_hi, count)
                    nc.gpsimd.tensor_tensor(actL[:, t, :], act32[:, t, :], actH[:, t, :].bitcast(F32), ALU.subtract).then_inc(h_lo, 1)

                def add_square(total, m, ready, added):
                    pool.wait_ge(ready, m + 1)
                    if m:
                        pool.wait_ge(added, m)
                    nc.gpsimd.tensor_tensor(total[:, :], total[:, :], square[:, m % 2, :], ALU.add).then_inc(added, 1)

                nc.gpsimd.memset(sumsq[:, :], 0.0).then_inc(zero, 1)
                for m in range(2):
                    lower(m, m + 1)
                for k in range(KD):
                    pool.wait_ge(m_hi, k + 1)
                    nc.gpsimd.tensor_tensor(g.AL[:, k, :], stage[:, k % 2, :], g.AH[:, k, :].bitcast(F32), ALU.subtract).then_inc(m_lo, 1)
                pool.wait_ge(zero, 1)
                for m in range(KD):
                    lower(m % 2, m + 3)
                    if m < KD - 1:
                        add_square(sumsq, m, sq_ready, sq_added)
                rests(g, pool, normed, ah_ready, al_ready)
                for t in range(2):
                    lower(0, W0 + 2 * t + 3)
                    lower(1, W0 + 2 * t + 4)
                    rest(t, t + 1)
                with pool.Fori(1, BLOCKS) as j:
                    for n in range(4):
                        lower(n % 2, j * 6 + (W0 + n + 1))
                    rest(0, j * 2 + 1)
                    for n in range(2):
                        lower(n % 2, j * 6 + (W0 + n + 5))
                    rest(1, j * 2 + 2)
                nc.gpsimd.memset(sumsq2[:, :], 0.0).then_inc(zero2, 1)
                pool.wait_ge(zero2, 1)
                for m in range(KD - 1):
                    add_square(sumsq2, m, sq2_ready, sq2_added)


PHASES = (phase_input, phase_mixers, phase_attention, phase_merge, phase_back)


_OUTS = (("y_prompt", (CTX, D)), ("y_sample", (LAT, D)), ("new_k", (CTX, NAW)), ("new_v", (CTX, NAW)))
_SCRATCH = (("xT", (KD, P, T)), ("qT", (4, P, T)), ("kT", (4, P, T + PAST)), ("v", (T, NAW)),
            ("branch", (KD, P, T)), ("merged", (KD, P, T)))


def build(nc, arrays, phases=9, scratch_kind="Internal"):
    g = Ctx()
    g.nc = nc
    g.d = {n: nc.dram_tensor(n + "_dram", a.shape, F32, kind="ExternalInput").ap() for n, a in arrays.items()}
    for n, shape in _OUTS:
        g.d[n] = nc.dram_tensor(n + "_dram", shape, F32, kind="ExternalOutput").ap()
    for n, shape in _SCRATCH:
        g.d[n] = nc.dram_tensor(n + "_dram", shape, F32, kind=scratch_kind).ap()
    with ExitStack() as ctx:
        sb = lambda name, shape, dt=F32: ctx.enter_context(nc.sbuf_tensor(name, shape, dt))
        g.cols = sb("cols", [P, NCOLS])
        g.mod = sb("mod", [P, 6 * KD, 2])
        g.gain = sb("gain", [P, 2, KD, 2])
        g.cs = sb("silu_c", [P, 2 * KD])
        g.ident = sb("ident", [P, P])
        g.ones = sb("ones", [P, P])
        g.eps = sb("eps", [P, 1])
        g.AH = sb("AH", [P, KD, T], FR)
        g.AL = sb("AL", [P, KD, T], FR)
        g.ps_all = ctx.enter_context(nc.psum_tensor("ps_all", [P, 8, 512], F32))
        g.ps = g.ps_all[:, 0:6, :].rearrange("p (s c) n -> p s c n", s=2)
        g.aux = g.ps_all[:, 6:8, :]
        for n, phase in enumerate(PHASES):
            if n < phases:
                phase(g)


def columns(v):
    return np.asarray(v).reshape(-1, P).T


def lay_out(i):
    both = np.stack([columns(i["c"][0]), columns(i["c_ctx"])], axis=2).reshape(P, 2 * KD)
    w_dw = np.asarray(i["w_dw"][0]).T.reshape(2, P, CONV_K).transpose(1, 0, 2).reshape(P, 2 * CONV_K)
    packed = [both] + [columns(v) for v in (i["b_mod"][0], i["norm1_g"][0], i["norm2_g"][0], i["b_gate"][0],
                                            i["pool_scale"][0], i["b_dw"][0], i["conv_norm_g"][0], i["conv_norm_b"][0])] + [w_dw]
    rpb = np.zeros((HEADS, 2 * KH - 1, 2 * GW - 1), np.float32)
    side = GW - KW
    rpb[:, :, side:side + 2 * KW - 1] = np.asarray(i["rpb"][0])[:, :, ::-1]
    start = np.clip(np.arange(GW) - KW // 2, 0, GW - KW)
    inside = (np.arange(GW)[None] >= start[:, None]) & (np.arange(GW)[None] < start[:, None] + KW)
    row = np.arange(P)[:, None] // GW
    seen = (np.arange(WIN)[None] >= row) & (np.arange(WIN)[None] < row + KH)
    inv = []
    for w in (2, 4, 8, 16):
        row = []
        for n in (LAT, CTX):
            t = np.arange(n)
            row.append(1.0 / (np.clip(t - w // 2 + w, 0, n) - np.clip(t - w // 2, 0, n)))
        inv.append(np.concatenate(row))
    a = {
        "cols": np.ascontiguousarray(np.concatenate(packed, axis=1)),
        "ident": np.eye(P, dtype=np.float32),
        "col_mask": np.tile(np.where(inside, 0.0, NEG), (2, 1)).astype(np.float32),
        "row_mask": np.where(seen, 0.0, NEG).astype(np.float32),
        "inv_count": np.stack(inv).astype(np.float32),
        "rpb": rpb, "final_g": np.asarray(i["final_g"]).reshape(1, D),
        "x_prompt": np.asarray(i["x_prompt"][0]), "x_sample": np.asarray(i["x_sample"][0]),
        "cache_k": np.asarray(i["cache_k"][0, 0]).reshape(PAST, NAW), "cache_v": np.asarray(i["cache_v"][0, 0]).reshape(PAST, NAW),
    }
    for n in ("w_mod", "w_in", "w_oa", "w_pool", "w_ob", "w_oc", "w_out", "w_gu", "w_down"):
        a[n] = np.asarray(i[n][0])
    return a


def kernel(**inputs):
    import concourse.bacc as bacc
    from concourse.bass_utils import run_bass_kernel_spmd

    arrays = lay_out(inputs)
    nc = bacc.Bacc("TRN2", target_bir_lowering=False, num_devices=1)
    build(nc, arrays)
    r = run_bass_kernel_spmd(nc, [{n + "_dram": a for n, a in arrays.items()}], core_ids=[0]).results[0]
    shape = (1, 1, CTX, HEADS, DH)
    return (r["y_prompt_dram"].reshape(1, CTX, D), r["y_sample_dram"].reshape(1, LAT, D),
            r["new_k_dram"].reshape(shape), r["new_v_dram"].reshape(shape))
```
